# Optimizing a Trainium2 kernel written in Bass

```python
import jax, jax.numpy as jnp
from jax import lax
import numpy as np
import math

D_MODEL = 1024
BATCH = 1
SEQ = 256
DEPTH = 1

HEAD_DIM = 64
DSA_GROUPS = ((128, 1), (512, 4), (2048, 16))
DSA_HEADS_PER_GROUP = 4
DSA_HEADS = DSA_HEADS_PER_GROUP * len(DSA_GROUPS)
MOBA_HEADS = 8
MOBA_BLOCK = 256
MOBA_TOPK = 3
MOBA_Q_CHUNK = 64
D_FF = ((8 * D_MODEL // 3 + 127) // 128) * 128
DSA_WIDTH = DSA_HEADS * HEAD_DIM
MOBA_WIDTH = MOBA_HEADS * HEAD_DIM
DSA_OUT = DSA_HEADS_PER_GROUP * HEAD_DIM
IN_WIDTH = 3 * DSA_WIDTH + 3 * MOBA_WIDTH + 2 * D_MODEL
EPS = 1e-6
NEG = -1e30


f32 = jnp.float32

def rmsnorm(x, g):
    xf = x.astype(f32)
    y = xf * lax.rsqrt(jnp.mean(xf * xf, axis=-1, keepdims=True) + EPS)
    return (y * g.astype(f32)).astype(x.dtype)

def swiglu(x, w_gate, w_up, w_down):
    return (jax.nn.silu(x @ w_gate) * (x @ w_up)) @ w_down

def alibi_slopes(n):
    return 2.0 ** (-8.0 * jnp.arange(1, n + 1, dtype=f32) / n)

def to_heads(a, n):
    b, s, _ = a.shape
    return a.reshape(b, s, n, HEAD_DIM).transpose(0, 2, 1, 3)

def dilated_window_attention(q, k, v, slopes, window, dilation):
    b, h, s, hd = q.shape
    blk = window // dilation
    L = s // dilation
    Lp = -(-L // blk) * blk
    nb = Lp // blk

    def to_residue(a):
        a = a.reshape(b, h, L, dilation, hd).transpose(0, 1, 3, 2, 4)
        return jnp.pad(a, ((0, 0), (0, 0), (0, 0), (0, Lp - L), (0, 0)))

    qr, kr, vr = to_residue(q), to_residue(k), to_residue(v)
    qb = qr.reshape(b, h, dilation, nb, blk, hd)

    def band(a):
        ap = jnp.pad(a, ((0, 0), (0, 0), (0, 0), (blk, 0), (0, 0)))
        prev = ap[:, :, :, :Lp].reshape(b, h, dilation, nb, blk, hd)
        cur = a.reshape(b, h, dilation, nb, blk, hd)
        return jnp.concatenate([prev, cur], axis=4)

    kb, vb = band(kr), band(vr)
    scores = jnp.einsum('bhrnqd,bhrnkd->bhrnqk', qb, kb).astype(f32)
    qi = jnp.arange(blk)[:, None]
    kj = jnp.arange(2 * blk)[None, :]
    delta = qi + blk - kj
    kpos = jnp.arange(nb)[:, None, None] * blk - blk + kj[None]
    valid = (delta >= 0)[None] & (delta <= blk)[None] & (kpos >= 0)
    bias = -slopes[:, None, None] * (delta * dilation).astype(f32)[None]
    scores = jnp.where(valid[None, None, None], scores + bias[None, :, None, None], NEG)
    lse = jax.nn.logsumexp(scores, axis=-1)
    p = jnp.exp(scores - lse[..., None]).astype(v.dtype)
    out = jnp.einsum('bhrnqk,bhrnkd->bhrnqd', p, vb)
    out = out.reshape(b, h, dilation, Lp, hd)[:, :, :, :L]
    out = out.transpose(0, 1, 3, 2, 4).reshape(b, h, s, hd)
    lse = lse.reshape(b, h, dilation, Lp)[..., :L].transpose(0, 1, 3, 2).reshape(b, h, s)
    return out, lse

def moba_attention(q, k, v, slopes):
    b, h, s, hd = q.shape
    nblk = -(-s // MOBA_BLOCK)
    sp = nblk * MOBA_BLOCK
    n_sel = min(MOBA_TOPK, nblk)
    padw = ((0, 0), (0, 0), (0, sp - s), (0, 0))
    q, k, v = jnp.pad(q, padw), jnp.pad(k, padw), jnp.pad(v, padw)
    bh = b * h
    kblk = k.reshape(bh, nblk, MOBA_BLOCK, hd)
    vblk = v.reshape(bh, nblk, MOBA_BLOCK, hd)
    qf = q.reshape(bh, sp, hd)
    kmean = jnp.mean(kblk.astype(f32), axis=2)
    gate = jnp.einsum('xtd,xnd->xtn', qf.astype(f32), kmean)
    own = jnp.arange(sp) // MOBA_BLOCK
    past = jnp.arange(nblk)[None, :] < own[:, None]
    gate = jnp.where(past[None], gate, NEG)
    _, sel = lax.top_k(gate, n_sel)
    slope_x = jnp.tile(slopes, b)
    nq = sp // MOBA_Q_CHUNK
    q_chunks = qf.reshape(bh, nq, MOBA_Q_CHUNK, hd).transpose(1, 0, 2, 3)
    sel_chunks = sel.reshape(bh, nq, MOBA_Q_CHUNK, n_sel).transpose(1, 0, 2, 3)
    take = jax.vmap(lambda blocks, ix: blocks[ix])
    blk_off = jnp.arange(MOBA_BLOCK)

    def chunk(args):
        qc, ix, c = args
        t = c * MOBA_Q_CHUNK + jnp.arange(MOBA_Q_CHUNK)
        own_blk = (c * MOBA_Q_CHUNK) // MOBA_BLOCK
        k_own = lax.dynamic_index_in_dim(kblk, own_blk, axis=1, keepdims=False)
        v_own = lax.dynamic_index_in_dim(vblk, own_blk, axis=1, keepdims=False)
        d_own = t[:, None] - (own_blk * MOBA_BLOCK + blk_off)[None, :]
        s_own = jnp.einsum('xqd,xkd->xqk', qc, k_own).astype(f32)
        s_own = jnp.where(d_own[None] >= 0,
                          s_own - slope_x[:, None, None] * d_own.astype(f32)[None], NEG)
        k_sel = take(kblk, ix)
        v_sel = take(vblk, ix)
        s_sel = jnp.einsum('xqd,xqjkd->xqjk', qc, k_sel).astype(f32)
        d_sel = t[None, :, None, None] - (ix[..., None] * MOBA_BLOCK + blk_off)
        ok = (ix < own_blk)[..., None]
        s_sel = jnp.where(ok, s_sel - slope_x[:, None, None, None] * d_sel.astype(f32), NEG)
        n_k = n_sel * MOBA_BLOCK
        scores = jnp.concatenate([s_sel.reshape(bh, MOBA_Q_CHUNK, n_k), s_own], axis=-1)
        p = jax.nn.softmax(scores, axis=-1).astype(v.dtype)
        p_sel = p[..., :n_k].reshape(bh, MOBA_Q_CHUNK, n_sel, MOBA_BLOCK)
        p_own = p[..., n_k:]
        return (jnp.einsum('xqjk,xqjkd->xqd', p_sel, v_sel)
                + jnp.einsum('xqk,xkd->xqd', p_own, v_own))

    out = lax.map(chunk, (q_chunks, sel_chunks, jnp.arange(nq)))
    return out.transpose(1, 0, 2, 3).reshape(b, h, sp, hd)[:, :, :s]

def hybrid_layer(x, norm_ffn1, ffn1_gate, ffn1_up, ffn1_down, norm_mix, w_in,
                 w_up_a, w_up_b, w_out, norm_ffn2, ffn2_gate, ffn2_up, ffn2_down):
    b, s, _ = x.shape
    x = x + 0.5 * swiglu(rmsnorm(x, norm_ffn1), ffn1_gate, ffn1_up, ffn1_down)
    h = rmsnorm(x, norm_mix)
    proj = h @ w_in
    o = 0
    parts = []
    for width in (DSA_WIDTH, DSA_WIDTH, DSA_WIDTH, MOBA_WIDTH, MOBA_WIDTH, MOBA_WIDTH,
                  D_MODEL, D_MODEL):
        parts.append(proj[..., o:o + width])
        o += width
    qa, ka, va, qb, kb, vb, g_a, g_b = parts
    scale = HEAD_DIM ** -0.5
    qa, ka, va = to_heads(qa, DSA_HEADS) * scale, to_heads(ka, DSA_HEADS), to_heads(va, DSA_HEADS)
    qb, kb, vb = to_heads(qb, MOBA_HEADS) * scale, to_heads(kb, MOBA_HEADS), to_heads(vb, MOBA_HEADS)

    slopes_a = alibi_slopes(DSA_HEADS)
    outs, lses = [], []
    for gi, (window, dilation) in enumerate(DSA_GROUPS):
        hs = slice(gi * DSA_HEADS_PER_GROUP, (gi + 1) * DSA_HEADS_PER_GROUP)
        og, lg = dilated_window_attention(qa[:, hs], ka[:, hs], va[:, hs], slopes_a[hs],
                                          window, dilation)
        outs.append(og)
        lses.append(lg)
    w_grp = jax.nn.softmax(jnp.stack(lses, 0), axis=0)
    y_a = jnp.sum(w_grp[..., None] * jnp.stack(outs, 0).astype(f32), axis=0).astype(x.dtype)
    y_a = y_a.transpose(0, 2, 1, 3).reshape(b, s, DSA_OUT)

    y_b = moba_attention(qb, kb, vb, alibi_slopes(MOBA_HEADS))
    y_b = y_b.transpose(0, 2, 1, 3).reshape(b, s, MOBA_WIDTH)

    merged = jax.nn.sigmoid(g_a) * (y_a @ w_up_a) + jax.nn.sigmoid(g_b) * (y_b @ w_up_b)
    x = x + merged @ w_out
    x = x + 0.5 * swiglu(rmsnorm(x, norm_ffn2), ffn2_gate, ffn2_up, ffn2_down)
    return x

def first_inputs(seed: int = 0) -> dict:
    key = jax.random.key(seed)
    ks = jax.random.split(key, 16)

    def dense(k, fan_in, fan_out):
        return jax.random.normal(k, (DEPTH, fan_in, fan_out), f32) * fan_in ** -0.5

    def gain(k):
        return 1.0 + 0.02 * jax.random.normal(k, (DEPTH, D_MODEL), f32)

    return {
        "x": jax.random.normal(ks[0], (BATCH, SEQ, D_MODEL), f32),
        "norm_ffn1": gain(ks[1]),
        "ffn1_gate": dense(ks[2], D_MODEL, D_FF),
        "ffn1_up": dense(ks[3], D_MODEL, D_FF),
        "ffn1_down": dense(ks[4], D_FF, D_MODEL),
        "norm_mix": gain(ks[5]),
        "w_in": dense(ks[6], D_MODEL, IN_WIDTH),
        "w_up_a": dense(ks[7], DSA_OUT, D_MODEL),
        "w_up_b": dense(ks[8], MOBA_WIDTH, D_MODEL),
        "w_out": dense(ks[9], D_MODEL, D_MODEL),
        "norm_ffn2": gain(ks[10]),
        "ffn2_gate": dense(ks[11], D_MODEL, D_FF),
        "ffn2_up": dense(ks[12], D_MODEL, D_FF),
        "ffn2_down": dense(ks[13], D_FF, D_MODEL),
        "norm_final": 1.0 + 0.02 * jax.random.normal(ks[14], (D_MODEL,), f32),
    }

def first_block(x, norm_ffn1, ffn1_gate, ffn1_up, ffn1_down, norm_mix, w_in, w_up_a,
              w_up_b, w_out, norm_ffn2, ffn2_gate, ffn2_up, ffn2_down, norm_final):
    for layer in range(DEPTH):
        x = hybrid_layer(x, norm_ffn1[layer], ffn1_gate[layer], ffn1_up[layer],
                         ffn1_down[layer], norm_mix[layer], w_in[layer], w_up_a[layer],
                         w_up_b[layer], w_out[layer], norm_ffn2[layer], ffn2_gate[layer],
                         ffn2_up[layer], ffn2_down[layer])
    return rmsnorm(x, norm_final)


MLA_HEADS = 8
MLA_NOPE_DIM = 64
MLA_ROPE_DIM = 32
MLA_QK_DIM = MLA_NOPE_DIM + MLA_ROPE_DIM
MLA_V_DIM = 64
MLA_WIDTH = MLA_HEADS * MLA_V_DIM
MLA_Q_RANK = 384
MLA_KV_RANK = 256
ROPE_THETA = 10000.0
Q_BLOCK = 128
GLA_HEADS = 4
GLA_DV = D_MODEL // 2
GLA_DK = GLA_DV // 2
GLA_HEAD_K = GLA_DK // GLA_HEADS
GLA_HEAD_V = GLA_DV // GLA_HEADS
GLA_GATE_RANK = 16
GLA_GATE_TAU = 16.0
GLA_CHUNK = 64
D_FF_2 = -(-8 * D_MODEL // (3 * 256)) * 256
NORM_EPS = 1e-6
IN_SIZES = (MLA_Q_RANK, MLA_KV_RANK, MLA_ROPE_DIM,
            GLA_DK, GLA_DK, GLA_DV, GLA_GATE_RANK, GLA_DV,
            D_MODEL, D_MODEL)
D_IN = sum(IN_SIZES)


def rmsnorm_2(x, w):
    xf = x.astype(jnp.float32)
    y = xf * lax.rsqrt(jnp.mean(xf * xf, axis=-1, keepdims=True) + NORM_EPS)
    return (y * w.astype(jnp.float32)).astype(x.dtype)

def rope_tables(positions):
    half = MLA_ROPE_DIM // 2
    inv = 1.0 / (ROPE_THETA ** (jnp.arange(half, dtype=jnp.float32) / half))
    ang = positions.astype(jnp.float32)[..., None] * inv
    return jnp.cos(ang), jnp.sin(ang)

def apply_rope(x, cos, sin):
    x1, x2 = jnp.split(x.astype(jnp.float32), 2, axis=-1)
    return jnp.concatenate([x1 * cos - x2 * sin, x2 * cos + x1 * sin], axis=-1).astype(x.dtype)

def mla(c_q, c_kv, k_rope, cos, sin, norm_cq, w_uq, norm_ckv, w_ukv):
    B, S, _ = c_q.shape
    H = MLA_HEADS
    q = (rmsnorm_2(c_q, norm_cq) @ w_uq).reshape(B, S, H, MLA_QK_DIM)
    q_nope, q_rope = q[..., :MLA_NOPE_DIM], q[..., MLA_NOPE_DIM:]
    q_rope = apply_rope(q_rope, cos[:, :, None], sin[:, :, None])
    kv = (rmsnorm_2(c_kv, norm_ckv) @ w_ukv).reshape(B, S, H, MLA_NOPE_DIM + MLA_V_DIM)
    k_nope, v = kv[..., :MLA_NOPE_DIM], kv[..., MLA_NOPE_DIM:]
    k_rope = apply_rope(k_rope, cos, sin)
    k = jnp.concatenate([k_nope, jnp.broadcast_to(k_rope[:, :, None], (B, S, H, MLA_ROPE_DIM)).astype(k_nope.dtype)], axis=-1)
    q = jnp.concatenate([q_nope, q_rope], axis=-1) * (MLA_QK_DIM ** -0.5)
    nb = S // Q_BLOCK
    q_blocks = q.reshape(B, nb, Q_BLOCK, H, MLA_QK_DIM).transpose(1, 0, 2, 3, 4)
    key_idx = jnp.arange(S)

    def attend(args):
        q_blk, start = args
        s = jnp.einsum('bqhd,bkhd->bhqk', q_blk, k).astype(jnp.float32)
        q_idx = start + jnp.arange(Q_BLOCK)
        mask = key_idx[None, :] <= q_idx[:, None]
        s = jnp.where(mask, s, -jnp.inf)
        p = jax.nn.softmax(s, axis=-1).astype(v.dtype)
        return jnp.einsum('bhqk,bkhd->bqhd', p, v)

    o = lax.map(attend, (q_blocks, jnp.arange(nb) * Q_BLOCK))
    return o.transpose(1, 0, 2, 3, 4).reshape(B, S, MLA_WIDTH)

def gla(q, k, v, g_lr, og, w_gate2, b_gate, norm_o):
    B, S, _ = q.shape
    H, C = GLA_HEADS, GLA_CHUNK
    n = S // C
    log_a = jax.nn.log_sigmoid((g_lr @ w_gate2 + b_gate).astype(jnp.float32)) / GLA_GATE_TAU

    def heads(t, d):
        return t.reshape(B, S, H, d).transpose(0, 2, 1, 3).astype(jnp.float32)

    def chunks(t):
        return t.reshape(B, H, n, C, t.shape[-1]).transpose(2, 0, 1, 3, 4)

    qh = heads(q, GLA_HEAD_K) * (GLA_HEAD_K ** -0.5)
    kh = heads(k, GLA_HEAD_K)
    vh = heads(v, GLA_HEAD_V)
    gh = heads(log_a, GLA_HEAD_K)
    bcum = jnp.cumsum(chunks(gh), axis=3)
    causal = jnp.tril(jnp.ones((C, C), dtype=bool))

    def step(state, xs):
        qc, kc, vc, bc = xs
        o_inter = jnp.einsum('bhcd,bhde->bhce', qc * jnp.exp(bc), state)
        diff = bc[:, :, :, None, :] - bc[:, :, None, :, :]
        decay = jnp.exp(jnp.where(causal[:, :, None], diff, -jnp.inf))
        attn = jnp.einsum('bhid,bhjd,bhijd->bhij', qc, kc, decay)
        o_intra = jnp.einsum('bhij,bhje->bhie', attn, vc)
        b_last = bc[:, :, -1:, :]
        k_dec = kc * jnp.exp(b_last - bc)
        state = jnp.exp(b_last[:, :, 0, :])[..., None] * state + jnp.einsum('bhcd,bhce->bhde', k_dec, vc)
        return state, o_inter + o_intra

    state0 = jnp.zeros((B, H, GLA_HEAD_K, GLA_HEAD_V), jnp.float32)
    _, o = lax.scan(step, state0, (chunks(qh), chunks(kh), chunks(vh), bcum))
    o = o.transpose(1, 0, 3, 2, 4).reshape(B, S, H, GLA_HEAD_V)
    o = rmsnorm_2(o, norm_o).reshape(B, S, GLA_DV)
    o = o * jax.nn.silu(og.astype(jnp.float32))
    return o.astype(q.dtype)

def second_inputs(seed: int = 0) -> dict:
    key = jax.random.key(seed)
    ks = jax.random.split(key, 24)
    L, D = DEPTH, D_MODEL

    def w(k, shape, fan_in):
        return jax.random.normal(k, shape, jnp.float32) * (fan_in ** -0.5)

    def gain(k, shape):
        return 1.0 + 0.02 * jax.random.normal(k, shape, jnp.float32)

    return {
        "x": jax.random.normal(ks[0], (BATCH, SEQ, D), jnp.float32),
        "positions": jnp.broadcast_to(jnp.arange(SEQ, dtype=jnp.int32), (BATCH, SEQ)),
        "ln_mix": gain(ks[1], (L, D)),
        "w_in": w(ks[2], (L, D, D_IN), D),
        "mla_norm_cq": gain(ks[3], (L, MLA_Q_RANK)),
        "mla_w_uq": w(ks[4], (L, MLA_Q_RANK, MLA_HEADS * MLA_QK_DIM), MLA_Q_RANK),
        "mla_norm_ckv": gain(ks[5], (L, MLA_KV_RANK)),
        "mla_w_ukv": w(ks[6], (L, MLA_KV_RANK, MLA_HEADS * (MLA_NOPE_DIM + MLA_V_DIM)), MLA_KV_RANK),
        "mla_w_o": w(ks[7], (L, MLA_WIDTH, D), MLA_WIDTH),
        "gla_w_gate2": w(ks[8], (L, GLA_GATE_RANK, GLA_DK), GLA_GATE_RANK),
        "gla_b_gate": 0.1 * jax.random.normal(ks[9], (L, GLA_DK), jnp.float32),
        "gla_norm": gain(ks[10], (L, GLA_HEAD_V)),
        "gla_w_o": w(ks[11], (L, GLA_DV, D), GLA_DV),
        "w_out": w(ks[12], (L, D, D), D),
        "ln_ffn": gain(ks[13], (L, D)),
        "ffn_w_gate": w(ks[14], (L, D, D_FF_2), D),
        "ffn_w_up": w(ks[15], (L, D, D_FF_2), D),
        "ffn_w_down": w(ks[16], (L, D_FF_2, D), D_FF_2),
        "final_norm": gain(ks[17], (D,)),
    }

def second_block(x, positions, ln_mix, w_in, mla_norm_cq, mla_w_uq, mla_norm_ckv, mla_w_ukv, mla_w_o,
              gla_w_gate2, gla_b_gate, gla_norm, gla_w_o, w_out, ln_ffn, ffn_w_gate, ffn_w_up,
              ffn_w_down, final_norm):
    offsets = np.cumsum(IN_SIZES)[:-1].tolist()
    cos, sin = rope_tables(positions)
    h = x
    for l in range(DEPTH):
        u = rmsnorm_2(h, ln_mix[l])
        z = u @ w_in[l]
        c_q, c_kv, k_rope, g_q, g_k, g_v, g_lr, g_og, gate_a, gate_b = jnp.split(z, offsets, axis=-1)
        y_a = mla(c_q, c_kv, k_rope, cos, sin, mla_norm_cq[l], mla_w_uq[l], mla_norm_ckv[l], mla_w_ukv[l]) @ mla_w_o[l]
        y_b = gla(g_q, g_k, g_v, g_lr, g_og, gla_w_gate2[l], gla_b_gate[l], gla_norm[l]) @ gla_w_o[l]
        mix = jax.nn.sigmoid(gate_a) * y_a + jax.nn.sigmoid(gate_b) * y_b
        h = h + mix @ w_out[l]
        u = rmsnorm_2(h, ln_ffn[l])
        h = h + (jax.nn.silu(u @ ffn_w_gate[l]) * (u @ ffn_w_up[l])) @ ffn_w_down[l]
    return rmsnorm_2(h, final_norm)


def setup_inputs(seed=0):
    out = dict(first_inputs(seed))
    for name, value in second_inputs(seed + 1).items():
        if name != "x":
            out[name + "_2"] = value
    return out


def reference(
    x, norm_ffn1, ffn1_gate, ffn1_up, ffn1_down, norm_mix, w_in, w_up_a, w_up_b, w_out,
    norm_ffn2, ffn2_gate, ffn2_up, ffn2_down, norm_final, positions_2, ln_mix_2, w_in_2,
    mla_norm_cq_2, mla_w_uq_2, mla_norm_ckv_2, mla_w_ukv_2, mla_w_o_2, gla_w_gate2_2,
    gla_b_gate_2, gla_norm_2, gla_w_o_2, w_out_2, ln_ffn_2, ffn_w_gate_2, ffn_w_up_2,
    ffn_w_down_2, final_norm_2,
):
    x = first_block(
        x, norm_ffn1, ffn1_gate, ffn1_up, ffn1_down, norm_mix, w_in, w_up_a, w_up_b, w_out,
        norm_ffn2, ffn2_gate, ffn2_up, ffn2_down, norm_final,
    )
    return second_block(
        x, positions_2, ln_mix_2, w_in_2, mla_norm_cq_2, mla_w_uq_2, mla_norm_ckv_2,
        mla_w_ukv_2, mla_w_o_2, gla_w_gate2_2, gla_b_gate_2, gla_norm_2, gla_w_o_2, w_out_2,
        ln_ffn_2, ffn_w_gate_2, ffn_w_up_2, ffn_w_down_2, final_norm_2,
    )


_drawn_inputs = setup_inputs


def setup_inputs(seed=0):
    import zlib

    import numpy as np

    out = dict(_drawn_inputs(seed))
    spreads = {}
    factors = {'norm_ffn1': 4.603,
     'norm_mix': 5.305,
     'norm_ffn2': 5.871,
     'ln_mix_2': 3.692,
     'mla_norm_cq_2': 8.0,
     'mla_norm_ckv_2': 8.0,
     'gla_b_gate_2': 4.179,
     'gla_norm_2': 8.0,
     'ln_ffn_2': 12.385,
     'final_norm_2': 8.064}
    for name, (base, spread) in spreads.items():
        noise = np.random.default_rng([zlib.crc32(name.encode()), seed]).standard_normal(out[name].shape)
        drawn = base * np.exp(spread * noise) if base else spread * noise
        out[name] = __import__('jax').numpy.asarray(drawn.astype(out[name].dtype))
    for name, factor in factors.items():
        out[name] = (out[name] * factor).astype(out[name].dtype)
    return out
```

```python
import math

import numpy as np
import concourse.bass as bass
from concourse import mybir

F32 = mybir.dt.float32
F32R = mybir.dt.float32r
I32 = mybir.dt.int32
ALU = mybir.AluOpType
ACT = mybir.ActivationFunctionType
AX = mybir.AxisListType

P = 128
BASE = 16384 + 128
T = 256
TT = T // P
D = 1024
KD = D // P
FF = 2816
NF = FF // P
EPS = 1e-6
HD = 64
GROUPS = ((128, 1), (512, 4), (2048, 16))
DSA_J = 4
DSA_W = 768
MOBA_W = 512
MLA_QK, MLA_NOPE, MLA_ROPE = 96, 64, 32
CQ, CKV = 384, 256
HEADS = 8
GLA_LEVELS = (128, 64, 32, 16, 8, 4, 2, 1)
GLA_CHUNK = 64
FAR = 1e33
RING = 4
RAW_W = 8 * 288
DOWN_K = ((0, 6), (6, 12), (12, 17), (17, 22))

QA, KA, VA = 0, DSA_W, 2 * DSA_W
QB = 3 * DSA_W
KB, VB = QB + MOBA_W, QB + 2 * MOBA_W
GA = QB + 3 * MOBA_W
C_KV = CQ
C_GQ = CQ + CKV + MLA_ROPE
C_GK, C_GV, C_LR = C_GQ + 256, C_GQ + 512, C_GQ + 1024
C_OG = C_LR + 16
C_GATES = C_OG + 512

VEC = {"norm_ffn1": 0, "norm_mix": 8, "norm_ffn2": 16, "norm_final": 24, "ln_mix_2": 32, "ln_ffn_2": 40,
       "final_norm_2": 48, "mla_norm_cq_2": 56, "mla_norm_ckv_2": 59, "gla_b_gate_2": 61, "gla_norm_2": 63}
NVEC = 64

C_IDENT, C_ONES, C_SEG, C_INV, C_SIGN = 0, 128, 256, 768 + 512, 768 + 513
C_DIST = C_SIGN + 1
NSEG = 384
N_CONST = C_DIST + 5 * NSEG


def constants():
    c = np.zeros((P, N_CONST), np.float32)
    c[:, C_IDENT:C_IDENT + P] = np.eye(P)
    c[:, C_ONES:C_ONES + P] = 1
    t = np.arange(2 * T)
    c[:, C_SEG:C_SEG + 2 * T] = t % GLA_CHUNK != 0
    c[:, C_SEG + 2 * T:C_SEG + 4 * T] = t % T != 0
    half = MLA_ROPE // 2
    inv = (np.float32(1.0) / (np.float32(10000.0) ** (np.arange(half, dtype=np.float32) / half))).astype(np.float32)
    p = np.arange(P)
    c[:, C_INV] = inv[p % half]
    c[:, C_SIGN] = np.where(p % MLA_ROPE < half, -1, 1)
    for g in range(5):
        for q0, k1, at in ((0, P, 0), (P, 2 * P, P)):
            d = (q0 + p[:, None]) - np.arange(k1)[None]
            ok = d >= 0
            if g < 3:
                window, dilation = GROUPS[g]
                ok &= (d <= window) & (d % dilation == 0)
            v = np.where(ok, d if g < 4 else 0, FAR)
            c[:, C_DIST + g * NSEG + at:C_DIST + g * NSEG + at + k1] = v
    m = np.zeros((P, 7, P), np.int32)
    j, i = p[:, None], p[None]
    for n, s in enumerate(GLA_LEVELS[2:]):
        m[:, n] = (j // (2 * s) == i // (2 * s)) & (j % (2 * s) < s) & (i % (2 * s) >= s)
    m[:, 6] = j == i
    return c, m.reshape(P, 7 * P)


class Half:

    def __init__(self, unit, kt, pieces):
        self.unit, self.kt, self.pieces = unit, kt, pieces

    def views(self, raw, part):
        return [(src(raw), dst(part[:, 0:self.kt * P].rearrange("p (k c) -> p k c", c=P)))
                for src, dst in self.pieces]


def plain(kt, width, c0):
    return [(lambda raw: raw[:, 0:kt * width].rearrange("p (k c) -> p k c", c=width)[:, :, c0:c0 + P],
             lambda part: part)]


def block2(kt, width, c0, stride, n, size):
    def src(raw):
        v = raw[:, 0:kt * width].rearrange("p (k g c) -> p k g c", k=kt, c=stride)
        return v[:, :, c0 // stride:c0 // stride + n, c0 % stride:c0 % stride + size]
    return [(src, lambda part: part.rearrange("p k (g c) -> p k g c", c=size))]


def swapped(kt, width, c0, stride, n):
    h = MLA_ROPE // 2
    out = []
    for e in range(2):
        def src(raw, e=e):
            v = raw[:, 0:kt * width].rearrange("p (k g c) -> p k g c", k=kt, c=stride)
            a = c0 % stride + (1 - e) * h
            return v[:, :, c0 // stride:c0 // stride + n, a:a + h]
        out.append((src, lambda part, e=e: part.rearrange("p k (g c) -> p k g c", c=MLA_ROPE)[
            :, :, :, e * h:e * h + h]))
    return out


def copies(kt, width, runs):
    total = sum(s for _, s in runs)
    out, at = [], 0
    for c0, size in runs:
        def src(raw, c0=c0, size=size):
            v = raw[:, 0:kt * width].rearrange("p (k c) -> p k c", c=width)[:, :, c0:c0 + size]
            return v.unsqueeze(2).to_broadcast([P, kt, P // total, size])
        out.append((src, lambda part, at=at, size=size: part.rearrange("p k (g c) -> p k g c", c=total)[
            :, :, :, at:at + size]))
        at += size
    return out


def mix1_plan(w):
    units, halves = [], []
    w_in = w["w_in"].rearrange("(k p) c -> p k c", p=P)

    def cols(c0):
        units.append([(0, KD, 256, w_in[:, :, c0:c0 + 256])])
        for h in range(2):
            halves.append(Half(len(units) - 1, KD, plain(KD, 256, h * P)))
    for c0 in range(QA, GA + 2 * D, 256):
        cols(c0)
    ua = w["w_up_a"].rearrange("(k p) c -> p k c", p=P)
    ub = w["w_up_b"].rearrange("(k p) c -> p k c", p=P)
    for c0 in range(0, D, 256):
        units.append([(0, 2, 256, ua[:, :, c0:c0 + 256]), (2, 4, 256, ub[:, :, c0:c0 + 256])])
        for h in range(2):
            halves.append(Half(len(units) - 1, 6, plain(6, 256, h * P)))
    wo = w["w_out"].rearrange("(k p) c -> p k c", p=P)
    for c0 in range(0, D, 256):
        units.append([(0, KD, 256, wo[:, :, c0:c0 + 256])])
        for h in range(2):
            halves.append(Half(len(units) - 1, KD, plain(KD, 256, h * P)))
    return units, halves


M1 = dict(qa=0, ka=6, va=12, qb=18, kb=22, vb=26, gates=30, merge=46, out=54, end=62)
M1_TOKEN = (12, 14, 16, 26, 28)
M2 = dict(lr=0, og=1, gq=3, gk=5, og2=7, kr=9, ckv=11, cq=13, gv=16, uq=20, uqr=24, ukv=28, uv=32,
          gates=36, merge=52, out=60, end=68)
M2_TOKEN = (16, 18, 32, 34)


def mix2_plan(w):
    units, halves = [], []
    w_in = w["w_in_2"].rearrange("(k p) c -> p k c", p=P)

    def unit(c0, width):
        units.append([(0, KD, width, w_in[:, :, c0:c0 + width])])
        return len(units) - 1

    def half(u, pieces, kt=KD):
        halves.append(Half(u, kt, pieces))

    u = unit(C_LR, 272)
    half(u, copies(KD, 272, [(0, 16)]))
    for h in range(2):
        half(u, plain(KD, 272, 16 + h * P))
    for c0 in (C_GQ, C_GK, C_OG + 256):
        u = unit(c0, 256)
        for h in range(2):
            half(u, plain(KD, 256, h * P))
    u = unit(C_KV, 288)
    half(u, copies(KD, 288, [(256, 32)]))
    half(u, copies(KD, 288, [(272, 16), (256, 16)]))
    for h in range(2):
        half(u, plain(KD, 288, h * P))
    u = unit(0, 256)
    for h in range(2):
        half(u, plain(KD, 256, h * P))
    half(unit(256, P), plain(KD, P, 0))
    for c0 in (C_GV, C_GV + 256):
        u = unit(c0, 256)
        for h in range(2):
            half(u, plain(KD, 256, h * P))
    kq, kk = CQ // P, CKV // P
    units.append([(0, kq, 768, w["mla_w_uq_2"].rearrange("(k p) c -> p k c", p=P))])
    u = len(units) - 1
    for c in range(4):
        half(u, block2(kq, 768, 2 * c * MLA_QK, MLA_QK, 2, MLA_NOPE), kq)
    for c in range(2):
        half(u, block2(kq, 768, 4 * c * MLA_QK + MLA_NOPE, MLA_QK, 4, MLA_ROPE), kq)
    for c in range(2):
        half(u, swapped(kq, 768, 4 * c * MLA_QK + MLA_NOPE, MLA_QK, 4), kq)
    units.append([(0, kk, 1024, w["mla_w_ukv_2"].rearrange("(k p) c -> p k c", p=P))])
    u = len(units) - 1
    for part in (0, MLA_NOPE):
        for c in range(4):
            half(u, block2(kk, 1024, 2 * c * P + part, P, 2, HD), kk)
    for c0 in range(C_GATES, C_GATES + 2 * D, 256):
        u = unit(c0, 256)
        for h in range(2):
            half(u, plain(KD, 256, h * P))
    oa = w["mla_w_o_2"].rearrange("(k p) c -> p k c", p=P)
    ob = w["gla_w_o_2"].rearrange("(k p) c -> p k c", p=P)
    for c0 in range(0, D, 256):
        units.append([(0, 4, 256, oa[:, :, c0:c0 + 256]), (4, 4, 256, ob[:, :, c0:c0 + 256])])
        for h in range(2):
            half(len(units) - 1, plain(8, 256, h * P), 8)
    wo = w["w_out_2"].rearrange("(k p) c -> p k c", p=P)
    for c0 in range(0, D, 256):
        units.append([(0, KD, 256, wo[:, :, c0:c0 + 256])])
        for h in range(2):
            half(len(units) - 1, plain(KD, 256, h * P))
    return units, halves


FFN_HALVES, FFN_UNITS = 4 * (NF // 2) + 4 * KD, NF + 4 * KD
FFN_UP = 4 * (NF // 2)
N_HALVES = (FFN_HALVES, M1["end"], FFN_HALVES, M2["end"], FFN_HALVES)
N_UNITS = (FFN_UNITS, 31, FFN_UNITS, 27, FFN_UNITS)
J0 = [sum(N_HALVES[:i]) for i in range(6)]
U0 = [sum(N_UNITS[:i]) for i in range(6)]

ROOTS = {n: i for i, n in enumerate(["x0", "x1", "x2", "x3", "y3", "ckv", "cq", "gla", "x4", "x5"])}

FIN_BANK = (0, 1, 2, 3, 4, 5, 7, 0)
NSEG1, NSEG2 = 20, 8
N_DSA = 12
SCORES1 = [12 + s for s in range(N_DSA)] + [14 + s for s in range(N_DSA, NSEG1)]
TURN1 = [17 + s for s in range(NSEG1)]
SCORES2 = [36 + s for s in range(NSEG2)]
TURN2 = [39 + s for s in range(NSEG2)]
OUT_LAG = 2
Z_AT, LEVEL_AT, GLA_O_AT, GLA_TURN_AT = 2, 9, 20, 23
SUM_CKV_AT, SUM_CQ_AT, COL_CKV_AT = 14, 17, 22
OG_HALVES = (1, 2, 7, 8)


def alibi(n, of):
    return 2.0 ** (-8.0 * (n + 1) / of)


def build(nc, w, out):
    units1, halves1 = mix1_plan(w)
    units2, halves2 = mix2_plan(w)
    assert len(units1) == N_UNITS[1] and len(halves1) == M1["end"]
    assert len(units2) == N_UNITS[3] and len(halves2) == M2["end"]

    top = [BASE]

    def place(name, shape, dt=F32, at=None):
        words = int(np.prod(shape[1:]))
        if at is None:
            at = top[0]
            top[0] += 4 * words
            top[0] += -top[0] % 32
        return nc.alloc_sbuf_tensor_at(name, list(shape), dt, offset=at)

    raw = place("raw", [P, RING, RAW_W])
    hi = place("hi", [P, RING, 8 * P], F32R)
    lo = place("lo", [P, RING, 8 * P], F32R)
    x = place("x", [P, KD, T])
    xh = place("xh", [P, KD, T], F32R)
    xl = place("xl", [P, KD, T], F32R)
    cst = place("cst", [P, C_DIST])
    dist_at = top[0]
    dist = place("dist", [P, 5, NSEG])
    masks = place("masks", [P, 7, P], I32)
    vec = place("vec", [P, NVEC])
    vec2 = place("vec2", [P, 16])
    cosT = place("cosT", [P, T], at=dist_at)
    sinT = place("sinT", [P, T], at=dist_at + 1024)
    rope_q = place("rope_q", [P, 2, T], at=dist_at + 2048)
    rope_k = place("rope_k", [P, 2, T], at=dist_at + 4096)
    acc = place("acc", [P, 2, T])
    sq = place("sq", [P, 2, T])
    R = place("R", [P, T])
    R1 = place("R1", [P, T])
    newton = place("newton", [P, T], at=top[0])
    Rq = place("Rq", [P, T])
    pos_i = place("pos_i", [P, T], I32, at=top[0])
    Rkv = place("Rkv", [P, T])
    var = place("var", [P, T])
    root = place("root", [P, T])
    rcol = place("rcol", [P, 2 * TT])
    tg = place("tg", [P, 2, T])
    tu = place("tu", [P, 2, T])
    sg = place("sg", [P, 2, T])
    hf = place("hf", [P, 2, T])
    region = top[0]
    hh = place("hh", [P, NF, T], F32R, at=region)
    hl = place("hl", [P, NF, T], F32R, at=region + 4 * NF * T)
    K = 1024
    x_in = place("x_in", [P, TT, D], at=region)
    vrow = place("vrow", [NVEC, P], at=region + 8 * K)
    qa = place("qa", [P, 6, T], at=region)
    ka = place("ka", [P, 6, T], at=region + 6 * K)
    va = place("va", [P, TT, DSA_W], at=region + 12 * K)
    gates1 = place("gates1", [P, 16, T], at=region)
    qb = place("qb", [P, 4, T], at=region + 18 * K)
    kb = place("kb", [P, 4, T], at=region + 22 * K)
    vb = place("vb", [P, TT, MOBA_W], at=region + 26 * K)
    mh1 = place("mh1", [P, KD, T], F32R, at=region + 18 * K)
    ml1 = place("ml1", [P, KD, T], F32R, at=region + 26 * K)
    s1 = place("s1", [P, 3, NSEG], at=region + 34 * K)
    p1 = place("p1", [P, 2, 3, NSEG], at=region + 39 * K)
    pt1 = place("pt1", [P, 2, NSEG], at=region + 48 * K)
    y1h = place("y1h", [P, 6, T], F32R, at=region + 51 * K)
    y1l = place("y1l", [P, 6, T], F32R, at=region + 57 * K)
    end1 = region + 63 * K
    ckv = place("ckv", [P, 2, T], at=region)
    ckvh = place("ckvh", [P, 2, T], F32R, at=region + 2 * K)
    ckvl = place("ckvl", [P, 2, T], F32R, at=region + 4 * K)
    cq = place("cq", [P, 3, T], at=region + 6 * K)
    cqh = place("cqh", [P, 3, T], F32R, at=region + 9 * K)
    cql = place("cql", [P, 3, T], F32R, at=region + 12 * K)
    gates2 = place("gates2", [P, 16, T], at=region)
    qn = place("qn", [P, 4, T], at=region + 16 * K)
    kn = place("kn", [P, 4, T], at=region + 20 * K)
    mv = place("mv", [P, TT, 512], at=region + 24 * K)
    qr = place("qr", [P, 2, T], at=region + 28 * K)
    kr = place("kr", [P, 1, T], at=region + 30 * K)
    mh2 = place("mh2", [P, KD, T], F32R, at=region + 16 * K)
    ml2 = place("ml2", [P, KD, T], F32R, at=region + 24 * K)
    gq = place("gq", [P, 2, T], at=region + 32 * K)
    gk = place("gk", [P, 2, T], at=region + 34 * K)
    run_chunk = place("run_chunk", [P, 2, T], at=region + 36 * K)
    run_all = place("run_all", [P, 2, T], at=region + 38 * K)
    s2 = place("s2", [P, 2, NSEG], at=region + 32 * K)
    p2 = place("p2", [P, 3, NSEG], at=region + 35 * K)
    pt2 = place("pt2", [P, 2, NSEG], at=dist_at + 2048)
    gv = place("gv", [P, TT, 512], at=region + 40 * K)
    lvq = place("lvq", [P, 2, 2, T], at=region + 44 * K)
    lvk = place("lvk", [P, 2, 2, T], at=region + 48 * K)
    y2ah = place("y2ah", [P, 4, T], F32R, at=region + 44 * K)
    y2al = place("y2al", [P, 4, T], F32R, at=region + 48 * K)
    at3 = place("at3", [P, 3, 4, P], at=region + 52 * K)
    osq = place("osq", [P, TT, 512], at=region + 44 * K)
    go_y = place("go_y", [P, 4, T], at=region + 52 * K)
    lr = place("lr", [P, T], at=region + 58 * K)
    wg2 = place("wg2", [16, 256], at=region + 59 * K)
    og = place("og", [P, 4, T], at=region + 60 * K)
    y2bh = place("y2bh", [P, 4, T], F32R, at=region + 56 * K)
    y2bl = place("y2bl", [P, 4, T], F32R, at=region + 40 * K)
    go = place("go", [P, TT, 512], at=region + 36 * K)
    zl = place("zl", [P, 2, T], at=region + 52 * K)
    ze = place("ze", [P, 2, T], at=region + 54 * K)
    end2 = region + 64 * K
    top[0] = max(end1, end2, region + 8 * NF * T)
    nmax = place("nmax", [P, 4])
    ssum = place("ssum", [P, 4])
    sinv = place("sinv", [P, 4])
    gss = place("gss", [P, 5, 8])
    assert top[0] <= 207 * K, top[0]
    o_fm = place("o_fm", [P, KD, T], at=region)
    o_tm = place("o_tm", [P, TT, D], at=region + 8 * K)
    lvd, lve = hf, sg
    ps = [nc.alloc_psum_tensor(f"bank{i}", [P, 512], F32) for i in range(8)]

    ident = cst[:, C_IDENT:C_IDENT + P]
    ones = cst[:, C_ONES:C_ONES + P]

    def sem(name):
        return nc.alloc_semaphore(name)

    raw_landed = [sem(f"raw_landed{i}") for i in range(RING)]
    const_in, x_landed, vec_in, dist_in, small_in, pos_in = (
        sem(n) for n in ("const_in", "x_landed", "vec_in", "dist_in", "small_in", "pos_in"))
    split_hi, split_lo, half_done = sem("split_hi"), sem("split_lo"), sem("half_done")
    vec_turned, vec_ready, x_turned = sem("vec_turned"), sem("vec_ready"), sem("x_turned")
    x_updated, xh_ready, xl_ready, acc_ready = (
        sem(n) for n in ("x_updated", "xh_ready", "xl_ready", "acc_ready"))
    sums_ready, var_ready, root_ready, r_ready = (
        sem(n) for n in ("sums_ready", "var_ready", "root_ready", "r_ready"))
    rcol_turned, rcol_ready = sem("rcol_turned"), sem("rcol_ready")
    gate_scaled, up_scaled, silu_ready, hidden_ready, hidden_hi, hidden_lo = (
        sem(n) for n in ("gate_scaled", "up_scaled", "silu_ready", "hidden_ready", "hidden_hi", "hidden_lo"))
    half_taken = sem("half_taken")
    z_ready, tanh_ready, sig_ready = sem("z_ready"), sem("tanh_ready"), sem("sig_ready")
    cx_ready, cx_hi, cx_lo, cx_acc = sem("cx_ready"), sem("cx_hi"), sem("cx_lo"), sem("cx_acc")
    merge_ab, merged, merged_hi, merged_lo = sem("merge_ab"), sem("merged"), sem("merged_hi"), sem("merged_lo")
    seg_scores, seg_biased, seg_max, seg_probs = (
        sem(n) for n in ("seg_scores", "seg_biased", "seg_max", "seg_probs"))
    seg_inv, seg_norm, seg_turned, seg_copied, seg_out, y_hi, y_lo = (
        sem(n) for n in ("seg_inv", "seg_norm", "seg_turned", "seg_copied", "seg_out", "y_hi", "y_lo"))
    decay_raw, decay_taken, decay_logs = sem("decay_raw"), sem("decay_taken"), sem("decay_logs")
    lv_zero, lv_diff, lv_exp, lv_ready, lv_done, lv_taken = (
        sem(n) for n in ("lv_zero", "lv_diff", "lv_exp", "lv_ready", "lv_done", "lv_taken"))
    gla_out, gla_scaled, gla_turned, gla_y, yb_hi, yb_lo = (
        sem(n) for n in ("gla_out", "gla_scaled", "gla_turned", "gla_y", "yb_hi", "yb_lo"))
    residual_scaled = sem("residual_scaled")
    sin_arg, sin_ready = sem("sin_arg"), sem("sin_ready")
    fin_ready, fin_turned, fin_scaled, out_stored = (
        sem(n) for n in ("fin_ready", "fin_turned", "fin_scaled", "out_stored"))
    dve_step, act_step, pool_step = sem("dve_step"), sem("act_step"), sem("pool_step")

    W_UP = (("ffn1_gate", "ffn1_up", "ffn1_down"), ("ffn2_gate", "ffn2_up", "ffn2_down"),
            ("ffn_w_gate_2", "ffn_w_up_2", "ffn_w_down_2"))
    JF, UF, EF = [J0[0], J0[2], J0[4]], [U0[0], U0[2], U0[4]], [0, NF, 2 * NF]
    GAIN = [vec[:, VEC["norm_ffn1"]:], vec[:, VEC["norm_mix"]:], vec[:, VEC["norm_ffn2"]:], vec2[:, 0:8],
            vec[:, VEC["ln_ffn_2"]:], vec[:, VEC["final_norm_2"]:]]

    def part_of(j):
        n = max(i for i in range(5) if J0[i] <= j)
        return n, j - J0[n]

    def ffn_half(q):
        if q < FFN_UP:
            i, r = divmod(q, 4)
            return 2 * i + r % 2, KD, (r // 2) * P, 256
        k0, k1 = DOWN_K[(q - FFN_UP) % 4]
        return NF + q - FFN_UP, k1 - k0, 0, P

    def half_views(j, part):
        n, q = part_of(j)
        slot = part[:, j % RING, :]
        if n % 2 == 0:
            u, kt, c0, width = ffn_half(q)
            h = Half(u, kt, plain(kt, width, c0))
        else:
            h = (halves1, halves2)[n // 2][q]
        u = U0[n] + h.unit
        return h.views(raw[:, u % RING, :], slot), u

    def last_half(u):
        n = max(i for i in range(5) if U0[i] <= u)
        v = u - U0[n]
        if n % 2 == 0:
            q = 4 * (v // 2) + 2 + v % 2 if v < NF else FFN_UP + v - NF
        else:
            q = max(i for i, h in enumerate((halves1, halves2)[n // 2]) if h.unit == v)
        return J0[n] + q

    def w_part(part, j, k):
        return part[:, j % RING, k * P:(k + 1) * P]

    def w_pair(part, j, k):
        s = j % RING
        return part[:, s:s + 2, k * P:(k + 1) * P]

    def last_segment(k):
        return 3 * k + 2 if k < 4 else N_DSA + k - 4

    def scores1(k):
        s = last_segment(k)
        return s1[:, :, :] if k < 4 else s1[:, s % 3:s % 3 + 1, :]

    def probs1(k):
        s = last_segment(k)
        return p1[:, k % 2, :, :] if k < 4 else p1[:, 0, s % 3:s % 3 + 1, :]

    def probs1_of(s):
        return p1[:, (s // 3) % 2, s % 3, :] if s < N_DSA else p1[:, 0, s % 3, :]

    def taken(part, n):
        first = M1 if part == 1 else M2
        if n >= first["merge"]:
            return merge_ab, 2 * ((0 if part == 1 else KD) + n - first["merge"] + 1)
        if n >= first["gates"]:
            return z_ready, (0 if part == 1 else 20) + n - first["gates"] + 1
        if part == 1:
            return half_taken, n + 1
        if n in OG_HALVES:
            return z_ready, 16 + OG_HALVES.index(n) + 1
        if M2["ckv"] <= n < M2["gv"]:
            return cx_ready, n - M2["ckv"] + 1
        other = len([i for i in range(n) if i in OG_HALVES or M2["ckv"] <= i < M2["gv"]])
        return half_taken, M1["gates"] + n - other + 1

    block = nc.Block()
    block_ctx = block.__enter__()

    @block_ctx.sync
    def _(sp):
        def load(u, pieces, value=None, freed=None):
            if u >= RING or freed is not None:
                sp.wait_ge(split_lo, last_half(u - RING) + 1 if freed is None else freed)
            for k0, kt, width, src in pieces:
                dst = raw[:, u % RING, k0 * width:(k0 + kt) * width].rearrange("p (k c) -> p k c", c=width)
                sp.dma_start(dst, src).then_inc(raw_landed[u % RING], 16)

        def ffn(f):
            gate, up, down = (w[n] for n in W_UP[f])
            gate = gate.rearrange("(k p) c -> p k c", p=P)
            up = up.rearrange("(k p) c -> p k c", p=P)
            down = down.rearrange("(k p) c -> p k c", p=P)

            def pair(i, at, freed=None):
                for r, src in enumerate((gate, up)):
                    load(UF[f] + 2 * at + r, [(0, KD, 256, src[:, :, bass.ds(i * 256, 256)])],
                         freed=None if freed is None else freed + r)
            for i in range(3):
                pair(i, i)
            with sp.Fori(0, (NF // 2 - 3) // 2) as i:
                for b in range(2):
                    pair(i * 2 + (3 + b), 3 + b, freed=i * 8 + (JF[f] + 4 * (1 + b) + 3))
            for q in range(4 * KD):
                k0, k1 = DOWN_K[q % 4]
                m = q // 4
                load(UF[f] + NF + q, [(0, k1 - k0, P, down[:, k0:k1, m * P:(m + 1) * P])])

        def mixing(n, units):
            for v, pieces in enumerate(units):
                load(U0[n] + v, pieces)

        ffn(0)
        mixing(1, units1)
        ffn(1)
        mixing(3, units2)
        ffn(2)
        for t in range(TT):
            sp.wait_ge(fin_scaled, 4 * (t + 1))
            sp.dma_start(out[t * P:(t + 1) * P, :], o_tm[:, t, :]).then_inc(out_stored, 16)
        sp.wait_ge(out_stored, 16 * TT)

    def landed(eng, u):
        eng.wait_ge(raw_landed[u % RING], LANDED[u])

    LANDED = {}
    count = [0] * RING
    for u in range(U0[5]):
        n = max(i for i in range(5) if U0[i] <= u)
        pieces = 1 if n % 2 == 0 else len((units1, units2)[n // 2][u - U0[n]])
        count[u % RING] += 16 * pieces
        LANDED[u] = count[u % RING]

    @block_ctx.scalar
    def _(act):
        steps = [0]

        def link(ins):
            steps[0] += 1
            ins.then_inc(act_step, 1)
            act.wait_ge(act_step, steps[0])

        act.dma_start(cst[:, :], w["consts"][:, 0:C_DIST]).then_inc(const_in, 16)
        act.dma_start(x_in[:, :, :], w["x"].rearrange("b (t p) d -> p (b t) d", p=P)).then_inc(x_landed, 16)
        for name, at in VEC.items():
            n = w[name].shape[-1] // P
            src = w[name] if len(w[name].shape) == 1 else w[name][0]
            act.dma_start(vrow[at:at + n, :], src.rearrange("(a b) -> a b", b=P)).then_inc(vec_in, 16)
        act.dma_start(dist[:, :, :], w["consts"][:, C_DIST:].rearrange("p (g c) -> p g c", c=NSEG)
                      ).then_inc(dist_in, 16)
        act.dma_start(masks[:, :, :], w["masks"].rearrange("p (g c) -> p g c", c=P)).then_inc(dist_in, 16)

        def split(j):
            views, u = half_views(j, hi)
            landed(act, u)
            if j >= RING:
                act.wait_ge(half_done, j - RING + 1)
            for n, (src, dst) in enumerate(views):
                ins = act.activation(dst, src, ACT.Copy)
                if n == len(views) - 1:
                    ins.then_inc(split_hi, 1)

        def x_parts(wv):
            def tile(m):
                act.wait_ge(x_updated, 8 * wv + m + 1)
                act.activation(xh[:, m, :], x[:, m, :], ACT.Copy, scale=GAIN[wv][:, m:m + 1]).then_inc(xh_ready, 1)
            return tile

        def square_root(name, src, dst):
            act.wait_ge(var_ready, ROOTS[name] + 1)
            act.activation(dst, src, ACT.Sqrt).then_inc(root_ready, 1)

        def ffn(f, xname):
            J, E = JF[f], EF[f]

            def pair(e, b, ft):
                act.wait_ge(gate_scaled, e + 1)
                act.activation(sg[:, b, :], tg[:, b, :], ACT.Silu).then_inc(silu_ready, 1)

                def after():
                    act.wait_ge(hidden_ready, e + 1)
                    act.activation(hh[:, ft, :] if isinstance(ft, int) else hh[:, bass.ds(ft, 1), :],
                                   hf[:, b, :], ACT.Copy).then_inc(hidden_hi, 1)
                return after

            def split_in_loop(i, q):
                j = J + q
                views, u = half_views(j, hi)
                act.wait_ge(raw_landed[u % RING], i * 16 + LANDED[u])
                act.wait_ge(half_done, i * 8 + (j - RING + 1))
                for src, dst in views:
                    act.activation(dst, src, ACT.Copy).then_inc(split_hi, 1)

            def run(q0, n):
                for q in range(q0, q0 + n):
                    after = pair(E + q // 2, (q // 2) % 2, q // 2) if q % 2 else None
                    split(J + q + 4)
                    if after:
                        after()

            square_root(xname, var[:, :], root[:, :])
            run(0, 4)
            with act.Fori(0, 4) as i:
                for q in range(4, 12):
                    after = pair(i * 4 + (E + q // 2), (q // 2) % 2, i * 4 + q // 2) if q % 2 else None
                    split_in_loop(i, q + 4)
                    if after:
                        after()
            run(36, 8)

        def down(f, tile, extra=None):
            J = JF[f]
            for q in range(FFN_UP, FFN_HALVES):
                if q % 4 == 3 and tile is not None:
                    tile((q - FFN_UP) // 4)
                if J + q + 4 < J0[5]:
                    split(J + q + 4)
                if extra is not None and q in extra:
                    extra[q]()

        def exp(k, scores, probs):
            for t, (a, b) in enumerate(((0, P), (P, NSEG))):
                c = 2 * (k % 2) + t
                act.wait_ge(seg_max, 2 * k + t + 1)
                act.activation(probs[:, :, a:b], scores[:, :, a:b], ACT.Exp, bias=nmax[:, c:c + 1],
                               accum_out=ssum[:, c:c + 1]).then_inc(seg_probs, 1)

        def normalize(k, probs):
            for t, (a, b) in enumerate(((0, P), (P, NSEG))):
                c = 2 * (k % 2) + t
                act.wait_ge(seg_inv, 2 * k + t + 1)
                act.activation(probs[:, :, a:b], probs[:, :, a:b], ACT.Copy,
                               scale=sinv[:, c:c + 1]).then_inc(seg_norm, 1)

        def copy_turned(s, dst):
            act.wait_ge(seg_turned, s + 1)
            act.activation(dst, ps[6 + s % 2][:, 0:NSEG], ACT.Copy).then_inc(seg_copied, 1)

        def y_high(g, dst, rows):
            act.wait_ge(seg_out, g + 1)
            act.activation(dst[rows], ps[3][rows, 0:T], ACT.Copy).then_inc(y_hi, 1)

        def tanh_half(i):
            act.wait_ge(z_ready, i + 1)
            act.activation(tg[:, i % 2, :], tu[:, i % 2, :], ACT.Tanh, scale=0.5).then_inc(tanh_ready, 1)

        def merge_high(i, dst, m):
            act.wait_ge(merged, i + 1)
            act.activation(dst[:, m, :], hf[:, m % 2, :], ACT.Copy).then_inc(merged_hi, 1)

        for j in range(4):
            split(j)
        tile = x_parts(0)
        act.wait_ge(vec_ready, 1)
        for m in range(KD):
            tile(m)
        ffn(0, "x0")
        down(0, x_parts(1))

        square_root("x1", var[:, :], root[:, :])
        tile2 = x_parts(2)
        for n in range(M1["end"]):
            if M1["gates"] <= n < M1["merge"]:
                tanh_half(n - M1["gates"])
            if M1["merge"] <= n < M1["out"]:
                merge_high(n - M1["merge"], mh1, n - M1["merge"])
            if n >= M1["out"]:
                tile2(n - M1["out"])
            split(J0[1] + n + 4)
            for s in range(NSEG1):
                if n == TURN1[s] + 1:
                    copy_turned(s, pt1[:, s % 2, :])
            for k in range(12):
                s = last_segment(k)
                if n == SCORES1[s] + 2:
                    normalize(k, probs1(k))
                if n == SCORES1[s] + 1:
                    exp(k, scores1(k), probs1(k))
                if n == TURN1[s] + OUT_LAG + 1:
                    y_high(k, y1h[:, k // 2, :], slice(HD * (k % 2), HD * (k % 2) + HD))
        act.wait_ge(half_done, J0[2])
        act.dma_start(wg2[:, :], w["gla_w_gate2_2"][0]).then_inc(small_in, 16)
        act.dma_start(pos_i[:, :], w["positions_2"].to_broadcast([P, T])).then_inc(pos_in, 16)
        ffn(1, "x2")

        def rope_sines():
            act.wait_ge(sin_arg, 1)
            act.activation(cosT[:, :], tg[:, 0, :], ACT.Sin).then_inc(sin_ready, 1)
            act.wait_ge(sin_arg, 2)
            act.activation(sinT[:, :], tg[:, 1, :], ACT.Sin).then_inc(sin_ready, 1)
        down(1, x_parts(3), {FFN_UP + 12: rope_sines})

        square_root("x3", var[:, :], root[:, :])
        square_root("y3", var[:, :], root[:, :])
        tile4 = x_parts(4)
        for n in range(M2["end"]):
            if n in OG_HALVES:
                tanh_half(16 + OG_HALVES.index(n))
            if M2["ckv"] <= n < M2["gv"]:
                i = n - M2["ckv"]
                src, dst, m, g = (ckv, ckvh, i, VEC["mla_norm_ckv_2"]) if i < 2 else (
                    cq, cqh, i - 2, VEC["mla_norm_cq_2"])
                act.wait_ge(cx_ready, i + 1)
                act.activation(dst[:, m, :], src[:, m, :], ACT.Copy,
                               scale=vec[:, g + m:g + m + 1]).then_inc(cx_hi, 1)
            if M2["gates"] <= n < M2["merge"]:
                tanh_half(20 + n - M2["gates"])
            if M2["merge"] <= n < M2["out"]:
                merge_high(KD + n - M2["merge"], mh2, n - M2["merge"])
            if n >= M2["out"]:
                tile4(n - M2["out"])
            split(J0[3] + n + 4)
            if n == Z_AT + 1:
                act.wait_ge(decay_taken, 2)
                link(act.activation(ze[:, :, :], zl[:, :, :], ACT.Abs))
                link(act.activation(ze[:, :, :], ze[:, :, :], ACT.Exp, scale=-1.0))
                act.activation(ze[:, :, :], ze[:, :, :], ACT.Ln, bias=1.0).then_inc(decay_logs, 1)
            if n == SUM_CKV_AT + 1:
                square_root("ckv", var[:, :], root[:, :])
            if n == SUM_CQ_AT + 1:
                square_root("cq", var[:, :], root[:, :])
            if n == GLA_O_AT + 1:
                square_root("gla", gss[:, 1, :], gss[:, 2, :])
            lv = n - LEVEL_AT + 2
            if 0 <= lv < 8:
                act.wait_ge(lv_diff, lv + 1)
                s = GLA_LEVELS[lv]
                dv = lvd[:, :, :].rearrange("p a (g c) -> p (a g) c", c=2 * s)
                ev = lve[:, :, :].rearrange("p a (g c) -> p (a g) c", c=2 * s)
                act.activation(ev[:, :, s:], dv[:, :, s:], ACT.Exp, scale=1.0 / 16.0).then_inc(lv_exp, 1)
                act.activation(ev[:, :, 0:s], dv[:, :, 0:s], ACT.Exp, scale=-1.0 / 16.0).then_inc(lv_exp, 1)
            if n == GLA_TURN_AT + 1:
                for h in range(4):
                    act.wait_ge(gla_y, h + 1)
                    act.activation(y2bh[:, h, :], go_y[:, h, :], ACT.Copy).then_inc(yb_hi, 1)
            for s in range(NSEG2):
                k = 12 + s
                if n == TURN2[s] + 1:
                    copy_turned(NSEG1 + s, pt2[:, s % 2, :])
                if n == SCORES2[s] + 2:
                    normalize(k, p2[:, s % 3:s % 3 + 1, :])
                if n == SCORES2[s] + 1:
                    exp(k, s2[:, s % 2:s % 2 + 1, :], p2[:, s % 3:s % 3 + 1, :])
                if n == TURN2[s] + OUT_LAG + 1:
                    y_high(k, y2ah[:, s // 2, :], slice(HD * (s % 2), HD * (s % 2) + HD))
        ffn(2, "x4")
        down(2, None)
        act.wait_ge(half_done, J0[5])
        for m in range(KD):
            act.wait_ge(x_updated, 8 * 5 + m + 1)
            act.activation(o_fm[:, m, :], x[:, m, :], ACT.Copy, scale=GAIN[5][:, m:m + 1]).then_inc(fin_ready, 1)
        square_root("x5", rcol[:, 0:2], rcol[:, 2:4])


    @block_ctx.vector
    def _(dve):
        steps = [0]

        def link(ins):
            steps[0] += 1
            ins.then_inc(dve_step, 1)
            dve.wait_ge(dve_step, steps[0])

        def split(j):
            views, u = half_views(j, lo)
            his = half_views(j, hi)[0]
            dve.wait_ge(split_hi, j + 1)
            for n, (src, dst) in enumerate(views):
                ins = dve.tensor_tensor(dst, src, his[n][1].bitcast(F32), ALU.subtract)
                if n == len(views) - 1:
                    ins.then_inc(split_lo, 1)

        def newton_root(name, v, s, tmp, dst):
            dve.wait_ge(root_ready, ROOTS[name] + 1)
            link(dve.reciprocal(s, s))
            link(dve.tensor_tensor(tmp, s, s, ALU.mult))
            link(dve.tensor_tensor(tmp, tmp, v, ALU.mult))
            link(dve.tensor_scalar(tmp, tmp, -0.5, 1.5, ALU.mult, ALU.add))
            dve.tensor_tensor(dst, tmp, s, ALU.mult).then_inc(r_ready, 1)
            dve.wait_ge(r_ready, ROOTS[name] + 1)

        def variance(dst, sums, n):
            dve.tensor_scalar(dst, sums, 1.0 / n, EPS, ALU.mult, ALU.add).then_inc(var_ready, 1)

        def norm(wv, name):
            dve.wait_ge(sums_ready, wv + 1 if wv < 4 else wv + 3)
            variance(var[:, :], ps[6][:, 0:T], D)
            newton_root(name, var[:, :], root[:, :], newton[:, :], R1[:, :] if wv == 3 else R[:, :])

        def update(wv, m, factor):
            if wv == 4:
                dve.wait_ge(residual_scaled, m + 1)
            b = ps[4 + m % 2][:, 0:T]
            if factor == 1.0:
                dve.tensor_tensor(x[:, m, :], b, x[:, m, :], ALU.add).then_inc(x_updated, 1)
            else:
                dve.scalar_tensor_tensor(out=x[:, m, :], in0=b, scalar=factor, in1=x[:, m, :],
                                         op0=ALU.mult, op1=ALU.add).then_inc(x_updated, 1)

        def x_low(wv, m):
            dve.wait_ge(xh_ready, 8 * wv + m + 1)
            dve.scalar_tensor_tensor(out=xl[:, m, :], in0=x[:, m, :], scalar=GAIN[wv][:, m:m + 1],
                                     in1=xh[:, m, :].bitcast(F32), op0=ALU.mult,
                                     op1=ALU.subtract).then_inc(xl_ready, 1)

        def ffn(f):
            J, E = JF[f], EF[f]

            def pair(e, q, done):
                b = (q // 2) % 2
                dve.wait_ge(half_done, done)
                dve.tensor_tensor(tg[:, b, :], ps[(q - 1) % 8][:, 0:T], R[:, :], ALU.mult).then_inc(gate_scaled, 1)
                dve.tensor_tensor(tu[:, b, :], ps[q % 8][:, 0:T], R[:, :], ALU.mult).then_inc(up_scaled, 1)
                dve.wait_ge(up_scaled, e + 1)
                dve.wait_ge(silu_ready, e + 1)
                dve.tensor_tensor(hf[:, b, :], sg[:, b, :], tu[:, b, :], ALU.mult).then_inc(hidden_ready, 1)

            def low(e, q, ft):
                b = (q // 2) % 2
                dve.wait_ge(hidden_ready, e + 1)
                dve.wait_ge(hidden_hi, e + 1)
                o = hl[:, ft, :] if isinstance(ft, int) else hl[:, bass.ds(ft, 1), :]
                h = hh[:, ft, :] if isinstance(ft, int) else hh[:, bass.ds(ft, 1), :]
                src = hf[:, b, :] if isinstance(ft, int) else hf[:, b:b + 1, :]
                dve.tensor_tensor(o, src, h.bitcast(F32), ALU.subtract).then_inc(hidden_lo, 1)

            def run(q0, n):
                for q in range(q0, q0 + n):
                    if q % 2:
                        pair(E + q // 2, q, J + q + 1)
                    split(J + q + 4)
                    if q % 2:
                        low(E + q // 2, q, q // 2)
            run(0, 4)
            with dve.Fori(0, 4) as i:
                for q in range(4, 12):
                    if q % 2:
                        pair(i * 4 + (E + q // 2), q, i * 8 + (J + q + 1))
                    j = J + q + 4
                    views = half_views(j, lo)[0]
                    his = half_views(j, hi)[0]
                    dve.wait_ge(split_hi, i * 8 + (j + 1))
                    for (src, dst), (_, h) in zip(views, his):
                        dve.tensor_tensor(dst, src, h.bitcast(F32), ALU.subtract).then_inc(split_lo, 1)
                    if q % 2:
                        low(i * 4 + (E + q // 2), q, i * 4 + q // 2)
            run(36, 8)

        def down(f, wv, factor, extra=None):
            J = JF[f]
            for q in range(FFN_UP, FFN_HALVES):
                m = (q - FFN_UP) // 4
                if q % 4 == 3:
                    dve.wait_ge(half_done, J + q + 1)
                    update(wv, m, factor)
                if J + q + 4 < J0[5]:
                    split(J + q + 4)
                if q % 4 == 3 and wv < 5:
                    x_low(wv, m)
                if extra is not None and q in extra:
                    extra[q]()

        def rms_column(i, src_bank, at):
            dve.wait_ge(rcol_turned, i + 1)
            dve.tensor_copy(rcol[:, at:at + TT], src_bank[:, 0:TT]).then_inc(rcol_ready, 1)
            dve.wait_ge(rcol_ready, i + 1)

        def gate_half(i, n):
            if i >= 2:
                dve.wait_ge(sig_ready, i - 1)
            dve.tensor_tensor(tu[:, i % 2, :], ps[n % 3][:, 0:T], R[:, :], ALU.mult).then_inc(z_ready, 1)

        def merge(i, m, n, gates):
            a = dve.tensor_tensor(tg[:, m % 2, :], ps[n % 3][:, 0:T], gates[:, m, :], ALU.mult)
            a.then_inc(merge_ab, 1)
            dve.tensor_tensor(tu[:, m % 2, :], ps[n % 3][:, T:2 * T], gates[:, KD + m, :],
                              ALU.mult).then_inc(merge_ab, 1)

        def merge_low(i, m, dst_hi, dst_lo):
            dve.wait_ge(merged_hi, i + 1)
            dve.tensor_tensor(dst_lo[:, m, :], hf[:, m % 2, :], dst_hi[:, m, :].bitcast(F32),
                              ALU.subtract).then_inc(merged_lo, 1)

        def bias(s, g, slope, dst, waits):
            dve.wait_ge(seg_scores, s + 1)
            if waits:
                dve.wait_ge(seg_probs, waits)
            dve.scalar_tensor_tensor(out=dst, in0=dist[:, g, :], scalar=-slope,
                                     in1=ps[4 + s % 2][:, 0:NSEG], op0=ALU.mult,
                                     op1=ALU.add).then_inc(seg_biased, 1)

        def maxima(k, s, scores):
            dve.wait_ge(seg_biased, s + 1)
            for t, (a, b) in enumerate(((0, P), (P, NSEG))):
                c = 2 * (k % 2) + t
                dve.tensor_reduce(nmax[:, c:c + 1], scores[:, :, a:b], AX.XY, ALU.max,
                                  negate=True).then_inc(seg_max, 1)

        def inverse(k):
            for t in range(2):
                c = 2 * (k % 2) + t
                dve.wait_ge(seg_probs, 2 * k + t + 1)
                dve.reciprocal(sinv[:, c:c + 1], ssum[:, c:c + 1]).then_inc(seg_inv, 1)

        def y_low(k, dst_hi, dst_lo, rows):
            dve.wait_ge(seg_out, k + 1)
            dve.wait_ge(y_hi, k + 1)
            dve.tensor_tensor(dst_lo[rows], ps[3][rows, 0:T], dst_hi[rows].bitcast(F32),
                              ALU.subtract).then_inc(y_lo, 1)

        for j in range(4):
            split(j)
        dve.wait_ge(vec_turned, 1)
        dve.tensor_copy(vec[:, :], ps[0][:, 0:NVEC]).then_inc(vec_ready, 1)
        dve.wait_ge(vec_ready, 1)
        vf, vl = VEC["norm_final"], VEC["ln_mix_2"]
        dve.tensor_tensor(vec2[:, 0:8], vec[:, vf:vf + 8], vec[:, vl:vl + 8], ALU.mult).then_inc(vec_ready, 1)
        dve.tensor_tensor(vec2[:, 8:16], vec[:, vf:vf + 8], vec[:, vf:vf + 8], ALU.mult).then_inc(vec_ready, 1)
        for m in range(KD):
            dve.wait_ge(x_turned, m + 1)
            dve.tensor_copy(x[:, m, :], ps[4 + m // 2][:, (m % 2) * T:(m % 2 + 1) * T]).then_inc(x_updated, 1)
        for m in range(KD):
            x_low(0, m)
        norm(0, "x0")
        ffn(0)
        down(0, 1, 0.5)

        norm(1, "x1")
        dve.wait_ge(dist_in, 32)
        for n in range(M1["end"]):
            if n < M1["out"] and not (n - 1 in M1_TOKEN or n in M1_TOKEN):
                dve.wait_ge(half_done, J0[1] + n + 1)
            bank = ps[n % 3][:, 0:T]
            if n < M1["ka"]:
                dve.scalar_tensor_tensor(out=qa[:, n, :], in0=bank, scalar=HD ** -0.5, in1=R[:, :],
                                         op0=ALU.mult, op1=ALU.mult).then_inc(half_taken, 1)
            elif n < M1["va"]:
                dve.tensor_tensor(ka[:, n - M1["ka"], :], bank, R[:, :], ALU.mult).then_inc(half_taken, 1)
            elif n - 1 in M1_TOKEN:
                dve.wait_ge(half_done, J0[1] + n + 1)
                dst, c = (va, n - 1 - M1["va"]) if n < M1["qb"] else (vb, n - 1 - M1["vb"])
                for t in range(TT):
                    dve.tensor_scalar(dst[:, t, c * P:c * P + 256], ps[(n - 1 + t) % 3][:, 0:T],
                                      rcol[:, t:t + 1], None, ALU.mult).then_inc(half_taken, 1)
            elif n in M1_TOKEN:
                pass
            elif n < M1["kb"]:
                dve.scalar_tensor_tensor(out=qb[:, n - M1["qb"], :], in0=bank, scalar=HD ** -0.5, in1=R[:, :],
                                         op0=ALU.mult, op1=ALU.mult).then_inc(half_taken, 1)
            elif n < M1["vb"]:
                dve.tensor_tensor(kb[:, n - M1["kb"], :], bank, R[:, :], ALU.mult).then_inc(half_taken, 1)
            elif n < M1["merge"]:
                gate_half(n - M1["gates"], n)
            elif n < M1["out"]:
                m = n - M1["merge"]
                if m == 0:
                    dve.wait_ge(sig_ready, 16)
                merge(m, m, n, gates1)
            else:
                m = n - M1["out"]
                dve.wait_ge(half_done, J0[1] + n + 1)
                update(2, m, 1.0)
            split(J0[1] + n + 4)
            if M1["merge"] <= n < M1["out"]:
                merge_low(n - M1["merge"], n - M1["merge"], mh1, ml1)
            if n >= M1["out"]:
                x_low(2, n - M1["out"])
            if n == 5:
                rms_column(0, ps[7], 0)
            for k in range(12):
                s = last_segment(k)
                if n == SCORES1[s] + 2:
                    inverse(k)
            for s in range(NSEG1):
                if n == SCORES1[s] + 1:
                    if s < N_DSA:
                        k, g = divmod(s, 3)
                        bias(s, g, alibi(4 * g + k, 12), s1[:, g, :], 2 * k)
                    else:
                        k, g = 4 + s - N_DSA, 2
                        bias(s, 3, alibi(s - N_DSA, HEADS), s1[:, s % 3, :], 8 if k < 7 else 2 * (k - 2))
                    if g == 2:
                        maxima(k, s, scores1(k))
            for k in range(12):
                if n == TURN1[last_segment(k)] + OUT_LAG + 1:
                    y_low(k, y1h[:, k // 2, :], y1l[:, k // 2, :], slice(HD * (k % 2), HD * (k % 2) + HD))
        norm(2, "x2")
        ffn(1)

        def rope_angles():
            dve.wait_ge(pos_in, 16)
            a, n_, b = tg[:, 0, :], tg[:, 1, :], tu[:, 0, :]
            link(dve.tensor_copy(a, pos_i[:, :]))
            link(dve.tensor_scalar(a, a, cst[:, C_INV:C_INV + 1], None, ALU.mult))
            two_pi = 2 * math.pi
            c1 = 6.28125
            c2 = float(np.floor((two_pi - c1) * 2.0 ** 20) / 2.0 ** 20)
            c3 = float(np.float32(two_pi - c1 - c2))
            magic = 1.5 * 2.0 ** 23
            for turns in (4096.0, 1.0):
                link(dve.tensor_scalar(n_, a, 1.0 / (two_pi * turns), None, ALU.mult))
                link(dve.tensor_scalar(n_, n_, magic, None, ALU.add))
                link(dve.tensor_scalar(n_, n_, -magic, None, ALU.add))
                for c in (c1, c2, c3):
                    link(dve.scalar_tensor_tensor(out=a, in0=n_, scalar=-c * turns, in1=a,
                                                  op0=ALU.mult, op1=ALU.add))
            lim = 3.1415925
            link(dve.tensor_scalar(n_, a, -lim, lim, ALU.max, ALU.min))
            link(dve.tensor_scalar(b, n_, -1.0, None, ALU.mult))
            link(dve.tensor_tensor(b, n_, b, ALU.max))
            dve.tensor_scalar(a, b, -1.0, math.pi / 2, ALU.mult, ALU.add).then_inc(sin_arg, 2)

        def rope_tables():
            dve.wait_ge(sin_ready, 2)
            link(dve.tensor_scalar(sinT[:, :], sinT[:, :], cst[:, C_SIGN:C_SIGN + 1], None, ALU.mult))
        down(1, 3, 0.5, {FFN_UP + 8: rope_angles, FFN_UP + 16: rope_tables})

        norm(3, "x3")
        dve.wait_ge(sums_ready, 4)
        link(dve.tensor_tensor(var[:, :], ps[6][:, T:2 * T], R1[:, :], ALU.mult))
        link(dve.tensor_tensor(var[:, :], var[:, :], R1[:, :], ALU.mult))
        variance(var[:, :], var[:, :], D)
        newton_root("y3", var[:, :], root[:, :], newton[:, :], R[:, :])
        link(dve.tensor_tensor(R[:, :], R[:, :], R1[:, :], ALU.mult))
        link(dve.tensor_tensor(rope_k[:, 0, :], cosT[:, :], R[:, :], ALU.mult))
        link(dve.tensor_tensor(rope_k[:, 1, :], sinT[:, :], R[:, :], ALU.mult))
        for n in range(M2["end"]):
            if n < M2["out"] and not (n - 1 in M2_TOKEN or n in M2_TOKEN):
                dve.wait_ge(half_done, J0[3] + n + 1)
            bank = ps[n % 3][:, 0:T]
            rot = acc[:, 1, :]
            if n == M2["lr"]:
                dve.tensor_tensor(lr[:, :], bank, R[:, :], ALU.mult).then_inc(half_taken, 1)
            elif n in OG_HALVES:
                gate_half(16 + OG_HALVES.index(n), n)
            elif n < M2["gk"]:
                dve.scalar_tensor_tensor(out=gq[:, n - M2["gq"], :], in0=bank, scalar=HD ** -0.5, in1=R[:, :],
                                         op0=ALU.mult, op1=ALU.mult).then_inc(half_taken, 1)
            elif n < M2["og2"]:
                dve.tensor_tensor(gk[:, n - M2["gk"], :], bank, R[:, :], ALU.mult).then_inc(half_taken, 1)
            elif n == M2["kr"]:
                dve.tensor_tensor(kr[:, 0, :], bank, rope_k[:, 0, :], ALU.mult).then_inc(half_taken, 1)
            elif n == M2["kr"] + 1:
                dve.tensor_tensor(rot, bank, rope_k[:, 1, :], ALU.mult).then_inc(half_taken, 1)
                dve.wait_ge(*taken(3, n))
                link(dve.tensor_tensor(kr[:, 0, :], kr[:, 0, :], rot, ALU.add))
            elif n < M2["gv"]:
                i = n - M2["ckv"]
                dst, m = (ckv, i) if i < 2 else (cq, i - 2)
                dve.tensor_tensor(dst[:, m, :], bank, R[:, :], ALU.mult).then_inc(cx_ready, 1)
            elif n - 1 in M2_TOKEN:
                dve.wait_ge(half_done, J0[3] + n + 1)
                dst, c, r = (gv, n - 1 - M2["gv"], 0) if n < M2["uq"] else (mv, n - 1 - M2["uv"], 2)
                for t in range(TT):
                    dve.tensor_scalar(dst[:, t, c * P:c * P + 256], ps[(n - 1 + t) % 3][:, 0:T],
                                      rcol[:, r + t:r + t + 1], None, ALU.mult).then_inc(half_taken, 1)
            elif n in M2_TOKEN:
                pass
            elif n < M2["uqr"]:
                dve.scalar_tensor_tensor(out=qn[:, n - M2["uq"], :], in0=bank, scalar=MLA_QK ** -0.5,
                                         in1=Rq[:, :], op0=ALU.mult, op1=ALU.mult).then_inc(half_taken, 1)
            elif n < M2["uqr"] + 2:
                dve.tensor_tensor(qr[:, n - M2["uqr"], :], bank, rope_q[:, 0, :], ALU.mult).then_inc(half_taken, 1)
            elif n < M2["ukv"]:
                c = n - M2["uqr"] - 2
                dve.tensor_tensor(rot, bank, rope_q[:, 1, :], ALU.mult).then_inc(half_taken, 1)
                dve.wait_ge(*taken(3, n))
                link(dve.tensor_tensor(qr[:, c, :], qr[:, c, :], rot, ALU.add))
            elif n < M2["uv"]:
                dve.tensor_tensor(kn[:, n - M2["ukv"], :], bank, Rkv[:, :], ALU.mult).then_inc(half_taken, 1)
            elif n < M2["merge"]:
                gate_half(20 + n - M2["gates"], n)
            elif n < M2["out"]:
                m = n - M2["merge"]
                if m == 0:
                    dve.wait_ge(sig_ready, 36)
                merge(KD + m, m, n, gates2)
            else:
                m = n - M2["out"]
                dve.wait_ge(half_done, J0[3] + n + 1)
                update(4, m, 1.0)
            split(J0[3] + n + 4)
            if M2["ckv"] <= n < M2["gv"]:
                i = n - M2["ckv"]
                src, dh, dl, m, g = (ckv, ckvh, ckvl, i, VEC["mla_norm_ckv_2"]) if i < 2 else (
                    cq, cqh, cql, i - 2, VEC["mla_norm_cq_2"])
                dve.wait_ge(cx_ready, i + 1)
                dve.wait_ge(cx_hi, i + 1)
                dve.scalar_tensor_tensor(out=dl[:, m, :], in0=src[:, m, :], scalar=vec[:, g + m:g + m + 1],
                                         in1=dh[:, m, :].bitcast(F32), op0=ALU.mult,
                                         op1=ALU.subtract).then_inc(cx_lo, 1)
            if M2["merge"] <= n < M2["out"]:
                merge_low(KD + n - M2["merge"], n - M2["merge"], mh2, ml2)
            if n >= M2["out"]:
                x_low(4, n - M2["out"])
            if n == 5:
                rms_column(1, ps[7], 0)
            if n == Z_AT + 1:
                dve.wait_ge(decay_raw, 1)
                for c in range(2):
                    v = VEC["gla_b_gate_2"] + c
                    dve.tensor_scalar(zl[:, c, :], ps[4][:, c * T:(c + 1) * T], vec[:, v:v + 1], None,
                                      ALU.add).then_inc(decay_taken, 1)
            if n == Z_AT + 2:
                dve.wait_ge(decay_logs, 1)
                link(dve.scalar_tensor_tensor(out=zl[:, :, :], in0=zl[:, :, :], scalar=0.0, in1=ze[:, :, :],
                                              op0=ALU.min, op1=ALU.subtract))
                flat = zl[:, :, :].rearrange("p a c -> p (a c)")
                for dst, c in ((run_chunk, C_SEG), (run_all, C_SEG + 2 * T)):
                    link(dve.tensor_tensor_scan(dst[:, :, :].rearrange("p a c -> p (a c)"), cst[:, c:c + 2 * T],
                                                flat, 0.0, ALU.mult, ALU.add))
            lv = n - LEVEL_AT + 1
            if 0 <= lv < 8:
                s = GLA_LEVELS[lv]
                dve.wait_ge(lv_exp, 2 * (lv + 1))
                dve.wait_ge(lv_zero, lv + 1)

                def at(v, a, b):
                    return v.rearrange("p a (g c) -> p (a g) c", c=2 * s)[:, :, a:b]
                dve.tensor_tensor(at(lvq[:, lv % 2, :, :], s, 2 * s), at(gq[:, :, :], s, 2 * s),
                                  at(lve[:, :, :], s, 2 * s), ALU.mult).then_inc(lv_ready, 1)
                dve.tensor_tensor(at(lvk[:, lv % 2, :, :], 0, s), at(gk[:, :, :], 0, s),
                                  at(lve[:, :, :], 0, s), ALU.mult).then_inc(lv_ready, 1)
            if 0 <= lv + 1 < 8:
                s = GLA_LEVELS[lv + 1]
                src = (run_all if s >= GLA_CHUNK else run_chunk)[:, :, :].rearrange("p a (g c) -> p (a g) c", c=2 * s)
                g = 2 * T // (2 * s)
                dve.tensor_tensor(lvd[:, :, :].rearrange("p a (g c) -> p (a g) c", c=2 * s), src,
                                  src[:, :, s - 1:s].to_broadcast([P, g, 2 * s]), ALU.subtract).then_inc(lv_diff, 1)
            lv = n - LEVEL_AT - 1
            if 0 <= lv < 9:
                dve.wait_ge(lv_done, lv + 1)
                if lv:
                    dve.wait_ge(lv_taken, 2 * lv)
                b = 4 + 2 * (lv % 2)
                for e in range(2):
                    if lv == 0:
                        ins = dve.tensor_copy(at3[:, 2, e::2, :], ps[b + e][:, 0:T].rearrange("p (h c) -> p h c", c=P))
                    else:
                        dst = at3[:, 0:2, e::2, :]
                        src = ps[b + e][:, :].rearrange("p (t h c) -> p t h c", h=2, c=P)
                        if lv == 1:
                            ins = dve.tensor_copy(dst, src)
                        else:
                            m_ = masks[:, lv - 2:lv - 1, :].unsqueeze(2).to_broadcast([P, 2, 2, P])
                            ins = dve.copy_predicated(dst, m_, src)
                    ins.then_inc(lv_taken, 1)
            if n == SUM_CKV_AT + 1:
                dve.wait_ge(sums_ready, 5)
                variance(var[:, :], ps[3][:, 0:T], CKV)
                newton_root("ckv", var[:, :], root[:, :], newton[:, :], Rkv[:, :])
            if n == SUM_CQ_AT + 1:
                dve.wait_ge(sums_ready, 6)
                variance(var[:, :], ps[3][:, T:2 * T], CQ)
                newton_root("cq", var[:, :], root[:, :], newton[:, :], Rq[:, :])
                for c, tab in enumerate((cosT, sinT)):
                    link(dve.scalar_tensor_tensor(out=rope_q[:, c, :], in0=tab[:, :], scalar=MLA_QK ** -0.5,
                                                  in1=Rq[:, :], op0=ALU.mult, op1=ALU.mult))
            if n == COL_CKV_AT + 1:
                rms_column(2, ps[3], 2)
            if n == GLA_O_AT + 1:
                dve.wait_ge(gla_out, 1)
                for t in range(TT):
                    link(dve.tensor_copy(go[:, t, :], ps[4 + t][:, :]))
                link(dve.tensor_tensor(osq[:, :, :], go[:, :, :], go[:, :, :], ALU.mult))
                link(dve.tensor_reduce(gss[:, 0, :], osq[:, :, :].rearrange("p t (h c) -> p (t h) c", c=P),
                                       AX.X, ALU.add))
                variance(gss[:, 1, :], gss[:, 0, :], P)
                newton_root("gla", gss[:, 1, :], gss[:, 2, :], gss[:, 3, :], gss[:, 4, :])
                gh = go[:, :, :].rearrange("p t (h c) -> p (t h) c", c=P)
                dve.tensor_tensor(gh, gh, gss[:, 4, :].unsqueeze(2).to_broadcast([P, 8, P]),
                                  ALU.mult).then_inc(gla_scaled, 1)
            if n == GLA_TURN_AT + 1:
                dve.wait_ge(gla_turned, 1)
                dve.wait_ge(sig_ready, 20)
                v = VEC["gla_norm_2"]
                for h in range(4):
                    dve.scalar_tensor_tensor(out=go_y[:, h, :], in0=ps[4 + h // 2][:, (h % 2) * T:(h % 2 + 1) * T],
                                             scalar=vec[:, v:v + 1], in1=og[:, h, :], op0=ALU.mult,
                                             op1=ALU.mult).then_inc(gla_y, 1)
                for h in range(4):
                    dve.wait_ge(gla_y, h + 1)
                    dve.wait_ge(yb_hi, h + 1)
                    dve.tensor_tensor(y2bl[:, h, :], go_y[:, h, :], y2bh[:, h, :].bitcast(F32),
                                      ALU.subtract).then_inc(yb_lo, 1)
            for s in range(NSEG2):
                k = 12 + s
                if n == SCORES2[s] + 2:
                    inverse(k)
            for s in range(NSEG2):
                k = 12 + s
                if n == SCORES2[s] + 1:
                    bias(NSEG1 + s, 4, 1.0, s2[:, s % 2, :], 2 * (k - 1) if s >= 2 else 0)
                    maxima(k, NSEG1 + s, s2[:, s % 2:s % 2 + 1, :])
                if n == TURN2[s] + OUT_LAG + 1:
                    y_low(k, y2ah[:, s // 2, :], y2al[:, s // 2, :], slice(HD * (s % 2), HD * (s % 2) + HD))
        norm(4, "x4")
        ffn(2)
        down(2, 5, 1.0)
        dve.wait_ge(sums_ready, 8)
        variance(rcol[:, 0:2], ps[6][:, 0:2], D)
        newton_root("x5", rcol[:, 0:2], rcol[:, 2:4], gss[:, 0, 0:2], gss[:, 1, 0:2])
        for t in range(TT):
            for c in range(4):
                dve.wait_ge(fin_turned, 4 * t + c + 1)
                dve.tensor_scalar(o_tm[:, t, c * 256:(c + 1) * 256], ps[FIN_BANK[4 * t + c]][:, 0:256],
                                  gss[:, 1, t:t + 1], None, ALU.mult).then_inc(fin_scaled, 1)

    @block_ctx.gpsimd
    def _(pool):
        steps = [0]

        def link(ins):
            steps[0] += 1
            ins.then_inc(pool_step, 1)
            pool.wait_ge(pool_step, steps[0])

        def squares(wv, m):
            pool.wait_ge(x_updated, 8 * wv + m + 1)
            two = wv == 3
            first = m == 0
            if 8 * wv + m:
                pool.wait_ge(acc_ready, 8 * wv + m)
            to = acc[:, 0, :] if first else sq[:, 0, :]
            ins = pool.tensor_tensor(to, x[:, m, :], x[:, m, :], ALU.mult)
            if first and not two:
                ins.then_inc(acc_ready, 1)
                return
            link(ins)
            if two:
                ins = pool.tensor_scalar(acc[:, 1, :] if first else sq[:, 1, :], to, vec2[:, 8 + m:9 + m], None,
                                         ALU.mult)
                if first:
                    ins.then_inc(acc_ready, 1)
                    return
                link(ins)
                link(pool.tensor_tensor(acc[:, 0, :], acc[:, 0, :], sq[:, 0, :], ALU.add))
                pool.tensor_tensor(acc[:, 1, :], acc[:, 1, :], sq[:, 1, :], ALU.add).then_inc(acc_ready, 1)
            else:
                pool.tensor_tensor(acc[:, 0, :], acc[:, 0, :], sq[:, 0, :], ALU.add).then_inc(acc_ready, 1)

        def sigmoid(i, dst):
            pool.wait_ge(tanh_ready, i + 1)
            pool.tensor_scalar(dst, tg[:, i % 2, :], 0.5, 0.5, ALU.mult, ALU.add).then_inc(sig_ready, 1)

        def add_parts(i):
            pool.wait_ge(merge_ab, 2 * (i + 1))
            pool.tensor_tensor(hf[:, i % 2, :], tg[:, i % 2, :], tu[:, i % 2, :], ALU.add).then_inc(merged, 1)

        for wv in (0, 1):
            for m in range(KD):
                squares(wv, m)
        for i in range(16):
            sigmoid(i, gates1[:, i, :])
        for m in range(KD):
            add_parts(m)
        for wv in (2, 3):
            for m in range(KD):
                squares(wv, m)

        def og_half(c):
            i = 16 + c
            pool.wait_ge(tanh_ready, i + 1)
            link(pool.tensor_scalar(tg[:, i % 2, :], tg[:, i % 2, :], 0.5, 0.5, ALU.mult, ALU.add))
            pool.tensor_tensor(og[:, c, :], tu[:, i % 2, :], tg[:, i % 2, :], ALU.mult).then_inc(sig_ready, 1)

        def level_zero(lv):
            if lv >= 2:
                pool.wait_ge(lv_done, lv - 1)
            link(pool.memset(lvq[:, lv % 2, :, :], 0.0))
            pool.memset(lvk[:, lv % 2, :, :], 0.0).then_inc(lv_zero, 1)

        def cx_squares(i):
            pool.wait_ge(cx_ready, i + 1)
            c, first = (0, i == 0) if i < 2 else (1, i == 2)
            src = ckv[:, i, :] if i < 2 else cq[:, i - 2, :]
            ins = pool.tensor_tensor(acc[:, c, :] if first else sq[:, 0, :], src, src, ALU.mult)
            if first:
                ins.then_inc(cx_acc, 1)
            else:
                link(ins)
                pool.wait_ge(cx_acc, i)
                pool.tensor_tensor(acc[:, c, :], acc[:, c, :], sq[:, 0, :], ALU.add).then_inc(cx_acc, 1)
        og_half(0)
        og_half(1)
        level_zero(0)
        level_zero(1)
        og_half(2)
        og_half(3)
        level_zero(2)
        for i in range(5):
            level_zero(3 + i)
            cx_squares(i)
        pool.wait_ge(xh_ready, 32)
        pool.wait_ge(xl_ready, 32)
        pool.wait_ge(r_ready, ROOTS["x3"] + 1)
        v = VEC["norm_final"]
        for m in range(KD):
            link(pool.tensor_scalar(x[:, m, :], x[:, m, :], vec[:, v + m:v + m + 1], None, ALU.mult))
            pool.tensor_tensor(x[:, m, :], x[:, m, :], R1[:, :], ALU.mult).then_inc(residual_scaled, 1)
        for i in range(16):
            sigmoid(20 + i, gates2[:, i, :])
        for m in range(KD):
            add_parts(KD + m)
        for wv in (4, 5):
            for m in range(KD):
                squares(wv, m)

    @block_ctx.tensor
    def _(pe):
        def feature_half(j, bank, k0, kt, xs, start=True, stop=True, each=None, at=0):
            for k in range(kt):
                if each is not None:
                    each(k)
                a = (w_part(hi, j, k0 + k), w_part(lo, j, k0 + k))
                b = (xs[0][:, k, :], xs[1][:, k, :])
                pe.matmul(bank[:, at:at + T], a[0], b[0], start=start and k == 0, stop=False)
                pe.matmul(bank[:, at:at + T], a[0], b[1], start=False, stop=False)
                ins = pe.matmul(bank[:, at:at + T], a[1], b[0], start=False, stop=stop and k == kt - 1)
            return ins

        def sums(wv):
            pe.wait_ge(acc_ready, 8 * (wv + 1))
            ins = pe.matmul(ps[6][:, 0:T], ones, acc[:, 0, :], start=True, stop=True)
            if wv == 3:
                ins = pe.matmul(ps[6][:, T:2 * T], ones, acc[:, 1, :], start=True, stop=True)
            ins.then_inc(sums_ready, 1)

        def column(src, bank, root_name):
            pe.wait_ge(r_ready, ROOTS[root_name] + 1)
            for t in range(TT):
                ins = pe.matmul(bank[:, t:t + 1], src[0:1, t * P:(t + 1) * P], ones[0:1, 0:1],
                                start=True, stop=True)
            ins.then_inc(rcol_turned, 1)

        def x_tiles(wv):
            return lambda k: pe.wait_ge(xl_ready, 8 * wv + k + 1)

        def ffn(f, wv):
            J, E = JF[f], EF[f]

            def up_half(q, ready, free=None, each=None):
                pe.wait_ge(split_lo, ready)
                if free is not None:
                    pe.wait_ge(up_scaled, free)
                feature_half(J + q, ps[q % 8], 0, KD, (xh, xl), each=each).then_inc(half_done, 1)

            for q in range(4):
                up_half(q, J + q + 1, each=x_tiles(wv) if q == 0 else None)
                if q == 0:
                    sums(wv)
            pe.wait_ge(x_updated, 8 * (wv + 1))
            pe.wait_ge(r_ready, ROOTS[f"x{wv}"] + 1)
            for q in range(4, 12):
                up_half(q, J + q + 1, free=E + q // 2 - 3 if q >= 8 else None)
            with pe.Fori(0, 4) as i:
                for q in range(12, 20):
                    up_half(q, i * 8 + (J + q + 1), free=i * 4 + (E + q // 2 - 3))
            pe.wait_ge(up_scaled, E + NF - 2)
            with pe.Fori(0, 4) as i:
                for q in range(8):
                    k0, k1 = DOWN_K[q % 4]
                    m = q // 4
                    j = J + FFN_UP + q
                    pe.wait_ge(split_lo, i * 8 + (j + 1))
                    pe.wait_ge(hidden_lo, E + k1)
                    if q % 4 == 0:
                        pe.wait_ge(x_updated, i * 2 + (8 * (wv + 1) + m - 1))
                    feature_half(j, ps[4 + m], 0, k1 - k0, (hh[:, k0:k1, :], hl[:, k0:k1, :]),
                                 start=q % 4 == 0, stop=q % 4 == 3).then_inc(half_done, 1)

        def scores(s, q, k, rope=None):
            if s >= 2:
                pe.wait_ge(seg_biased, s - 1)
            b = ps[4 + s % 2]
            for a, c0, w_ in ((0, 0, P), (P, P, 2 * P)):
                ins = pe.matmul(b[:, c0:c0 + w_], q[:, a:a + P], k[:, 0:w_], start=True, stop=rope is None)
                if rope is not None:
                    ins = pe.matmul(b[:, c0:c0 + w_], rope[0][:, a:a + P], rope[1][:, 0:w_],
                                    start=False, stop=True)
            ins.then_inc(seg_scores, 1)

        def turn(s, k, probs):
            pe.wait_ge(seg_norm, 2 * (k + 1))
            if s >= 2:
                pe.wait_ge(seg_copied, s - 1)
            for c in range(3):
                ins = pe.transpose(ps[6 + s % 2][:, c * P:(c + 1) * P], probs[:, c * P:(c + 1) * P], ident)
            ins.then_inc(seg_turned, 1)

        def weighted(s, k, first, last, v, pt):
            pe.wait_ge(seg_copied, s + 1)
            if first and k >= 2:
                pe.wait_ge(y_lo, k - 1)
            rows = slice(HD * (k % 2), HD * (k % 2) + HD)
            pe.matmul(ps[3][rows, 0:T], v[0], pt[:, 0:T], start=first, stop=False)
            ins = pe.matmul(ps[3][rows, P:T], v[1], pt[:, T:T + P], start=False, stop=last)
            if last:
                ins.then_inc(seg_out, 1)

        def mixing_half(part, n, j):
            pe.wait_ge(split_lo, j + 1)
            if n >= 3:
                pe.wait_ge(*taken(part, n - 3))

        def token_pair(n, j, kt, xs):
            for t in range(TT):
                bank = ps[(n - 1 + t) % 3][:, 0:T].rearrange("p (a c) -> p a c", c=P)
                for k in range(kt):
                    a = (xs[0][:, k, t * P:(t + 1) * P], xs[1][:, k, t * P:(t + 1) * P])
                    b = (w_pair(hi, j - 1, k), w_pair(lo, j - 1, k))
                    pe.matmul(bank, a[0], b[0], start=k == 0, stop=False)
                    pe.matmul(bank, a[0], b[1], start=False, stop=False)
                    ins = pe.matmul(bank, a[1], b[0], start=False, stop=k == kt - 1)
            ins.then_inc(half_done, 2)

        def head_rows(h):
            return slice(HD * (h % 2), HD * (h % 2) + HD)

        pe.wait_ge(const_in, 16)
        pe.wait_ge(vec_in, 16 * len(VEC))
        pe.transpose(ps[0][:, 0:NVEC], vrow[:, :], ident[0:NVEC, 0:NVEC]).then_inc(vec_turned, 1)
        pe.wait_ge(x_landed, 16)
        for m in range(KD):
            for t in range(TT):
                a = (m % 2) * T + t * P
                ins = pe.transpose(ps[4 + m // 2][:, a:a + P], x_in[:, t, m * P:(m + 1) * P], ident)
            if m % 2:
                ins.then_inc(x_turned, 2)
        pe.wait_ge(vec_ready, 1)
        ffn(0, 0)

        for n in range(M1["end"]):
            j = J0[1] + n
            if n in M1_TOKEN:
                mixing_half(1, n, j)
            elif n - 1 in M1_TOKEN:
                mixing_half(1, n, j)
                token_pair(n, j, KD, (xh, xl))
            elif n < M1["merge"]:
                mixing_half(1, n, j)
                feature_half(j, ps[n % 3], 0, KD, (xh, xl), each=x_tiles(1) if n == 0 else None
                             ).then_inc(half_done, 1)
            elif n < M1["out"]:
                mixing_half(1, n, j)
                if n == M1["merge"]:
                    pe.wait_ge(y_lo, 12)
                feature_half(j, ps[n % 3], 0, 2, (y1h[:, 0:2, :], y1l[:, 0:2, :]))
                feature_half(j, ps[n % 3], 2, 4, (y1h[:, 2:6, :], y1l[:, 2:6, :]), at=T).then_inc(half_done, 1)
            else:
                m = n - M1["out"]
                pe.wait_ge(split_lo, j + 1)
                if m >= 2:
                    pe.wait_ge(x_updated, 8 * 2 + m - 1)
                feature_half(j, ps[4 + m % 2], 0, KD, (mh1, ml1),
                             each=(lambda k: pe.wait_ge(merged_lo, k + 1)) if m == 0 else None
                             ).then_inc(half_done, 1)
            if n == 0:
                sums(1)
            if n == 4:
                column(R, ps[7], "x1")
            for s in range(NSEG1):
                k = s // 3 if s < N_DSA else 4 + s - N_DSA
                head = 4 * (s % 3) + k if s < N_DSA else s - N_DSA
                if n == TURN1[s] + OUT_LAG:
                    pe.wait_ge(*taken(1, M1["qb"] - 1 if s < N_DSA else M1["gates"] - 1))
                    v = va if s < N_DSA else vb
                    weighted(s, k, s >= N_DSA or s % 3 == 0, s >= N_DSA or s % 3 == 2,
                             [v[:, t, head * HD:(head + 1) * HD] for t in range(TT)], pt1[:, s % 2, :])
            for s in range(NSEG1):
                k = s // 3 if s < N_DSA else 4 + s - N_DSA
                head = 4 * (s % 3) + k if s < N_DSA else s - N_DSA
                if n == TURN1[s]:
                    if s < 2:
                        pe.wait_ge(rcol_ready, 1)
                    turn(s, k, probs1_of(s))
                if n == SCORES1[s]:
                    q, kk = (qa, ka) if s < N_DSA else (qb, kb)
                    pe.wait_ge(*taken(1, M1["va"] - 1 if s < N_DSA else M1["kb"] + head // 2))
                    scores(s, q[head_rows(head), head // 2, :], kk[head_rows(head), head // 2, :])
        ffn(1, 2)

        for n in range(M2["end"]):
            j = J0[3] + n
            if n in M2_TOKEN:
                mixing_half(3, n, j)
            elif n - 1 in M2_TOKEN:
                mixing_half(3, n, j)
                token_pair(n, j, KD if n < M2["uq"] else CKV // P, (xh, xl) if n < M2["uq"] else (ckvh, ckvl))
            elif M2["uq"] <= n < M2["ukv"]:
                mixing_half(3, n, j)
                pe.wait_ge(cx_lo, 5)
                feature_half(j, ps[n % 3], 0, CQ // P, (cqh, cql)).then_inc(half_done, 1)
            elif M2["ukv"] <= n < M2["uv"]:
                mixing_half(3, n, j)
                feature_half(j, ps[n % 3], 0, CKV // P, (ckvh, ckvl)).then_inc(half_done, 1)
            elif n < M2["merge"]:
                mixing_half(3, n, j)
                feature_half(j, ps[n % 3], 0, KD, (xh, xl), each=x_tiles(3) if n == 0 else None
                             ).then_inc(half_done, 1)
            elif n < M2["out"]:
                mixing_half(3, n, j)
                if n == M2["merge"]:
                    pe.wait_ge(y_lo, 20)
                    pe.wait_ge(yb_lo, 4)
                feature_half(j, ps[n % 3], 0, 4, (y2ah, y2al))
                feature_half(j, ps[n % 3], 4, 4, (y2bh, y2bl), at=T).then_inc(half_done, 1)
            else:
                m = n - M2["out"]
                pe.wait_ge(split_lo, j + 1)
                if m >= 2:
                    pe.wait_ge(x_updated, 8 * 4 + m - 1)
                feature_half(j, ps[4 + m % 2], 0, KD, (mh2, ml2),
                             each=(lambda k: pe.wait_ge(merged_lo, KD + k + 1)) if m == 0 else None
                             ).then_inc(half_done, 1)
            if n == 0:
                sums(3)
            if n == 4:
                column(R, ps[7], "y3")
            if n == Z_AT:
                pe.wait_ge(*taken(3, M2["lr"]))
                pe.wait_ge(small_in, 16)
                for c in range(2):
                    ins = pe.matmul(ps[4][:, c * T:(c + 1) * T], wg2[:, c * P:(c + 1) * P], lr[0:16, :],
                                    start=True, stop=True)
                ins.then_inc(decay_raw, 1)
            lv = n - LEVEL_AT
            if 0 <= lv < 9:
                b = 4 + 2 * (lv % 2)
                if lv >= 2:
                    pe.wait_ge(lv_taken, 2 * (lv - 1))
                elif lv == 0:
                    pe.wait_ge(decay_taken, 2)
                else:
                    pe.wait_ge(rcol_ready, 2)
                if lv < 8:
                    pe.wait_ge(lv_ready, 2 * (lv + 1))
                for t in range(TT) if lv else (0,):
                    j0, i0 = (t * P, t * P) if lv else (0, P)
                    for h in range(4):
                        r, c = head_rows(h), h // 2
                        kk = lvk[r, lv % 2, c, :] if lv < 8 else gk[r, c, :]
                        qq = lvq[r, lv % 2, c, :] if lv < 8 else gq[r, c, :]
                        a = (2 * t + c) * P
                        ins = pe.matmul(ps[b + h % 2][:, a:a + P], kk[:, j0:j0 + P], qq[:, i0:i0 + P],
                                        start=True, stop=True)
                ins.then_inc(lv_done, 1)
            if n == SUM_CKV_AT:
                pe.wait_ge(cx_acc, 2)
                pe.matmul(ps[3][:, 0:T], ones, acc[:, 0, :], start=True, stop=True).then_inc(sums_ready, 1)
            if n == SUM_CQ_AT:
                pe.wait_ge(cx_acc, 5)
                pe.wait_ge(r_ready, ROOTS["ckv"] + 1)
                pe.matmul(ps[3][:, T:2 * T], ones, acc[:, 1, :], start=True, stop=True).then_inc(sums_ready, 1)
            if n == COL_CKV_AT:
                column(Rkv, ps[3], "cq")
            if n == GLA_O_AT:
                pe.wait_ge(lv_taken, 18)
                pe.wait_ge(*taken(3, M2["uq"] - 1))
                for t in range(TT):
                    for h in range(4):
                        o = ps[4 + t][:, h * P:(h + 1) * P]
                        if t == 0:
                            ins = pe.matmul(o, at3[:, 0, h, :], gv[:, 0, h * P:(h + 1) * P], start=True, stop=True)
                        else:
                            pe.matmul(o, at3[:, 2, h, :], gv[:, 0, h * P:(h + 1) * P], start=True, stop=False)
                            ins = pe.matmul(o, at3[:, 1, h, :], gv[:, 1, h * P:(h + 1) * P], start=False, stop=True)
                ins.then_inc(gla_out, 1)
            if n == GLA_TURN_AT:
                pe.wait_ge(gla_scaled, 1)
                for h in range(4):
                    for t in range(TT):
                        a = (h % 2) * T + t * P
                        ins = pe.transpose(ps[4 + h // 2][:, a:a + P], go[:, t, h * P:(h + 1) * P], ident)
                ins.then_inc(gla_turned, 1)
            for s in range(NSEG2):
                if n == TURN2[s] + OUT_LAG:
                    pe.wait_ge(*taken(3, M2["gates"] - 1))
                    if s < 2:
                        pe.wait_ge(rcol_ready, 3)
                    weighted(NSEG1 + s, 12 + s, True, True,
                             [mv[:, t, s * HD:(s + 1) * HD] for t in range(TT)], pt2[:, s % 2, :])
            for s in range(NSEG2):
                if n == TURN2[s]:
                    turn(NSEG1 + s, 12 + s, p2[:, s % 3, :])
                if n == SCORES2[s]:
                    pe.wait_ge(*taken(3, M2["uv"] - 1))
                    if s == 0:
                        pe.wait_ge(gla_y, 4)
                    r = slice(32 * (s % 4), 32 * (s % 4) + 32)
                    scores(NSEG1 + s, qn[head_rows(s), s // 2, :], kn[head_rows(s), s // 2, :],
                           (qr[r, s // 4, :], kr[r, 0, :]))
        ffn(2, 4)

        pe.wait_ge(acc_ready, 48)
        for t in range(TT):
            ins = pe.matmul(ps[6][:, t:t + 1], acc[:, 0, t * P:(t + 1) * P], ones[:, 0:1], start=True, stop=True)
        ins.then_inc(sums_ready, 1)
        pe.wait_ge(fin_ready, KD)
        for g in range(8):
            t, c = divmod(g, 4)
            if g == 7:
                pe.wait_ge(fin_scaled, 1)
            for e in range(2):
                ins = pe.transpose(ps[FIN_BANK[g]][:, e * P:(e + 1) * P],
                                   o_fm[:, 2 * c + e, t * P:(t + 1) * P], ident)
            ins.then_inc(fin_turned, 1)

    block.__exit__(None, None, None)


_INS = ["x", "norm_ffn1", "ffn1_gate", "ffn1_up", "ffn1_down", "norm_mix", "w_in", "w_up_a", "w_up_b", "w_out",
        "norm_ffn2", "ffn2_gate", "ffn2_up", "ffn2_down", "norm_final", "positions_2", "ln_mix_2", "w_in_2",
        "mla_norm_cq_2", "mla_w_uq_2", "mla_norm_ckv_2", "mla_w_ukv_2", "mla_w_o_2", "gla_w_gate2_2",
        "gla_b_gate_2", "gla_norm_2", "gla_w_o_2", "w_out_2", "ln_ffn_2", "ffn_w_gate_2", "ffn_w_up_2",
        "ffn_w_down_2", "final_norm_2"]


def kernel(**inputs):
    import concourse.bacc as bacc
    from concourse.bass_utils import run_bass_kernel_spmd

    nc = bacc.Bacc("TRN2", target_bir_lowering=False, num_devices=1)
    arrays = {f"in_{n}": np.ascontiguousarray(inputs[n]) for n in _INS}
    arrays["in_consts"], arrays["in_masks"] = constants()
    w = {}
    for name, a in arrays.items():
        ap = nc.dram_tensor(name, a.shape, mybir.dt.from_np(a.dtype), kind="ExternalInput").ap()
        w[name[3:]] = ap[0] if len(a.shape) == 3 and name not in ("in_x", "in_gla_w_gate2_2") else ap
    out = nc.dram_tensor("out_0", (1, T, D), F32, kind="ExternalOutput").ap()
    build(nc, w, out[0])
    r = run_bass_kernel_spmd(nc, [arrays], core_ids=[0])
    return r.results[0]["out_0"]
```

```python
import math

import numpy as np
import concourse.bass as bass
from concourse import mybir

F32 = mybir.dt.float32
F32R = mybir.dt.float32r
I32 = mybir.dt.int32
ALU = mybir.AluOpType
ACT = mybir.ActivationFunctionType
AX = mybir.AxisListType

P = 128
BASE = 16384 + 128
T = 256
TT = T // P
D = 1024
KD = D // P
FF = 2816
NF = FF // P
EPS = 1e-6
HD = 64
GROUPS = ((128, 1), (512, 4), (2048, 16))
DSA_J = 4
DSA_W = 768
MOBA_W = 512
MLA_QK, MLA_NOPE, MLA_ROPE = 96, 64, 32
CQ, CKV = 384, 256
HEADS = 8
GLA_LEVELS = (128, 64, 32, 16, 8, 4, 2, 1)
GLA_CHUNK = 64
FAR = 1e33
RING = 4
RAW_W = 8 * 288
DOWN_K = ((0, 6), (6, 12), (12, 17), (17, 22))

QA, KA, VA = 0, DSA_W, 2 * DSA_W
QB = 3 * DSA_W
KB, VB = QB + MOBA_W, QB + 2 * MOBA_W
GA = QB + 3 * MOBA_W
C_KV = CQ
C_GQ = CQ + CKV + MLA_ROPE
C_GK, C_GV, C_LR = C_GQ + 256, C_GQ + 512, C_GQ + 1024
C_OG = C_LR + 16
C_GATES = C_OG + 512

VEC = {"norm_ffn1": 0, "norm_mix": 8, "norm_ffn2": 16, "norm_final": 24, "ln_mix_2": 32, "ln_ffn_2": 40,
       "final_norm_2": 48, "mla_norm_cq_2": 56, "mla_norm_ckv_2": 59, "gla_b_gate_2": 61, "gla_norm_2": 63}
NVEC = 64

C_IDENT, C_ONES, C_SEG, C_INV, C_SIGN = 0, 128, 256, 768 + 512, 768 + 513
C_DIST = C_SIGN + 1
NSEG = 384
N_CONST = C_DIST + 5 * NSEG


def constants():
    c = np.zeros((P, N_CONST), np.float32)
    c[:, C_IDENT:C_IDENT + P] = np.eye(P)
    c[:, C_ONES:C_ONES + P] = 1
    t = np.arange(2 * T)
    c[:, C_SEG:C_SEG + 2 * T] = t % GLA_CHUNK != 0
    c[:, C_SEG + 2 * T:C_SEG + 4 * T] = t % T != 0
    half = MLA_ROPE // 2
    inv = (np.float32(1.0) / (np.float32(10000.0) ** (np.arange(half, dtype=np.float32) / half))).astype(np.float32)
    p = np.arange(P)
    c[:, C_INV] = inv[p % half]
    c[:, C_SIGN] = np.where(p % MLA_ROPE < half, -1, 1)
    for g in range(5):
        for q0, k1, at in ((0, P, 0), (P, 2 * P, P)):
            d = (q0 + p[:, None]) - np.arange(k1)[None]
            ok = d >= 0
            if g < 3:
                window, dilation = GROUPS[g]
                ok &= (d <= window) & (d % dilation == 0)
            v = np.where(ok, d if g < 4 else 0, FAR)
            c[:, C_DIST + g * NSEG + at:C_DIST + g * NSEG + at + k1] = v
    m = np.zeros((P, 7, P), np.int32)
    j, i = p[:, None], p[None]
    for n, s in enumerate(GLA_LEVELS[2:]):
        m[:, n] = (j // (2 * s) == i // (2 * s)) & (j % (2 * s) < s) & (i % (2 * s) >= s)
    m[:, 6] = j == i
    return c, m.reshape(P, 7 * P)


class Half:

    def __init__(self, unit, kt, pieces):
        self.unit, self.kt, self.pieces = unit, kt, pieces

    def views(self, raw, part):
        return [(src(raw), dst(part[:, 0:self.kt * P].rearrange("p (k c) -> p k c", c=P)))
                for src, dst in self.pieces]


def plain(kt, width, c0):
    return [(lambda raw: raw[:, 0:kt * width].rearrange("p (k c) -> p k c", c=width)[:, :, c0:c0 + P],
             lambda part: part)]


def block2(kt, width, c0, stride, n, size):
    def src(raw):
        v = raw[:, 0:kt * width].rearrange("p (k g c) -> p k g c", k=kt, c=stride)
        return v[:, :, c0 // stride:c0 // stride + n, c0 % stride:c0 % stride + size]
    return [(src, lambda part: part.rearrange("p k (g c) -> p k g c", c=size))]


def swapped(kt, width, c0, stride, n):
    h = MLA_ROPE // 2
    out = []
    for e in range(2):
        def src(raw, e=e):
            v = raw[:, 0:kt * width].rearrange("p (k g c) -> p k g c", k=kt, c=stride)
            a = c0 % stride + (1 - e) * h
            return v[:, :, c0 // stride:c0 // stride + n, a:a + h]
        out.append((src, lambda part, e=e: part.rearrange("p k (g c) -> p k g c", c=MLA_ROPE)[
            :, :, :, e * h:e * h + h]))
    return out


def copies(kt, width, runs):
    total = sum(s for _, s in runs)
    out, at = [], 0
    for c0, size in runs:
        def src(raw, c0=c0, size=size):
            v = raw[:, 0:kt * width].rearrange("p (k c) -> p k c", c=width)[:, :, c0:c0 + size]
            return v.unsqueeze(2).to_broadcast([P, kt, P // total, size])
        out.append((src, lambda part, at=at, size=size: part.rearrange("p k (g c) -> p k g c", c=total)[
            :, :, :, at:at + size]))
        at += size
    return out


def mix1_plan(w):
    units, halves = [], []
    w_in = w["w_in"].rearrange("(k p) c -> p k c", p=P)

    def cols(c0):
        units.append([(0, KD, 256, w_in[:, :, c0:c0 + 256])])
        for h in range(2):
            halves.append(Half(len(units) - 1, KD, plain(KD, 256, h * P)))
    for c0 in range(QA, GA + 2 * D, 256):
        cols(c0)
    ua = w["w_up_a"].rearrange("(k p) c -> p k c", p=P)
    ub = w["w_up_b"].rearrange("(k p) c -> p k c", p=P)
    for c0 in range(0, D, 256):
        units.append([(0, 2, 256, ua[:, :, c0:c0 + 256]), (2, 4, 256, ub[:, :, c0:c0 + 256])])
        for h in range(2):
            halves.append(Half(len(units) - 1, 6, plain(6, 256, h * P)))
    wo = w["w_out"].rearrange("(k p) c -> p k c", p=P)
    for c0 in range(0, D, 256):
        units.append([(0, KD, 256, wo[:, :, c0:c0 + 256])])
        for h in range(2):
            halves.append(Half(len(units) - 1, KD, plain(KD, 256, h * P)))
    return units, halves


M1 = dict(qa=0, ka=6, va=12, qb=18, kb=22, vb=26, gates=30, merge=46, out=54, end=62)
M1_TOKEN = (12, 14, 16, 26, 28)
M2 = dict(lr=0, og=1, gq=3, gk=5, og2=7, kr=9, ckv=11, cq=13, gv=16, uq=20, uqr=24, ukv=28, uv=32,
          gates=36, merge=52, out=60, end=68)
M2_TOKEN = (16, 18, 32, 34)


def mix2_plan(w):
    units, halves = [], []
    w_in = w["w_in_2"].rearrange("(k p) c -> p k c", p=P)

    def unit(c0, width):
        units.append([(0, KD, width, w_in[:, :, c0:c0 + width])])
        return len(units) - 1

    def half(u, pieces, kt=KD):
        halves.append(Half(u, kt, pieces))

    u = unit(C_LR, 272)
    half(u, copies(KD, 272, [(0, 16)]))
    for h in range(2):
        half(u, plain(KD, 272, 16 + h * P))
    for c0 in (C_GQ, C_GK, C_OG + 256):
        u = unit(c0, 256)
        for h in range(2):
            half(u, plain(KD, 256, h * P))
    u = unit(C_KV, 288)
    half(u, copies(KD, 288, [(256, 32)]))
    half(u, copies(KD, 288, [(272, 16), (256, 16)]))
    for h in range(2):
        half(u, plain(KD, 288, h * P))
    u = unit(0, 256)
    for h in range(2):
        half(u, plain(KD, 256, h * P))
    half(unit(256, P), plain(KD, P, 0))
    for c0 in (C_GV, C_GV + 256):
        u = unit(c0, 256)
        for h in range(2):
            half(u, plain(KD, 256, h * P))
    kq, kk = CQ // P, CKV // P
    units.append([(0, kq, 768, w["mla_w_uq_2"].rearrange("(k p) c -> p k c", p=P))])
    u = len(units) - 1
    for c in range(4):
        half(u, block2(kq, 768, 2 * c * MLA_QK, MLA_QK, 2, MLA_NOPE), kq)
    for c in range(2):
        half(u, block2(kq, 768, 4 * c * MLA_QK + MLA_NOPE, MLA_QK, 4, MLA_ROPE), kq)
    for c in range(2):
        half(u, swapped(kq, 768, 4 * c * MLA_QK + MLA_NOPE, MLA_QK, 4), kq)
    units.append([(0, kk, 1024, w["mla_w_ukv_2"].rearrange("(k p) c -> p k c", p=P))])
    u = len(units) - 1
    for part in (0, MLA_NOPE):
        for c in range(4):
            half(u, block2(kk, 1024, 2 * c * P + part, P, 2, HD), kk)
    for c0 in range(C_GATES, C_GATES + 2 * D, 256):
        u = unit(c0, 256)
        for h in range(2):
            half(u, plain(KD, 256, h * P))
    oa = w["mla_w_o_2"].rearrange("(k p) c -> p k c", p=P)
    ob = w["gla_w_o_2"].rearrange("(k p) c -> p k c", p=P)
    for c0 in range(0, D, 256):
        units.append([(0, 4, 256, oa[:, :, c0:c0 + 256]), (4, 4, 256, ob[:, :, c0:c0 + 256])])
        for h in range(2):
            half(len(units) - 1, plain(8, 256, h * P), 8)
    wo = w["w_out_2"].rearrange("(k p) c -> p k c", p=P)
    for c0 in range(0, D, 256):
        units.append([(0, KD, 256, wo[:, :, c0:c0 + 256])])
        for h in range(2):
            half(len(units) - 1, plain(KD, 256, h * P))
    return units, halves


FFN_HALVES, FFN_UNITS = 4 * (NF // 2) + 4 * KD, NF + 4 * KD
FFN_UP = 4 * (NF // 2)
N_HALVES = (FFN_HALVES, M1["end"], FFN_HALVES, M2["end"], FFN_HALVES)
N_UNITS = (FFN_UNITS, 31, FFN_UNITS, 27, FFN_UNITS)
J0 = [sum(N_HALVES[:i]) for i in range(6)]
U0 = [sum(N_UNITS[:i]) for i in range(6)]

ROOTS = {n: i for i, n in enumerate(["x0", "x1", "x2", "x3", "ckv", "cq", "gla", "x4", "x5"])}
SUMS = {n: i for i, n in enumerate(["x1", "x2", "x3", "ckv", "cq", "x4", "x5"])}
ROWS = {n: i for i, n in enumerate(["x0", "x1", "x2", "x3", "ckv", "cq", "x4"])}
RCOL = {"ckv": 4, "cq": 6}

FIN_BANK = (0, 1, 2, 3, 4, 5, 6, 0)
NSEG1, NSEG2 = 20, 8
N_DSA = 12
SCORES1 = [12 + s for s in range(N_DSA)] + [14 + s for s in range(N_DSA, NSEG1)]
TURN1 = [17 + s for s in range(NSEG1)]
SCORES2 = [36 + s for s in range(NSEG2)]
TURN2 = [39 + s for s in range(NSEG2)]
OUT_LAG = 2
Z_AT, LEVEL_AT, GLA_O_AT, GLA_TURN_AT = 2, 9, 20, 23
SUM_CKV_AT, SUM_CQ_AT = 14, 17
OG_HALVES = (1, 2, 7, 8)


def alibi(n, of):
    return 2.0 ** (-8.0 * (n + 1) / of)


def build(nc, w, out):
    units1, halves1 = mix1_plan(w)
    units2, halves2 = mix2_plan(w)
    assert len(units1) == N_UNITS[1] and len(halves1) == M1["end"]
    assert len(units2) == N_UNITS[3] and len(halves2) == M2["end"]

    top = [BASE]

    def place(name, shape, dt=F32, at=None):
        words = int(np.prod(shape[1:]))
        if at is None:
            at = top[0]
            top[0] += 4 * words
            top[0] += -top[0] % 32
        return nc.alloc_sbuf_tensor_at(name, list(shape), dt, offset=at)

    raw = place("raw", [P, RING, RAW_W])
    hi = place("hi", [P, RING, 8 * P], F32R)
    lo = place("lo", [P, RING, 8 * P], F32R)
    x = place("x", [P, KD, T])
    xh = place("xh", [P, KD, T], F32R)
    xl = place("xl", [P, KD, T], F32R)
    cst = place("cst", [P, C_DIST])
    dist_at = top[0]
    dist = place("dist", [P, 5, NSEG])
    masks = place("masks", [P, 7, P], I32)
    vec = place("vec", [P, NVEC])
    vec2 = place("vec2", [P, 16])
    cosT = place("cosT", [P, T], at=dist_at)
    sinT = place("sinT", [P, T], at=dist_at + 1024)
    rope_q = place("rope_q", [P, 2, T], at=dist_at + 2048)
    rope_k = place("rope_k", [P, 2, T], at=dist_at + 4096)
    acc = place("acc", [P, 2, T])
    sq = place("sq", [P, 2, T])
    R = place("R", [P, T])
    R1 = place("R1", [P, T])
    Rq = place("Rq", [P, T])
    pos_i = place("pos_i", [P, T], I32, at=top[0])
    Rkv = place("Rkv", [P, T])
    var = place("var", [P, 2 * TT])
    root = place("root", [P, 2 * TT])
    newton = place("newton", [P, 2 * TT])
    rcol = place("rcol", [P, 4 * TT])
    x_sum = place("x_sum", [P, TT])
    scrap = place("scrap", [P, 8])
    tg = place("tg", [P, 2, T])
    tu = place("tu", [P, 2, T])
    sg = place("sg", [P, 2, T])
    hf = place("hf", [P, 2, T])
    region = top[0]
    hh = place("hh", [P, NF, T], F32R, at=region)
    hl = place("hl", [P, NF, T], F32R, at=region + 4 * NF * T)
    K = 1024
    x_in = place("x_in", [P, TT, D], at=region)
    vrow = place("vrow", [NVEC, P], at=region + 8 * K)
    x_sq = place("x_sq", [P, TT, D], at=region + 9 * K)
    qa = place("qa", [P, 6, T], at=region)
    ka = place("ka", [P, 6, T], at=region + 6 * K)
    va = place("va", [P, TT, DSA_W], at=region + 12 * K)
    gates1 = place("gates1", [P, 16, T], at=region)
    qb = place("qb", [P, 4, T], at=region + 18 * K)
    kb = place("kb", [P, 4, T], at=region + 22 * K)
    vb = place("vb", [P, TT, MOBA_W], at=region + 26 * K)
    mh1 = place("mh1", [P, KD, T], F32R, at=region + 18 * K)
    ml1 = place("ml1", [P, KD, T], F32R, at=region + 26 * K)
    s1 = place("s1", [P, 3, NSEG], at=region + 34 * K)
    p1 = place("p1", [P, 2, 3, NSEG], at=region + 39 * K)
    pt1 = place("pt1", [P, 2, NSEG], at=region + 48 * K)
    y1h = place("y1h", [P, 6, T], F32R, at=region + 51 * K)
    y1l = place("y1l", [P, 6, T], F32R, at=region + 57 * K)
    end1 = region + 63 * K
    ckv = place("ckv", [P, 2, T], at=region)
    ckvh = place("ckvh", [P, 2, T], F32R, at=region + 2 * K)
    ckvl = place("ckvl", [P, 2, T], F32R, at=region + 4 * K)
    cq = place("cq", [P, 3, T], at=region + 6 * K)
    cqh = place("cqh", [P, 3, T], F32R, at=region + 9 * K)
    cql = place("cql", [P, 3, T], F32R, at=region + 12 * K)
    gates2 = place("gates2", [P, 16, T], at=region)
    qn = place("qn", [P, 4, T], at=region + 16 * K)
    kn = place("kn", [P, 4, T], at=region + 20 * K)
    mv = place("mv", [P, TT, 512], at=region + 24 * K)
    qr = place("qr", [P, 2, T], at=region + 28 * K)
    kr = place("kr", [P, 1, T], at=region + 30 * K)
    mh2 = place("mh2", [P, KD, T], F32R, at=region + 16 * K)
    ml2 = place("ml2", [P, KD, T], F32R, at=region + 24 * K)
    gq = place("gq", [P, 2, T], at=region + 32 * K)
    gk = place("gk", [P, 2, T], at=region + 34 * K)
    run_chunk = place("run_chunk", [P, 2, T], at=region + 36 * K)
    run_all = place("run_all", [P, 2, T], at=region + 38 * K)
    s2 = place("s2", [P, 2, NSEG], at=region + 32 * K)
    p2 = place("p2", [P, 3, NSEG], at=region + 35 * K)
    pt2 = place("pt2", [P, 2, NSEG], at=dist_at + 2048)
    gv = place("gv", [P, TT, 512], at=region + 40 * K)
    lvq = place("lvq", [P, 2, 2, T], at=region + 44 * K)
    lvk = place("lvk", [P, 2, 2, T], at=region + 48 * K)
    y2ah = place("y2ah", [P, 4, T], F32R, at=region + 44 * K)
    y2al = place("y2al", [P, 4, T], F32R, at=region + 48 * K)
    at3 = place("at3", [P, 3, 4, P], at=region + 52 * K)
    osq = place("osq", [P, TT, 512], at=region + 44 * K)
    go_y = place("go_y", [P, 4, T], at=region + 52 * K)
    lr = place("lr", [P, T], at=region + 58 * K)
    wg2 = place("wg2", [16, 256], at=region + 59 * K)
    og = place("og", [P, 4, T], at=region + 60 * K)
    y2bh = place("y2bh", [P, 4, T], F32R, at=region + 56 * K)
    y2bl = place("y2bl", [P, 4, T], F32R, at=region + 40 * K)
    go = place("go", [P, TT, 512], at=region + 36 * K)
    zl = place("zl", [P, 2, T], at=region + 52 * K)
    ze = place("ze", [P, 2, T], at=region + 54 * K)
    end2 = region + 64 * K
    top[0] = max(end1, end2, region + 8 * NF * T)
    nmax = place("nmax", [P, 4])
    ssum = place("ssum", [P, 4])
    sinv = place("sinv", [P, 4])
    gss = place("gss", [P, 5, 8])
    assert top[0] <= 207 * K, top[0]
    o_fm = place("o_fm", [P, KD, T], at=region)
    o_tm = place("o_tm", [P, TT, D], at=region + 8 * K)
    lvd, lve = hf, sg
    ps = [nc.alloc_psum_tensor(f"bank{i}", [P, 512], F32) for i in range(8)]

    ident = cst[:, C_IDENT:C_IDENT + P]
    ones = cst[:, C_ONES:C_ONES + P]

    def sem(name):
        return nc.alloc_semaphore(name)

    raw_landed = [sem(f"raw_landed{i}") for i in range(RING)]
    ident_in, x_landed, gain_in, vec_in, const_in, small_in, pos_in = (
        sem(n) for n in ("ident_in", "x_landed", "gain_in", "vec_in", "const_in", "small_in", "pos_in"))
    split_hi, split_lo, half_done = sem("split_hi"), sem("split_lo"), sem("half_done")
    vec_turned, vec_ready, x_turned = sem("vec_turned"), sem("vec_ready"), sem("x_turned")
    x_updated, xh_ready, xl_ready, acc_ready = (
        sem(n) for n in ("x_updated", "xh_ready", "xl_ready", "acc_ready"))
    sums_ready, var_ready, root_ready, r_ready = (
        sem(n) for n in ("sums_ready", "var_ready", "root_ready", "r_ready"))
    token_sums, row_spread, row_ready = sem("token_sums"), sem("row_spread"), sem("row_ready")
    gate_scaled, up_scaled, silu_ready, hidden_ready, hidden_hi, hidden_lo = (
        sem(n) for n in ("gate_scaled", "up_scaled", "silu_ready", "hidden_ready", "hidden_hi", "hidden_lo"))
    half_taken = sem("half_taken")
    z_ready, tanh_ready, sig_ready = sem("z_ready"), sem("tanh_ready"), sem("sig_ready")
    cx_ready, cx_hi, cx_lo, cx_acc = sem("cx_ready"), sem("cx_hi"), sem("cx_lo"), sem("cx_acc")
    merge_ab, merged, merged_hi, merged_lo = sem("merge_ab"), sem("merged"), sem("merged_hi"), sem("merged_lo")
    seg_scores, seg_biased, seg_max, seg_probs = (
        sem(n) for n in ("seg_scores", "seg_biased", "seg_max", "seg_probs"))
    seg_inv, seg_norm, seg_turned, seg_copied, seg_out, y_hi, y_lo = (
        sem(n) for n in ("seg_inv", "seg_norm", "seg_turned", "seg_copied", "seg_out", "y_hi", "y_lo"))
    decay_raw, decay_taken, decay_logs = sem("decay_raw"), sem("decay_taken"), sem("decay_logs")
    lv_zero, lv_diff, lv_exp, lv_ready, lv_done, lv_taken = (
        sem(n) for n in ("lv_zero", "lv_diff", "lv_exp", "lv_ready", "lv_done", "lv_taken"))
    gla_out, gla_scaled, gla_turned, gla_y, yb_hi, yb_lo = (
        sem(n) for n in ("gla_out", "gla_scaled", "gla_turned", "gla_y", "yb_hi", "yb_lo"))
    residual_scaled = sem("residual_scaled")
    sin_arg, sin_ready = sem("sin_arg"), sem("sin_ready")
    fin_ready, fin_turned, fin_scaled, out_stored = (
        sem(n) for n in ("fin_ready", "fin_turned", "fin_scaled", "out_stored"))
    dve_step, act_step, pool_step = sem("dve_step"), sem("act_step"), sem("pool_step")

    W_UP = (("ffn1_gate", "ffn1_up", "ffn1_down"), ("ffn2_gate", "ffn2_up", "ffn2_down"),
            ("ffn_w_gate_2", "ffn_w_up_2", "ffn_w_down_2"))
    JF, UF, EF = [J0[0], J0[2], J0[4]], [U0[0], U0[2], U0[4]], [0, NF, 2 * NF]
    GAIN = [vec[:, VEC["norm_ffn1"]:], vec[:, VEC["norm_mix"]:], vec[:, VEC["norm_ffn2"]:], vec2[:, 0:8],
            vec[:, VEC["ln_ffn_2"]:], vec[:, VEC["final_norm_2"]:]]

    def part_of(j):
        n = max(i for i in range(5) if J0[i] <= j)
        return n, j - J0[n]

    def ffn_half(q):
        if q < FFN_UP:
            i, r = divmod(q, 4)
            return 2 * i + r % 2, KD, (r // 2) * P, 256
        k0, k1 = DOWN_K[(q - FFN_UP) % 4]
        return NF + q - FFN_UP, k1 - k0, 0, P

    def half_views(j, part):
        n, q = part_of(j)
        slot = part[:, j % RING, :]
        if n % 2 == 0:
            u, kt, c0, width = ffn_half(q)
            h = Half(u, kt, plain(kt, width, c0))
        else:
            h = (halves1, halves2)[n // 2][q]
        u = U0[n] + h.unit
        return h.views(raw[:, u % RING, :], slot), u

    def last_half(u):
        n = max(i for i in range(5) if U0[i] <= u)
        v = u - U0[n]
        if n % 2 == 0:
            q = 4 * (v // 2) + 2 + v % 2 if v < NF else FFN_UP + v - NF
        else:
            q = max(i for i, h in enumerate((halves1, halves2)[n // 2]) if h.unit == v)
        return J0[n] + q

    def w_part(part, j, k):
        return part[:, j % RING, k * P:(k + 1) * P]

    def w_pair(part, j, k):
        s = j % RING
        return part[:, s:s + 2, k * P:(k + 1) * P]

    def last_segment(k):
        return 3 * k + 2 if k < 4 else N_DSA + k - 4

    def scores1(k):
        s = last_segment(k)
        return s1[:, :, :] if k < 4 else s1[:, s % 3:s % 3 + 1, :]

    def probs1(k):
        s = last_segment(k)
        return p1[:, k % 2, :, :] if k < 4 else p1[:, 0, s % 3:s % 3 + 1, :]

    def probs1_of(s):
        return p1[:, (s // 3) % 2, s % 3, :] if s < N_DSA else p1[:, 0, s % 3, :]

    def taken(part, n):
        first = M1 if part == 1 else M2
        if n >= first["merge"]:
            return merge_ab, 2 * ((0 if part == 1 else KD) + n - first["merge"] + 1)
        if n >= first["gates"]:
            return z_ready, (0 if part == 1 else 20) + n - first["gates"] + 1
        if part == 1:
            return half_taken, n + 1
        if n in OG_HALVES:
            return z_ready, 16 + OG_HALVES.index(n) + 1
        if M2["ckv"] <= n < M2["gv"]:
            return cx_ready, n - M2["ckv"] + 1
        other = len([i for i in range(n) if i in OG_HALVES or M2["ckv"] <= i < M2["gv"]])
        return half_taken, M1["gates"] + n - other + 1

    block = nc.Block()
    block_ctx = block.__enter__()

    @block_ctx.sync
    def _(sp):
        def load(u, pieces, value=None, freed=None):
            if u >= RING or freed is not None:
                sp.wait_ge(split_lo, last_half(u - RING) + 1 if freed is None else freed)
            for k0, kt, width, src in pieces:
                dst = raw[:, u % RING, k0 * width:(k0 + kt) * width].rearrange("p (k c) -> p k c", c=width)
                sp.dma_start(dst, src).then_inc(raw_landed[u % RING], 16)

        def ffn(f):
            gate, up, down = (w[n] for n in W_UP[f])
            gate = gate.rearrange("(k p) c -> p k c", p=P)
            up = up.rearrange("(k p) c -> p k c", p=P)
            down = down.rearrange("(k p) c -> p k c", p=P)

            def pair(i, at, freed=None):
                for r, src in enumerate((gate, up)):
                    load(UF[f] + 2 * at + r, [(0, KD, 256, src[:, :, bass.ds(i * 256, 256)])],
                         freed=None if freed is None else freed + r)
            for i in range(3):
                pair(i, i)
            with sp.Fori(0, (NF // 2 - 3) // 2) as i:
                for b in range(2):
                    pair(i * 2 + (3 + b), 3 + b, freed=i * 8 + (JF[f] + 4 * (1 + b) + 3))
            for q in range(4 * KD):
                k0, k1 = DOWN_K[q % 4]
                m = q // 4
                load(UF[f] + NF + q, [(0, k1 - k0, P, down[:, k0:k1, m * P:(m + 1) * P])])

        def mixing(n, units):
            for v, pieces in enumerate(units):
                load(U0[n] + v, pieces)

        sp.dma_start(x_in[:, :, :], w["x"].rearrange("b (t p) d -> p (b t) d", p=P)).then_inc(x_landed, 16)
        sp.dma_start(cst[:, 0:C_SEG], w["consts"][:, 0:C_SEG]).then_inc(ident_in, 16)
        ffn(0)
        mixing(1, units1)
        ffn(1)
        mixing(3, units2)
        ffn(2)
        for t in range(TT):
            sp.wait_ge(fin_scaled, 4 * (t + 1))
            sp.dma_start(out[t * P:(t + 1) * P, :], o_tm[:, t, :]).then_inc(out_stored, 16)
        sp.wait_ge(out_stored, 16 * TT)

    def landed(eng, u):
        eng.wait_ge(raw_landed[u % RING], LANDED[u])

    LANDED = {}
    count = [0] * RING
    for u in range(U0[5]):
        n = max(i for i in range(5) if U0[i] <= u)
        pieces = 1 if n % 2 == 0 else len((units1, units2)[n // 2][u - U0[n]])
        count[u % RING] += 16 * pieces
        LANDED[u] = count[u % RING]

    @block_ctx.scalar
    def _(act):
        steps = [0]

        def link(ins):
            steps[0] += 1
            ins.then_inc(act_step, 1)
            act.wait_ge(act_step, steps[0])

        def vector(name, at, landed):
            n = w[name].shape[-1] // P
            src = w[name] if len(w[name].shape) == 1 else w[name][0]
            act.dma_start(vrow[at:at + n, :], src.rearrange("(a b) -> a b", b=P)).then_inc(landed, 16)

        def warm(func):
            link(act.activation(scrap[:, 0:1], ones[:, 0:1], func))

        def split(j):
            views, u = half_views(j, hi)
            landed(act, u)
            if j >= RING:
                act.wait_ge(half_done, j - RING + 1)
            for n, (src, dst) in enumerate(views):
                ins = act.activation(dst, src, ACT.Copy)
                if n == len(views) - 1:
                    ins.then_inc(split_hi, 1)

        def x_parts(wv):
            def tile(m):
                act.wait_ge(x_updated, 8 * wv + m + 1)
                act.activation(xh[:, m, :], x[:, m, :], ACT.Copy, scale=GAIN[wv][:, m:m + 1]).then_inc(xh_ready, 1)
            return tile

        def square_root(name, src=var[:, 0:TT], dst=root[:, 0:TT]):
            act.wait_ge(var_ready, ROOTS[name] + 1)
            act.activation(dst, src, ACT.Sqrt).then_inc(root_ready, 1)

        def ffn(f):
            J, E = JF[f], EF[f]

            def pair(e, b, ft):
                act.wait_ge(gate_scaled, e + 1)
                act.activation(sg[:, b, :], tg[:, b, :], ACT.Silu).then_inc(silu_ready, 1)

                def after():
                    act.wait_ge(hidden_ready, e + 1)
                    act.activation(hh[:, ft, :] if isinstance(ft, int) else hh[:, bass.ds(ft, 1), :],
                                   hf[:, b, :], ACT.Copy).then_inc(hidden_hi, 1)
                return after

            def split_in_loop(i, q):
                j = J + q
                views, u = half_views(j, hi)
                act.wait_ge(raw_landed[u % RING], i * 16 + LANDED[u])
                act.wait_ge(half_done, i * 8 + (j - RING + 1))
                for src, dst in views:
                    act.activation(dst, src, ACT.Copy).then_inc(split_hi, 1)

            def run(q0, n):
                for q in range(q0, q0 + n):
                    after = pair(E + q // 2, (q // 2) % 2, q // 2) if q % 2 else None
                    split(J + q + 4)
                    if after:
                        after()

            if f:
                square_root(f"x{2 * f}")
            warm(ACT.Silu)
            run(0, 4)
            with act.Fori(0, 4) as i:
                for q in range(4, 12):
                    after = pair(i * 4 + (E + q // 2), (q // 2) % 2, i * 4 + q // 2) if q % 2 else None
                    split_in_loop(i, q + 4)
                    if after:
                        after()
            run(36, 8)

        def down(f, tile, extra=None):
            J = JF[f]
            for q in range(FFN_UP, FFN_HALVES):
                if q % 4 == 3 and tile is not None:
                    tile((q - FFN_UP) // 4)
                if J + q + 4 < J0[5]:
                    split(J + q + 4)
                if q == FFN_HALVES - 8:
                    warm(ACT.Sqrt)
                if extra is not None and q in extra:
                    extra[q]()

        def exp(k, scores, probs):
            for t, (a, b) in enumerate(((0, P), (P, NSEG))):
                c = 2 * (k % 2) + t
                act.wait_ge(seg_max, 2 * k + t + 1)
                act.activation(probs[:, :, a:b], scores[:, :, a:b], ACT.Exp, bias=nmax[:, c:c + 1],
                               accum_out=ssum[:, c:c + 1]).then_inc(seg_probs, 1)

        def normalize(k, probs):
            for t, (a, b) in enumerate(((0, P), (P, NSEG))):
                c = 2 * (k % 2) + t
                act.wait_ge(seg_inv, 2 * k + t + 1)
                act.activation(probs[:, :, a:b], probs[:, :, a:b], ACT.Copy,
                               scale=sinv[:, c:c + 1]).then_inc(seg_norm, 1)

        def copy_turned(s, dst):
            act.wait_ge(seg_turned, s + 1)
            act.activation(dst, ps[6 + s % 2][:, 0:NSEG], ACT.Copy).then_inc(seg_copied, 1)

        def y_high(g, dst, rows):
            act.wait_ge(seg_out, g + 1)
            act.activation(dst[rows], ps[3][rows, 0:T], ACT.Copy).then_inc(y_hi, 1)

        def tanh_half(i):
            act.wait_ge(z_ready, i + 1)
            act.activation(tg[:, i % 2, :], tu[:, i % 2, :], ACT.Tanh, scale=0.5).then_inc(tanh_ready, 1)

        def merge_high(i, dst, m):
            act.wait_ge(merged, i + 1)
            act.activation(dst[:, m, :], hf[:, m % 2, :], ACT.Copy).then_inc(merged_hi, 1)

        vector("norm_ffn1", 0, gain_in)
        for name, at in VEC.items():
            if at:
                vector(name, at, vec_in)
        act.wait_ge(x_landed, 16)
        for t in range(TT):
            act.activation(x_sq[:, t, :], x_in[:, t, :], ACT.Square,
                           accum_out=x_sum[:, t:t + 1]).then_inc(token_sums, 1)
        act.wait_ge(ident_in, 16)
        warm(ACT.Sqrt)
        square_root("x0")
        split(0)
        tile = x_parts(0)
        act.wait_ge(vec_ready, 1)
        for m in range(KD):
            tile(m)
            if m % 2 and m < 6:
                split(m // 2 + 1)
        act.dma_start(cst[:, C_SEG:], w["consts"][:, C_SEG:C_DIST]).then_inc(const_in, 16)
        act.dma_start(dist[:, :, :], w["consts"][:, C_DIST:].rearrange("p (g c) -> p g c", c=NSEG)
                      ).then_inc(const_in, 16)
        act.dma_start(masks[:, :, :], w["masks"].rearrange("p (g c) -> p g c", c=P)).then_inc(const_in, 16)
        ffn(0)
        down(0, x_parts(1))

        square_root("x1")
        warm(ACT.Exp)
        tile2 = x_parts(2)
        for n in range(M1["end"]):
            for s in range(NSEG1):
                if n == TURN1[s] + 1:
                    copy_turned(s, pt1[:, s % 2, :])
            for k in range(12):
                if n == TURN1[last_segment(k)] + OUT_LAG + 1:
                    y_high(k, y1h[:, k // 2, :], slice(HD * (k % 2), HD * (k % 2) + HD))
            for k in range(12):
                s = last_segment(k)
                if n == SCORES1[s] + 2:
                    normalize(k, probs1(k))
                if n == SCORES1[s] + 1:
                    exp(k, scores1(k), probs1(k))
            if M1["gates"] <= n < M1["merge"]:
                tanh_half(n - M1["gates"])
            if n >= M1["out"]:
                tile2(n - M1["out"])
            if n == M1["out"] + 4:
                warm(ACT.Sqrt)
            split(J0[1] + n + 4)
            if M1["merge"] <= n < M1["out"]:
                merge_high(n - M1["merge"], mh1, n - M1["merge"])
        act.wait_ge(half_done, J0[2])
        act.dma_start(wg2[:, :], w["gla_w_gate2_2"][0]).then_inc(small_in, 16)
        act.dma_start(pos_i[:, :], w["positions_2"].to_broadcast([P, T])).then_inc(pos_in, 16)
        ffn(1)

        def rope_sines():
            act.wait_ge(sin_arg, 1)
            act.activation(cosT[:, :], tg[:, 0, :], ACT.Sin).then_inc(sin_ready, 1)
            act.wait_ge(sin_arg, 2)
            act.activation(sinT[:, :], tg[:, 1, :], ACT.Sin).then_inc(sin_ready, 1)
        down(1, x_parts(3), {FFN_UP + 14: rope_sines})

        square_root("x3", var[:, :], root[:, :])
        warm(ACT.Tanh)
        tile4 = x_parts(4)
        for n in range(M2["end"]):
            if n == Z_AT + 1:
                act.wait_ge(decay_taken, 2)
                link(act.activation(ze[:, :, :], zl[:, :, :], ACT.Abs))
                link(act.activation(ze[:, :, :], ze[:, :, :], ACT.Exp, scale=-1.0))
                act.activation(ze[:, :, :], ze[:, :, :], ACT.Ln, bias=1.0).then_inc(decay_logs, 1)
            if n == SUM_CKV_AT + 1:
                square_root("ckv")
            if n == SUM_CQ_AT + 1:
                square_root("cq")
            if n == GLA_O_AT + 1:
                square_root("gla", gss[:, 1, :], gss[:, 2, :])
            lv = n - LEVEL_AT + 2
            if 0 <= lv < 8:
                act.wait_ge(lv_diff, lv + 1)
                s = GLA_LEVELS[lv]
                dv = lvd[:, :, :].rearrange("p a (g c) -> p (a g) c", c=2 * s)
                ev = lve[:, :, :].rearrange("p a (g c) -> p (a g) c", c=2 * s)
                act.activation(ev[:, :, s:], dv[:, :, s:], ACT.Exp, scale=1.0 / 16.0).then_inc(lv_exp, 1)
                act.activation(ev[:, :, 0:s], dv[:, :, 0:s], ACT.Exp, scale=-1.0 / 16.0).then_inc(lv_exp, 1)
            if n == GLA_TURN_AT + 1:
                for h in range(4):
                    act.wait_ge(gla_y, h + 1)
                    act.activation(y2bh[:, h, :], go_y[:, h, :], ACT.Copy).then_inc(yb_hi, 1)
            for s in range(NSEG2):
                k = 12 + s
                if n == TURN2[s] + 1:
                    copy_turned(NSEG1 + s, pt2[:, s % 2, :])
                if n == TURN2[s] + OUT_LAG + 1:
                    y_high(k, y2ah[:, s // 2, :], slice(HD * (s % 2), HD * (s % 2) + HD))
            for s in range(NSEG2):
                k = 12 + s
                if n == SCORES2[s] + 2:
                    normalize(k, p2[:, s % 3:s % 3 + 1, :])
                if n == SCORES2[s] + 1:
                    exp(k, s2[:, s % 2:s % 2 + 1, :], p2[:, s % 3:s % 3 + 1, :])
            if n in OG_HALVES:
                tanh_half(16 + OG_HALVES.index(n))
            if M2["ckv"] <= n < M2["gv"]:
                i = n - M2["ckv"]
                src, dst, m, g = (ckv, ckvh, i, VEC["mla_norm_ckv_2"]) if i < 2 else (
                    cq, cqh, i - 2, VEC["mla_norm_cq_2"])
                act.wait_ge(cx_ready, i + 1)
                act.activation(dst[:, m, :], src[:, m, :], ACT.Copy,
                               scale=vec[:, g + m:g + m + 1]).then_inc(cx_hi, 1)
            if M2["gates"] <= n < M2["merge"]:
                tanh_half(20 + n - M2["gates"])
            if n >= M2["out"]:
                tile4(n - M2["out"])
            if n == M2["out"] + 4:
                warm(ACT.Sqrt)
            split(J0[3] + n + 4)
            if M2["merge"] <= n < M2["out"]:
                merge_high(KD + n - M2["merge"], mh2, n - M2["merge"])
        ffn(2)
        down(2, None)
        act.wait_ge(half_done, J0[5])
        for m in range(KD):
            act.wait_ge(x_updated, 8 * 5 + m + 1)
            act.activation(o_fm[:, m, :], x[:, m, :], ACT.Copy, scale=GAIN[5][:, m:m + 1]).then_inc(fin_ready, 1)
        square_root("x5")


    @block_ctx.vector
    def _(dve):
        steps = [0]

        def link(ins):
            steps[0] += 1
            ins.then_inc(dve_step, 1)
            dve.wait_ge(dve_step, steps[0])

        def split(j):
            views, u = half_views(j, lo)
            his = half_views(j, hi)[0]
            dve.wait_ge(split_hi, j + 1)
            for n, (src, dst) in enumerate(views):
                ins = dve.tensor_tensor(dst, src, his[n][1].bitcast(F32), ALU.subtract)
                if n == len(views) - 1:
                    ins.then_inc(split_lo, 1)

        def newton_root(name, v, s, tmp, dst):
            dve.wait_ge(root_ready, ROOTS[name] + 1)
            link(dve.reciprocal(s, s))
            link(dve.tensor_tensor(tmp, s, s, ALU.mult))
            link(dve.tensor_tensor(tmp, tmp, v, ALU.mult))
            link(dve.tensor_scalar(tmp, tmp, -0.5, 1.5, ALU.mult, ALU.add))
            dve.tensor_tensor(dst, tmp, s, ALU.mult).then_inc(r_ready, 1)
            dve.wait_ge(r_ready, ROOTS[name] + 1)

        def variance(dst, sums, n):
            dve.tensor_scalar(dst, sums, 1.0 / n, EPS, ALU.mult, ALU.add).then_inc(var_ready, 1)

        def row(name, src, *dsts):
            dve.wait_ge(row_spread, ROWS[name] + 1)
            for i, dst in enumerate(dsts):
                ins = dve.tensor_copy(dst, src[:, i * T:(i + 1) * T])
            ins.then_inc(row_ready, 1)
            dve.wait_ge(row_ready, ROWS[name] + 1)

        def norm(wv):
            name = f"x{wv}"
            if wv:
                dve.wait_ge(sums_ready, SUMS[name] + 1)
            else:
                dve.wait_ge(token_sums, TT)
            if wv == 3:
                link(dve.tensor_scalar(var[:, TT:], ps[7][:, 0:TT], 1.0 / D, EPS, ALU.mult, ALU.add))
                link(dve.tensor_scalar(var[:, 0:TT], ps[7][:, TT:2 * TT], 1.0 / D, None, ALU.mult))
                dve.scalar_tensor_tensor(out=var[:, 0:TT], in0=var[:, TT:], scalar=EPS, in1=var[:, 0:TT],
                                         op0=ALU.mult, op1=ALU.add).then_inc(var_ready, 1)
                newton_root(name, var[:, :], root[:, :], newton[:, :], rcol[:, 0:2 * TT])
            else:
                variance(var[:, 0:TT], ps[7][:, 0:TT] if wv else x_sum[:, :], D)
                newton_root(name, var[:, 0:TT], root[:, 0:TT], newton[:, 0:TT], rcol[:, 0:TT])

        def norm_row(wv):
            row(f"x{wv}", ps[6], R[:, :], *([R1[:, :]] if wv == 3 else []))

        def update(wv, m, factor):
            if wv == 4:
                dve.wait_ge(residual_scaled, m + 1)
            b = ps[4 + m % 2][:, 0:T]
            if factor == 1.0:
                dve.tensor_tensor(x[:, m, :], b, x[:, m, :], ALU.add).then_inc(x_updated, 1)
            else:
                dve.scalar_tensor_tensor(out=x[:, m, :], in0=b, scalar=factor, in1=x[:, m, :],
                                         op0=ALU.mult, op1=ALU.add).then_inc(x_updated, 1)

        def x_low(wv, m):
            dve.wait_ge(xh_ready, 8 * wv + m + 1)
            dve.scalar_tensor_tensor(out=xl[:, m, :], in0=x[:, m, :], scalar=GAIN[wv][:, m:m + 1],
                                     in1=xh[:, m, :].bitcast(F32), op0=ALU.mult,
                                     op1=ALU.subtract).then_inc(xl_ready, 1)

        def ffn(f):
            J, E = JF[f], EF[f]

            def pair(e, q, done):
                b = (q // 2) % 2
                dve.wait_ge(half_done, done)
                dve.tensor_tensor(tg[:, b, :], ps[(q - 1) % 8][:, 0:T], R[:, :], ALU.mult).then_inc(gate_scaled, 1)
                dve.tensor_tensor(tu[:, b, :], ps[q % 8][:, 0:T], R[:, :], ALU.mult).then_inc(up_scaled, 1)
                dve.wait_ge(up_scaled, e + 1)
                dve.wait_ge(silu_ready, e + 1)
                dve.tensor_tensor(hf[:, b, :], sg[:, b, :], tu[:, b, :], ALU.mult).then_inc(hidden_ready, 1)

            def low(e, q, ft):
                b = (q // 2) % 2
                dve.wait_ge(hidden_ready, e + 1)
                dve.wait_ge(hidden_hi, e + 1)
                o = hl[:, ft, :] if isinstance(ft, int) else hl[:, bass.ds(ft, 1), :]
                h = hh[:, ft, :] if isinstance(ft, int) else hh[:, bass.ds(ft, 1), :]
                src = hf[:, b, :] if isinstance(ft, int) else hf[:, b:b + 1, :]
                dve.tensor_tensor(o, src, h.bitcast(F32), ALU.subtract).then_inc(hidden_lo, 1)

            def run(q0, n):
                for q in range(q0, q0 + n):
                    if q % 2:
                        pair(E + q // 2, q, J + q + 1)
                    split(J + q + 4)
                    if q % 2:
                        low(E + q // 2, q, q // 2)
            run(0, 4)
            with dve.Fori(0, 4) as i:
                for q in range(4, 12):
                    if q % 2:
                        pair(i * 4 + (E + q // 2), q, i * 8 + (J + q + 1))
                    j = J + q + 4
                    views = half_views(j, lo)[0]
                    his = half_views(j, hi)[0]
                    dve.wait_ge(split_hi, i * 8 + (j + 1))
                    for (src, dst), (_, h) in zip(views, his):
                        dve.tensor_tensor(dst, src, h.bitcast(F32), ALU.subtract).then_inc(split_lo, 1)
                    if q % 2:
                        low(i * 4 + (E + q // 2), q, i * 4 + q // 2)
            run(36, 8)

        def down(f, wv, factor, extra=None):
            J = JF[f]
            for q in range(FFN_UP, FFN_HALVES):
                m = (q - FFN_UP) // 4
                if q % 4 == 3:
                    dve.wait_ge(half_done, J + q + 1)
                    update(wv, m, factor)
                if q == FFN_HALVES - 1 and wv < 5:
                    x_low(wv, m)
                if J + q + 4 < J0[5]:
                    split(J + q + 4)
                if q % 4 == 3 and wv < 5 and q < FFN_HALVES - 1:
                    x_low(wv, m)
                if extra is not None and q in extra:
                    extra[q]()

        def latent_norm(name, n):
            dve.wait_ge(sums_ready, SUMS[name] + 1)
            variance(var[:, 0:TT], ps[3][:, T:T + TT], n)
            newton_root(name, var[:, 0:TT], root[:, 0:TT], newton[:, 0:TT], rcol[:, RCOL[name]:RCOL[name] + TT])

        def gate_half(i, n):
            if i >= 2:
                dve.wait_ge(sig_ready, i - 1)
            dve.tensor_tensor(tu[:, i % 2, :], ps[n % 3][:, 0:T], R[:, :], ALU.mult).then_inc(z_ready, 1)

        def merge(i, m, n, gates):
            a = dve.tensor_tensor(tg[:, m % 2, :], ps[n % 3][:, 0:T], gates[:, m, :], ALU.mult)
            a.then_inc(merge_ab, 1)
            dve.tensor_tensor(tu[:, m % 2, :], ps[n % 3][:, T:2 * T], gates[:, KD + m, :],
                              ALU.mult).then_inc(merge_ab, 1)

        def merge_low(i, m, dst_hi, dst_lo):
            dve.wait_ge(merged_hi, i + 1)
            dve.tensor_tensor(dst_lo[:, m, :], hf[:, m % 2, :], dst_hi[:, m, :].bitcast(F32),
                              ALU.subtract).then_inc(merged_lo, 1)

        def bias(s, g, slope, dst, waits):
            dve.wait_ge(seg_scores, s + 1)
            if waits:
                dve.wait_ge(seg_probs, waits)
            dve.scalar_tensor_tensor(out=dst, in0=dist[:, g, :], scalar=-slope,
                                     in1=ps[4 + s % 2][:, 0:NSEG], op0=ALU.mult,
                                     op1=ALU.add).then_inc(seg_biased, 1)

        def maxima(k, s, scores):
            dve.wait_ge(seg_biased, s + 1)
            for t, (a, b) in enumerate(((0, P), (P, NSEG))):
                c = 2 * (k % 2) + t
                dve.tensor_reduce(nmax[:, c:c + 1], scores[:, :, a:b], AX.XY, ALU.max,
                                  negate=True).then_inc(seg_max, 1)

        def inverse(k):
            for t in range(2):
                c = 2 * (k % 2) + t
                dve.wait_ge(seg_probs, 2 * k + t + 1)
                dve.reciprocal(sinv[:, c:c + 1], ssum[:, c:c + 1]).then_inc(seg_inv, 1)

        def y_low(k, dst_hi, dst_lo, rows):
            dve.wait_ge(seg_out, k + 1)
            dve.wait_ge(y_hi, k + 1)
            dve.tensor_tensor(dst_lo[rows], ps[3][rows, 0:T], dst_hi[rows].bitcast(F32),
                              ALU.subtract).then_inc(y_lo, 1)

        norm(0)
        dve.wait_ge(vec_turned, 1)
        dve.tensor_copy(vec[:, 0:KD], ps[0][:, 0:KD]).then_inc(vec_ready, 1)
        dve.wait_ge(vec_ready, 1)
        for m in range(KD):
            dve.wait_ge(x_turned, m + 1)
            dve.tensor_copy(x[:, m, :], ps[4 + m // 2][:, (m % 2) * T:(m % 2 + 1) * T]).then_inc(x_updated, 1)
            dve.wait_ge(x_updated, m + 1)
            if m == 1:
                split(0)
            if m:
                x_low(0, m - 1)
        split(1)
        x_low(0, KD - 1)
        split(2)
        norm_row(0)
        split(3)
        dve.wait_ge(vec_turned, 2)
        dve.tensor_copy(vec[:, KD:], ps[7][:, KD:NVEC]).then_inc(vec_ready, 1)
        dve.wait_ge(vec_ready, 2)
        vf, vl = VEC["norm_final"], VEC["ln_mix_2"]
        dve.tensor_tensor(vec2[:, 0:8], vec[:, vf:vf + 8], vec[:, vl:vl + 8], ALU.mult).then_inc(vec_ready, 1)
        dve.tensor_tensor(vec2[:, 8:16], vec[:, vf:vf + 8], vec[:, vf:vf + 8], ALU.mult).then_inc(vec_ready, 1)
        ffn(0)
        down(0, 1, 0.5)

        norm(1)
        norm_row(1)
        dve.wait_ge(const_in, 48)
        for n in range(M1["end"]):
            for k in range(12):
                s = last_segment(k)
                if n == SCORES1[s] + 2:
                    inverse(k)
            for s in range(NSEG1):
                if n == SCORES1[s] + 1:
                    if s < N_DSA:
                        k, g = divmod(s, 3)
                        bias(s, g, alibi(4 * g + k, 12), s1[:, g, :], 2 * k)
                    else:
                        k, g = 4 + s - N_DSA, 2
                        bias(s, 3, alibi(s - N_DSA, HEADS), s1[:, s % 3, :], 8 if k < 7 else 2 * (k - 2))
                    if g == 2:
                        maxima(k, s, scores1(k))
            for k in range(12):
                if n == TURN1[last_segment(k)] + OUT_LAG + 1:
                    y_low(k, y1h[:, k // 2, :], y1l[:, k // 2, :], slice(HD * (k % 2), HD * (k % 2) + HD))
            if n < M1["out"] and not (n - 1 in M1_TOKEN or n in M1_TOKEN):
                dve.wait_ge(half_done, J0[1] + n + 1)
            bank = ps[n % 3][:, 0:T]
            if n < M1["ka"]:
                dve.scalar_tensor_tensor(out=qa[:, n, :], in0=bank, scalar=HD ** -0.5, in1=R[:, :],
                                         op0=ALU.mult, op1=ALU.mult).then_inc(half_taken, 1)
            elif n < M1["va"]:
                dve.tensor_tensor(ka[:, n - M1["ka"], :], bank, R[:, :], ALU.mult).then_inc(half_taken, 1)
            elif n - 1 in M1_TOKEN:
                dve.wait_ge(half_done, J0[1] + n + 1)
                dst, c = (va, n - 1 - M1["va"]) if n < M1["qb"] else (vb, n - 1 - M1["vb"])
                for t in range(TT):
                    dve.tensor_scalar(dst[:, t, c * P:c * P + 256], ps[(n - 1 + t) % 3][:, 0:T],
                                      rcol[:, t:t + 1], None, ALU.mult).then_inc(half_taken, 1)
            elif n in M1_TOKEN:
                pass
            elif n < M1["kb"]:
                dve.scalar_tensor_tensor(out=qb[:, n - M1["qb"], :], in0=bank, scalar=HD ** -0.5, in1=R[:, :],
                                         op0=ALU.mult, op1=ALU.mult).then_inc(half_taken, 1)
            elif n < M1["vb"]:
                dve.tensor_tensor(kb[:, n - M1["kb"], :], bank, R[:, :], ALU.mult).then_inc(half_taken, 1)
            elif n < M1["merge"]:
                gate_half(n - M1["gates"], n)
            elif n < M1["out"]:
                m = n - M1["merge"]
                if m == 0:
                    dve.wait_ge(sig_ready, 16)
                merge(m, m, n, gates1)
            else:
                m = n - M1["out"]
                dve.wait_ge(half_done, J0[1] + n + 1)
                update(2, m, 1.0)
                if m == KD - 1:
                    x_low(2, m)
            split(J0[1] + n + 4)
            if M1["merge"] <= n < M1["out"]:
                merge_low(n - M1["merge"], n - M1["merge"], mh1, ml1)
            if M1["out"] <= n < M1["end"] - 1:
                x_low(2, n - M1["out"])
        norm(2)
        norm_row(2)
        ffn(1)

        angle, whole = tg[:, 0, :], tg[:, 1, :]

        def rope_start():
            dve.wait_ge(pos_in, 16)
            link(dve.tensor_copy(angle, pos_i[:, :]))
            link(dve.tensor_scalar(angle, angle, cst[:, C_INV:C_INV + 1], None, ALU.mult))

        def rope_whole(turns):
            magic = 1.5 * 2.0 ** 23
            link(dve.tensor_scalar(whole, angle, 1.0 / (2 * math.pi * turns), None, ALU.mult))
            link(dve.tensor_scalar(whole, whole, magic, None, ALU.add))
            link(dve.tensor_scalar(whole, whole, -magic, None, ALU.add))

        def rope_less(turns):
            c1 = 6.28125
            c2 = float(np.floor((2 * math.pi - c1) * 2.0 ** 20) / 2.0 ** 20)
            for c in (c1, c2, float(np.float32(2 * math.pi - c1 - c2))):
                link(dve.scalar_tensor_tensor(out=angle, in0=whole, scalar=-c * turns, in1=angle,
                                              op0=ALU.mult, op1=ALU.add))

        def rope_arguments():
            lim = 3.1415925
            link(dve.tensor_scalar(whole, angle, -lim, lim, ALU.max, ALU.min))
            link(dve.tensor_scalar(angle, whole, -1.0, None, ALU.mult))
            link(dve.tensor_tensor(angle, whole, angle, ALU.max))
            dve.tensor_scalar(angle, angle, -1.0, math.pi / 2, ALU.mult, ALU.add).then_inc(sin_arg, 2)

        def rope_tables():
            dve.wait_ge(sin_ready, 2)
            link(dve.tensor_scalar(sinT[:, :], sinT[:, :], cst[:, C_SIGN:C_SIGN + 1], None, ALU.mult))
        down(1, 3, 0.5, {FFN_UP + 2: rope_start, FFN_UP + 4: lambda: rope_whole(4096.0),
                         FFN_UP + 5: lambda: rope_less(4096.0), FFN_UP + 8: lambda: rope_whole(1.0),
                         FFN_UP + 9: lambda: rope_less(1.0), FFN_UP + 12: rope_arguments,
                         FFN_UP + 18: rope_tables})

        norm(3)
        norm_row(3)
        link(dve.tensor_tensor(rope_k[:, 0, :], cosT[:, :], R[:, :], ALU.mult))
        link(dve.tensor_tensor(rope_k[:, 1, :], sinT[:, :], R[:, :], ALU.mult))
        for n in range(M2["end"]):
            if n == Z_AT + 1:
                dve.wait_ge(decay_raw, 1)
                for c in range(2):
                    v = VEC["gla_b_gate_2"] + c
                    dve.tensor_scalar(zl[:, c, :], ps[4][:, c * T:(c + 1) * T], vec[:, v:v + 1], None,
                                      ALU.add).then_inc(decay_taken, 1)
            if n == Z_AT + 2:
                dve.wait_ge(decay_logs, 1)
                link(dve.scalar_tensor_tensor(out=zl[:, :, :], in0=zl[:, :, :], scalar=0.0, in1=ze[:, :, :],
                                              op0=ALU.min, op1=ALU.subtract))
                flat = zl[:, :, :].rearrange("p a c -> p (a c)")
                for dst, c in ((run_chunk, C_SEG), (run_all, C_SEG + 2 * T)):
                    link(dve.tensor_tensor_scan(dst[:, :, :].rearrange("p a c -> p (a c)"), cst[:, c:c + 2 * T],
                                                flat, 0.0, ALU.mult, ALU.add))
            lv = n - LEVEL_AT + 1
            if 0 <= lv < 8:
                s = GLA_LEVELS[lv]
                dve.wait_ge(lv_exp, 2 * (lv + 1))
                dve.wait_ge(lv_zero, lv + 1)

                def at(v, a, b):
                    return v.rearrange("p a (g c) -> p (a g) c", c=2 * s)[:, :, a:b]
                dve.tensor_tensor(at(lvq[:, lv % 2, :, :], s, 2 * s), at(gq[:, :, :], s, 2 * s),
                                  at(lve[:, :, :], s, 2 * s), ALU.mult).then_inc(lv_ready, 1)
                dve.tensor_tensor(at(lvk[:, lv % 2, :, :], 0, s), at(gk[:, :, :], 0, s),
                                  at(lve[:, :, :], 0, s), ALU.mult).then_inc(lv_ready, 1)
            if 0 <= lv + 1 < 8:
                s = GLA_LEVELS[lv + 1]
                src = (run_all if s >= GLA_CHUNK else run_chunk)[:, :, :].rearrange("p a (g c) -> p (a g) c", c=2 * s)
                g = 2 * T // (2 * s)
                dve.tensor_tensor(lvd[:, :, :].rearrange("p a (g c) -> p (a g) c", c=2 * s), src,
                                  src[:, :, s - 1:s].to_broadcast([P, g, 2 * s]), ALU.subtract).then_inc(lv_diff, 1)
            lv = n - LEVEL_AT - 1
            if 0 <= lv < 9:
                dve.wait_ge(lv_done, lv + 1)
                if lv:
                    dve.wait_ge(lv_taken, 2 * lv)
                b = 4 + 2 * (lv % 2)
                for e in range(2):
                    if lv == 0:
                        ins = dve.tensor_copy(at3[:, 2, e::2, :], ps[b + e][:, 0:T].rearrange("p (h c) -> p h c", c=P))
                    else:
                        dst = at3[:, 0:2, e::2, :]
                        src = ps[b + e][:, :].rearrange("p (t h c) -> p t h c", h=2, c=P)
                        if lv == 1:
                            ins = dve.tensor_copy(dst, src)
                        else:
                            m_ = masks[:, lv - 2:lv - 1, :].unsqueeze(2).to_broadcast([P, 2, 2, P])
                            ins = dve.copy_predicated(dst, m_, src)
                    ins.then_inc(lv_taken, 1)
            if n == SUM_CKV_AT + 1:
                latent_norm("ckv", CKV)
            if n == SUM_CKV_AT + 2:
                row("ckv", ps[3], Rkv[:, :])
            if n == SUM_CQ_AT + 1:
                latent_norm("cq", CQ)
            if n == SUM_CQ_AT + 2:
                row("cq", ps[3], Rq[:, :])
                for c, tab in enumerate((cosT, sinT)):
                    link(dve.scalar_tensor_tensor(out=rope_q[:, c, :], in0=tab[:, :], scalar=MLA_QK ** -0.5,
                                                  in1=Rq[:, :], op0=ALU.mult, op1=ALU.mult))
            if n == GLA_O_AT + 1:
                dve.wait_ge(gla_out, 1)
                for t in range(TT):
                    link(dve.tensor_copy(go[:, t, :], ps[4 + t][:, :]))
                link(dve.tensor_tensor(osq[:, :, :], go[:, :, :], go[:, :, :], ALU.mult))
                link(dve.tensor_reduce(gss[:, 0, :], osq[:, :, :].rearrange("p t (h c) -> p (t h) c", c=P),
                                       AX.X, ALU.add))
                variance(gss[:, 1, :], gss[:, 0, :], P)
                newton_root("gla", gss[:, 1, :], gss[:, 2, :], gss[:, 3, :], gss[:, 4, :])
                gh = go[:, :, :].rearrange("p t (h c) -> p (t h) c", c=P)
                dve.tensor_tensor(gh, gh, gss[:, 4, :].unsqueeze(2).to_broadcast([P, 8, P]),
                                  ALU.mult).then_inc(gla_scaled, 1)
            if n == GLA_TURN_AT + 1:
                dve.wait_ge(gla_turned, 1)
                dve.wait_ge(sig_ready, 20)
                v = VEC["gla_norm_2"]
                for h in range(4):
                    dve.scalar_tensor_tensor(out=go_y[:, h, :], in0=ps[4 + h // 2][:, (h % 2) * T:(h % 2 + 1) * T],
                                             scalar=vec[:, v:v + 1], in1=og[:, h, :], op0=ALU.mult,
                                             op1=ALU.mult).then_inc(gla_y, 1)
                for h in range(4):
                    dve.wait_ge(gla_y, h + 1)
                    dve.wait_ge(yb_hi, h + 1)
                    dve.tensor_tensor(y2bl[:, h, :], go_y[:, h, :], y2bh[:, h, :].bitcast(F32),
                                      ALU.subtract).then_inc(yb_lo, 1)
            for s in range(NSEG2):
                k = 12 + s
                if n == SCORES2[s] + 2:
                    inverse(k)
            for s in range(NSEG2):
                k = 12 + s
                if n == SCORES2[s] + 1:
                    bias(NSEG1 + s, 4, 1.0, s2[:, s % 2, :], 2 * (k - 1) if s >= 2 else 0)
                    maxima(k, NSEG1 + s, s2[:, s % 2:s % 2 + 1, :])
                if n == TURN2[s] + OUT_LAG + 1:
                    y_low(k, y2ah[:, s // 2, :], y2al[:, s // 2, :], slice(HD * (s % 2), HD * (s % 2) + HD))
            if n < M2["out"] and not (n - 1 in M2_TOKEN or n in M2_TOKEN):
                dve.wait_ge(half_done, J0[3] + n + 1)
            bank = ps[n % 3][:, 0:T]
            rot = acc[:, 1, :]
            if n == M2["lr"]:
                dve.tensor_tensor(lr[:, :], bank, R[:, :], ALU.mult).then_inc(half_taken, 1)
            elif n in OG_HALVES:
                gate_half(16 + OG_HALVES.index(n), n)
            elif n < M2["gk"]:
                dve.scalar_tensor_tensor(out=gq[:, n - M2["gq"], :], in0=bank, scalar=HD ** -0.5, in1=R[:, :],
                                         op0=ALU.mult, op1=ALU.mult).then_inc(half_taken, 1)
            elif n < M2["og2"]:
                dve.tensor_tensor(gk[:, n - M2["gk"], :], bank, R[:, :], ALU.mult).then_inc(half_taken, 1)
            elif n == M2["kr"]:
                dve.tensor_tensor(kr[:, 0, :], bank, rope_k[:, 0, :], ALU.mult).then_inc(half_taken, 1)
            elif n == M2["kr"] + 1:
                dve.tensor_tensor(rot, bank, rope_k[:, 1, :], ALU.mult).then_inc(half_taken, 1)
                dve.wait_ge(*taken(3, n))
                link(dve.tensor_tensor(kr[:, 0, :], kr[:, 0, :], rot, ALU.add))
            elif n < M2["gv"]:
                i = n - M2["ckv"]
                dst, m = (ckv, i) if i < 2 else (cq, i - 2)
                dve.tensor_tensor(dst[:, m, :], bank, R[:, :], ALU.mult).then_inc(cx_ready, 1)
            elif n - 1 in M2_TOKEN:
                dve.wait_ge(half_done, J0[3] + n + 1)
                dst, c, r = (gv, n - 1 - M2["gv"], 0) if n < M2["uq"] else (mv, n - 1 - M2["uv"], RCOL["ckv"])
                for t in range(TT):
                    dve.tensor_scalar(dst[:, t, c * P:c * P + 256], ps[(n - 1 + t) % 3][:, 0:T],
                                      rcol[:, r + t:r + t + 1], None, ALU.mult).then_inc(half_taken, 1)
            elif n in M2_TOKEN:
                pass
            elif n < M2["uqr"]:
                dve.scalar_tensor_tensor(out=qn[:, n - M2["uq"], :], in0=bank, scalar=MLA_QK ** -0.5,
                                         in1=Rq[:, :], op0=ALU.mult, op1=ALU.mult).then_inc(half_taken, 1)
            elif n < M2["uqr"] + 2:
                dve.tensor_tensor(qr[:, n - M2["uqr"], :], bank, rope_q[:, 0, :], ALU.mult).then_inc(half_taken, 1)
            elif n < M2["ukv"]:
                c = n - M2["uqr"] - 2
                dve.tensor_tensor(rot, bank, rope_q[:, 1, :], ALU.mult).then_inc(half_taken, 1)
                dve.wait_ge(*taken(3, n))
                link(dve.tensor_tensor(qr[:, c, :], qr[:, c, :], rot, ALU.add))
            elif n < M2["uv"]:
                dve.tensor_tensor(kn[:, n - M2["ukv"], :], bank, Rkv[:, :], ALU.mult).then_inc(half_taken, 1)
            elif n < M2["merge"]:
                gate_half(20 + n - M2["gates"], n)
            elif n < M2["out"]:
                m = n - M2["merge"]
                if m == 0:
                    dve.wait_ge(sig_ready, 36)
                merge(KD + m, m, n, gates2)
            else:
                m = n - M2["out"]
                dve.wait_ge(half_done, J0[3] + n + 1)
                update(4, m, 1.0)
                if m == KD - 1:
                    x_low(4, m)
            split(J0[3] + n + 4)
            if M2["ckv"] <= n < M2["gv"]:
                i = n - M2["ckv"]
                src, dh, dl, m, g = (ckv, ckvh, ckvl, i, VEC["mla_norm_ckv_2"]) if i < 2 else (
                    cq, cqh, cql, i - 2, VEC["mla_norm_cq_2"])
                dve.wait_ge(cx_ready, i + 1)
                dve.wait_ge(cx_hi, i + 1)
                dve.scalar_tensor_tensor(out=dl[:, m, :], in0=src[:, m, :], scalar=vec[:, g + m:g + m + 1],
                                         in1=dh[:, m, :].bitcast(F32), op0=ALU.mult,
                                         op1=ALU.subtract).then_inc(cx_lo, 1)
            if M2["merge"] <= n < M2["out"]:
                merge_low(KD + n - M2["merge"], n - M2["merge"], mh2, ml2)
            if M2["out"] <= n < M2["end"] - 1:
                x_low(4, n - M2["out"])
        norm(4)
        norm_row(4)
        ffn(2)
        down(2, 5, 1.0)
        norm(5)
        for t in range(TT):
            for c in range(4):
                dve.wait_ge(fin_turned, 4 * t + c + 1)
                dve.tensor_scalar(o_tm[:, t, c * 256:(c + 1) * 256], ps[FIN_BANK[4 * t + c]][:, 0:256],
                                  rcol[:, t:t + 1], None, ALU.mult).then_inc(fin_scaled, 1)

    @block_ctx.gpsimd
    def _(pool):
        steps = [0]

        def link(ins):
            steps[0] += 1
            ins.then_inc(pool_step, 1)
            pool.wait_ge(pool_step, steps[0])

        def squares(wv, m):
            pool.wait_ge(x_updated, 8 * wv + m + 1)
            two = wv == 3
            first = m == 0
            if wv > 1 or m:
                pool.wait_ge(acc_ready, 8 * (wv - 1) + m)
            to = acc[:, 0, :] if first else sq[:, 0, :]
            ins = pool.tensor_tensor(to, x[:, m, :], x[:, m, :], ALU.mult)
            if first and not two:
                ins.then_inc(acc_ready, 1)
                return
            link(ins)
            if two:
                ins = pool.tensor_scalar(acc[:, 1, :] if first else sq[:, 1, :], to, vec2[:, 8 + m:9 + m], None,
                                         ALU.mult)
                if first:
                    ins.then_inc(acc_ready, 1)
                    return
                link(ins)
                link(pool.tensor_tensor(acc[:, 0, :], acc[:, 0, :], sq[:, 0, :], ALU.add))
                pool.tensor_tensor(acc[:, 1, :], acc[:, 1, :], sq[:, 1, :], ALU.add).then_inc(acc_ready, 1)
            else:
                pool.tensor_tensor(acc[:, 0, :], acc[:, 0, :], sq[:, 0, :], ALU.add).then_inc(acc_ready, 1)

        def sigmoid(i, dst):
            pool.wait_ge(tanh_ready, i + 1)
            pool.tensor_scalar(dst, tg[:, i % 2, :], 0.5, 0.5, ALU.mult, ALU.add).then_inc(sig_ready, 1)

        def add_parts(i):
            pool.wait_ge(merge_ab, 2 * (i + 1))
            pool.tensor_tensor(hf[:, i % 2, :], tg[:, i % 2, :], tu[:, i % 2, :], ALU.add).then_inc(merged, 1)

        for m in range(KD):
            squares(1, m)
        for i in range(16):
            sigmoid(i, gates1[:, i, :])
        for m in range(KD):
            add_parts(m)
        for wv in (2, 3):
            for m in range(KD):
                squares(wv, m)

        def og_half(c):
            i = 16 + c
            pool.wait_ge(tanh_ready, i + 1)
            link(pool.tensor_scalar(tg[:, i % 2, :], tg[:, i % 2, :], 0.5, 0.5, ALU.mult, ALU.add))
            pool.tensor_tensor(og[:, c, :], tu[:, i % 2, :], tg[:, i % 2, :], ALU.mult).then_inc(sig_ready, 1)

        def level_zero(lv):
            if lv >= 2:
                pool.wait_ge(lv_done, lv - 1)
            link(pool.memset(lvq[:, lv % 2, :, :], 0.0))
            pool.memset(lvk[:, lv % 2, :, :], 0.0).then_inc(lv_zero, 1)

        def cx_squares(i):
            pool.wait_ge(cx_ready, i + 1)
            c, first = (0, i == 0) if i < 2 else (1, i == 2)
            src = ckv[:, i, :] if i < 2 else cq[:, i - 2, :]
            ins = pool.tensor_tensor(acc[:, c, :] if first else sq[:, 0, :], src, src, ALU.mult)
            if first:
                ins.then_inc(cx_acc, 1)
            else:
                link(ins)
                pool.wait_ge(cx_acc, i)
                pool.tensor_tensor(acc[:, c, :], acc[:, c, :], sq[:, 0, :], ALU.add).then_inc(cx_acc, 1)
        og_half(0)
        og_half(1)
        level_zero(0)
        level_zero(1)
        og_half(2)
        og_half(3)
        level_zero(2)
        for i in range(5):
            level_zero(3 + i)
            cx_squares(i)
        pool.wait_ge(xh_ready, 32)
        pool.wait_ge(xl_ready, 32)
        pool.wait_ge(row_ready, ROWS["x3"] + 1)
        v = VEC["norm_final"]
        for m in range(KD):
            link(pool.tensor_scalar(x[:, m, :], x[:, m, :], vec[:, v + m:v + m + 1], None, ALU.mult))
            pool.tensor_tensor(x[:, m, :], x[:, m, :], R1[:, :], ALU.mult).then_inc(residual_scaled, 1)
        for i in range(16):
            sigmoid(20 + i, gates2[:, i, :])
        for m in range(KD):
            add_parts(KD + m)
        for wv in (4, 5):
            for m in range(KD):
                squares(wv, m)

    @block_ctx.tensor
    def _(pe):
        def feature_half(j, bank, k0, kt, xs, start=True, stop=True, each=None, at=0):
            for k in range(kt):
                if each is not None:
                    each(k)
                a = (w_part(hi, j, k0 + k), w_part(lo, j, k0 + k))
                b = (xs[0][:, k, :], xs[1][:, k, :])
                pe.matmul(bank[:, at:at + T], a[0], b[0], start=start and k == 0, stop=False)
                pe.matmul(bank[:, at:at + T], a[0], b[1], start=False, stop=False)
                ins = pe.matmul(bank[:, at:at + T], a[1], b[0], start=False, stop=stop and k == kt - 1)
            return ins

        def first_half(j, bank, wv):
            for k in range(KD):
                pe.wait_ge(xh_ready, 8 * wv + k + 1)
                pe.matmul(bank[:, 0:T], w_part(hi, j, k), xh[:, k, :], start=k == 0, stop=False)
                pe.matmul(bank[:, 0:T], w_part(lo, j, k), xh[:, k, :], start=False, stop=False)
            for k in range(KD):
                pe.wait_ge(xl_ready, 8 * wv + k + 1)
                ins = pe.matmul(bank[:, 0:T], w_part(hi, j, k), xl[:, k, :], start=False, stop=k == KD - 1)
            return ins

        def sums(wv):
            pe.wait_ge(acc_ready, 8 * wv)
            for e in range(2 if wv == 3 else 1):
                ins = token_sum(ps[7], e * TT, e)
            ins.then_inc(sums_ready, 1)

        def token_sum(bank, at, e):
            for t in range(TT):
                ins = pe.matmul(bank[:, at + t:at + t + 1], acc[:, e, t * P:(t + 1) * P], ones[:, 0:1],
                                start=True, stop=True)
            return ins

        def row(name, bank, *cols):
            pe.wait_ge(r_ready, ROOTS[name] + 1)
            for i, c in enumerate(cols):
                for t in range(TT):
                    ins = pe.matmul(bank[:, i * T + t * P:i * T + (t + 1) * P],
                                    rcol[:, c + t:c + t + 1].to_broadcast([P, P]), ident, start=True, stop=True)
            ins.then_inc(row_spread, 1)

        def x_row(wv):
            row(f"x{wv}", ps[6], 0, *([TT] if wv == 3 else []))

        def ffn(f, wv):
            J, E = JF[f], EF[f]

            def up_half(q, ready, free=None, first=None):
                pe.wait_ge(split_lo, ready)
                if free is not None:
                    pe.wait_ge(up_scaled, free)
                if first is not None:
                    first_half(J + q, ps[q % 8], first).then_inc(half_done, 1)
                else:
                    feature_half(J + q, ps[q % 8], 0, KD, (xh, xl)).then_inc(half_done, 1)

            for q in range(4):
                up_half(q, J + q + 1, first=wv if q == 0 else None)
                if q == 0 and f:
                    sums(wv)
                if q == 1:
                    if f == 0:
                        pe.wait_ge(x_updated, 8)
                    x_row(wv)
                if q == 2 and f == 0:
                    pe.wait_ge(vec_in, 16 * (len(VEC) - 1))
                    pe.transpose(ps[7][:, 0:NVEC], vrow[:, :], ident[0:NVEC, 0:NVEC]).then_inc(vec_turned, 1)
            if f == 0:
                pe.wait_ge(vec_ready, 2)
            pe.wait_ge(x_updated, 8 * (wv + 1))
            pe.wait_ge(row_ready, ROWS[f"x{wv}"] + 1)
            for q in range(4, 12):
                up_half(q, J + q + 1, free=E + q // 2 - 3 if q >= 8 else None)
            with pe.Fori(0, 4) as i:
                for q in range(12, 20):
                    up_half(q, i * 8 + (J + q + 1), free=i * 4 + (E + q // 2 - 3))
            pe.wait_ge(up_scaled, E + NF - 2)
            with pe.Fori(0, 4) as i:
                for q in range(8):
                    k0, k1 = DOWN_K[q % 4]
                    m = q // 4
                    j = J + FFN_UP + q
                    pe.wait_ge(split_lo, i * 8 + (j + 1))
                    pe.wait_ge(hidden_lo, E + k1)
                    if q % 4 == 0:
                        pe.wait_ge(x_updated, i * 2 + (8 * (wv + 1) + m - 1))
                    feature_half(j, ps[4 + m], 0, k1 - k0, (hh[:, k0:k1, :], hl[:, k0:k1, :]),
                                 start=q % 4 == 0, stop=q % 4 == 3).then_inc(half_done, 1)

        def scores(s, q, k, rope=None):
            if s >= 2:
                pe.wait_ge(seg_biased, s - 1)
            b = ps[4 + s % 2]
            for a, c0, w_ in ((0, 0, P), (P, P, 2 * P)):
                ins = pe.matmul(b[:, c0:c0 + w_], q[:, a:a + P], k[:, 0:w_], start=True, stop=rope is None)
                if rope is not None:
                    ins = pe.matmul(b[:, c0:c0 + w_], rope[0][:, a:a + P], rope[1][:, 0:w_],
                                    start=False, stop=True)
            ins.then_inc(seg_scores, 1)

        def turn(s, k, probs):
            pe.wait_ge(seg_norm, 2 * (k + 1))
            if s >= 2:
                pe.wait_ge(seg_copied, s - 1)
            for c in range(3):
                ins = pe.transpose(ps[6 + s % 2][:, c * P:(c + 1) * P], probs[:, c * P:(c + 1) * P], ident)
            ins.then_inc(seg_turned, 1)

        def weighted(s, k, first, last, v, pt):
            pe.wait_ge(seg_copied, s + 1)
            if first and k >= 2:
                pe.wait_ge(y_lo, k - 1)
            rows = slice(HD * (k % 2), HD * (k % 2) + HD)
            pe.matmul(ps[3][rows, 0:T], v[0], pt[:, 0:T], start=first, stop=False)
            ins = pe.matmul(ps[3][rows, P:T], v[1], pt[:, T:T + P], start=False, stop=last)
            if last:
                ins.then_inc(seg_out, 1)

        def mixing_half(part, n, j):
            pe.wait_ge(split_lo, j + 1)
            if n >= 3:
                pe.wait_ge(*taken(part, n - 3))

        def token_pair(n, j, kt, xs):
            for t in range(TT):
                bank = ps[(n - 1 + t) % 3][:, 0:T].rearrange("p (a c) -> p a c", c=P)
                for k in range(kt):
                    a = (xs[0][:, k, t * P:(t + 1) * P], xs[1][:, k, t * P:(t + 1) * P])
                    b = (w_pair(hi, j - 1, k), w_pair(lo, j - 1, k))
                    pe.matmul(bank, a[0], b[0], start=k == 0, stop=False)
                    pe.matmul(bank, a[0], b[1], start=False, stop=False)
                    ins = pe.matmul(bank, a[1], b[0], start=False, stop=k == kt - 1)
            ins.then_inc(half_done, 2)

        def head_rows(h):
            return slice(HD * (h % 2), HD * (h % 2) + HD)

        pe.wait_ge(ident_in, 16)
        pe.wait_ge(gain_in, 16)
        pe.transpose(ps[0][:, 0:KD], vrow[0:KD, :], ident[0:KD, 0:KD]).then_inc(vec_turned, 1)
        pe.wait_ge(x_landed, 16)
        for m in range(KD):
            for t in range(TT):
                a = (m % 2) * T + t * P
                ins = pe.transpose(ps[4 + m // 2][:, a:a + P], x_in[:, t, m * P:(m + 1) * P], ident)
            if m % 2:
                ins.then_inc(x_turned, 2)
        pe.wait_ge(vec_ready, 1)
        ffn(0, 0)

        for n in range(M1["end"]):
            j = J0[1] + n
            if n in M1_TOKEN:
                mixing_half(1, n, j)
            elif n - 1 in M1_TOKEN:
                mixing_half(1, n, j)
                token_pair(n, j, KD, (xh, xl))
            elif n < M1["merge"]:
                mixing_half(1, n, j)
                if n == 0:
                    first_half(j, ps[n % 3], 1).then_inc(half_done, 1)
                else:
                    feature_half(j, ps[n % 3], 0, KD, (xh, xl)).then_inc(half_done, 1)
            elif n < M1["out"]:
                mixing_half(1, n, j)
                if n == M1["merge"]:
                    pe.wait_ge(y_lo, 12)
                feature_half(j, ps[n % 3], 0, 2, (y1h[:, 0:2, :], y1l[:, 0:2, :]))
                feature_half(j, ps[n % 3], 2, 4, (y1h[:, 2:6, :], y1l[:, 2:6, :]), at=T).then_inc(half_done, 1)
            else:
                m = n - M1["out"]
                pe.wait_ge(split_lo, j + 1)
                if m >= 2:
                    pe.wait_ge(x_updated, 8 * 2 + m - 1)
                feature_half(j, ps[4 + m % 2], 0, KD, (mh1, ml1),
                             each=(lambda k: pe.wait_ge(merged_lo, k + 1)) if m == 0 else None
                             ).then_inc(half_done, 1)
            if n == 0:
                sums(1)
            if n == 1:
                x_row(1)
            for s in range(NSEG1):
                k = s // 3 if s < N_DSA else 4 + s - N_DSA
                head = 4 * (s % 3) + k if s < N_DSA else s - N_DSA
                if n == TURN1[s] + OUT_LAG:
                    pe.wait_ge(*taken(1, M1["qb"] - 1 if s < N_DSA else M1["gates"] - 1))
                    v = va if s < N_DSA else vb
                    weighted(s, k, s >= N_DSA or s % 3 == 0, s >= N_DSA or s % 3 == 2,
                             [v[:, t, head * HD:(head + 1) * HD] for t in range(TT)], pt1[:, s % 2, :])
            for s in range(NSEG1):
                k = s // 3 if s < N_DSA else 4 + s - N_DSA
                head = 4 * (s % 3) + k if s < N_DSA else s - N_DSA
                if n == TURN1[s]:
                    if s < 2:
                        pe.wait_ge(row_ready, ROWS["x1"] + 1)
                    turn(s, k, probs1_of(s))
                if n == SCORES1[s]:
                    q, kk = (qa, ka) if s < N_DSA else (qb, kb)
                    pe.wait_ge(*taken(1, M1["va"] - 1 if s < N_DSA else M1["kb"] + head // 2))
                    scores(s, q[head_rows(head), head // 2, :], kk[head_rows(head), head // 2, :])
        ffn(1, 2)

        for n in range(M2["end"]):
            j = J0[3] + n
            if n in M2_TOKEN:
                mixing_half(3, n, j)
            elif n - 1 in M2_TOKEN:
                mixing_half(3, n, j)
                token_pair(n, j, KD if n < M2["uq"] else CKV // P, (xh, xl) if n < M2["uq"] else (ckvh, ckvl))
            elif M2["uq"] <= n < M2["ukv"]:
                mixing_half(3, n, j)
                pe.wait_ge(cx_lo, 5)
                feature_half(j, ps[n % 3], 0, CQ // P, (cqh, cql)).then_inc(half_done, 1)
            elif M2["ukv"] <= n < M2["uv"]:
                mixing_half(3, n, j)
                feature_half(j, ps[n % 3], 0, CKV // P, (ckvh, ckvl)).then_inc(half_done, 1)
            elif n < M2["merge"]:
                mixing_half(3, n, j)
                if n == 0:
                    first_half(j, ps[n % 3], 3).then_inc(half_done, 1)
                else:
                    feature_half(j, ps[n % 3], 0, KD, (xh, xl)).then_inc(half_done, 1)
            elif n < M2["out"]:
                mixing_half(3, n, j)
                if n == M2["merge"]:
                    pe.wait_ge(y_lo, 20)
                    pe.wait_ge(yb_lo, 4)
                feature_half(j, ps[n % 3], 0, 4, (y2ah, y2al))
                feature_half(j, ps[n % 3], 4, 4, (y2bh, y2bl), at=T).then_inc(half_done, 1)
            else:
                m = n - M2["out"]
                pe.wait_ge(split_lo, j + 1)
                if m >= 2:
                    pe.wait_ge(x_updated, 8 * 4 + m - 1)
                feature_half(j, ps[4 + m % 2], 0, KD, (mh2, ml2),
                             each=(lambda k: pe.wait_ge(merged_lo, KD + k + 1)) if m == 0 else None
                             ).then_inc(half_done, 1)
            if n == 0:
                sums(3)
            if n == 1:
                x_row(3)
            if n == Z_AT:
                pe.wait_ge(*taken(3, M2["lr"]))
                pe.wait_ge(small_in, 16)
                for c in range(2):
                    ins = pe.matmul(ps[4][:, c * T:(c + 1) * T], wg2[:, c * P:(c + 1) * P], lr[0:16, :],
                                    start=True, stop=True)
                ins.then_inc(decay_raw, 1)
            lv = n - LEVEL_AT
            if 0 <= lv < 9:
                b = 4 + 2 * (lv % 2)
                if lv >= 2:
                    pe.wait_ge(lv_taken, 2 * (lv - 1))
                elif lv == 0:
                    pe.wait_ge(decay_taken, 2)
                else:
                    pe.wait_ge(row_ready, ROWS["x3"] + 1)
                if lv < 8:
                    pe.wait_ge(lv_ready, 2 * (lv + 1))
                for t in range(TT) if lv else (0,):
                    j0, i0 = (t * P, t * P) if lv else (0, P)
                    for h in range(4):
                        r, c = head_rows(h), h // 2
                        kk = lvk[r, lv % 2, c, :] if lv < 8 else gk[r, c, :]
                        qq = lvq[r, lv % 2, c, :] if lv < 8 else gq[r, c, :]
                        a = (2 * t + c) * P
                        ins = pe.matmul(ps[b + h % 2][:, a:a + P], kk[:, j0:j0 + P], qq[:, i0:i0 + P],
                                        start=True, stop=True)
                ins.then_inc(lv_done, 1)
            if n == SUM_CKV_AT:
                pe.wait_ge(cx_acc, 2)
                token_sum(ps[3], T, 0).then_inc(sums_ready, 1)
            if n == SUM_CKV_AT + 1:
                row("ckv", ps[3], RCOL["ckv"])
            if n == SUM_CQ_AT:
                pe.wait_ge(cx_acc, 5)
                pe.wait_ge(row_ready, ROWS["ckv"] + 1)
                token_sum(ps[3], T, 1).then_inc(sums_ready, 1)
            if n == SUM_CQ_AT + 1:
                row("cq", ps[3], RCOL["cq"])
            if n == GLA_O_AT:
                pe.wait_ge(lv_taken, 18)
                pe.wait_ge(*taken(3, M2["uq"] - 1))
                for t in range(TT):
                    for h in range(4):
                        o = ps[4 + t][:, h * P:(h + 1) * P]
                        if t == 0:
                            ins = pe.matmul(o, at3[:, 0, h, :], gv[:, 0, h * P:(h + 1) * P], start=True, stop=True)
                        else:
                            pe.matmul(o, at3[:, 2, h, :], gv[:, 0, h * P:(h + 1) * P], start=True, stop=False)
                            ins = pe.matmul(o, at3[:, 1, h, :], gv[:, 1, h * P:(h + 1) * P], start=False, stop=True)
                ins.then_inc(gla_out, 1)
            if n == GLA_TURN_AT:
                pe.wait_ge(gla_scaled, 1)
                for h in range(4):
                    for t in range(TT):
                        a = (h % 2) * T + t * P
                        ins = pe.transpose(ps[4 + h // 2][:, a:a + P], go[:, t, h * P:(h + 1) * P], ident)
                ins.then_inc(gla_turned, 1)
            for s in range(NSEG2):
                if n == TURN2[s] + OUT_LAG:
                    pe.wait_ge(*taken(3, M2["gates"] - 1))
                    if s < 2:
                        pe.wait_ge(row_ready, ROWS["cq"] + 1)
                    weighted(NSEG1 + s, 12 + s, True, True,
                             [mv[:, t, s * HD:(s + 1) * HD] for t in range(TT)], pt2[:, s % 2, :])
            for s in range(NSEG2):
                if n == TURN2[s]:
                    turn(NSEG1 + s, 12 + s, p2[:, s % 3, :])
                if n == SCORES2[s]:
                    pe.wait_ge(*taken(3, M2["uv"] - 1))
                    if s == 0:
                        pe.wait_ge(gla_y, 4)
                    r = slice(32 * (s % 4), 32 * (s % 4) + 32)
                    scores(NSEG1 + s, qn[head_rows(s), s // 2, :], kn[head_rows(s), s // 2, :],
                           (qr[r, s // 4, :], kr[r, 0, :]))
        ffn(2, 4)

        sums(5)
        pe.wait_ge(fin_ready, KD)
        for g in range(8):
            t, c = divmod(g, 4)
            if g == 7:
                pe.wait_ge(fin_scaled, 1)
            for e in range(2):
                ins = pe.transpose(ps[FIN_BANK[g]][:, e * P:(e + 1) * P],
                                   o_fm[:, 2 * c + e, t * P:(t + 1) * P], ident)
            ins.then_inc(fin_turned, 1)

    block.__exit__(None, None, None)


_INS = ["x", "norm_ffn1", "ffn1_gate", "ffn1_up", "ffn1_down", "norm_mix", "w_in", "w_up_a", "w_up_b", "w_out",
        "norm_ffn2", "ffn2_gate", "ffn2_up", "ffn2_down", "norm_final", "positions_2", "ln_mix_2", "w_in_2",
        "mla_norm_cq_2", "mla_w_uq_2", "mla_norm_ckv_2", "mla_w_ukv_2", "mla_w_o_2", "gla_w_gate2_2",
        "gla_b_gate_2", "gla_norm_2", "gla_w_o_2", "w_out_2", "ln_ffn_2", "ffn_w_gate_2", "ffn_w_up_2",
        "ffn_w_down_2", "final_norm_2"]


def kernel(**inputs):
    import concourse.bacc as bacc
    from concourse.bass_utils import run_bass_kernel_spmd

    nc = bacc.Bacc("TRN2", target_bir_lowering=False, num_devices=1)
    arrays = {f"in_{n}": np.ascontiguousarray(inputs[n]) for n in _INS}
    arrays["in_consts"], arrays["in_masks"] = constants()
    w = {}
    for name, a in arrays.items():
        ap = nc.dram_tensor(name, a.shape, mybir.dt.from_np(a.dtype), kind="ExternalInput").ap()
        w[name[3:]] = ap[0] if len(a.shape) == 3 and name not in ("in_x", "in_gla_w_gate2_2") else ap
    out = nc.dram_tensor("out_0", (1, T, D), F32, kind="ExternalOutput").ap()
    build(nc, w, out[0])
    r = run_bass_kernel_spmd(nc, [arrays], core_ids=[0])
    return r.results[0]["out_0"]
```

```python
import math

import numpy as np
import concourse.bass as bass
from concourse import mybir

F32 = mybir.dt.float32
F32R = mybir.dt.float32r
I32 = mybir.dt.int32
ALU = mybir.AluOpType
ACT = mybir.ActivationFunctionType
AX = mybir.AxisListType

P = 128
BASE = 16384 + 128
T = 256
TT = T // P
D = 1024
KD = D // P
FF = 2816
NF = FF // P
EPS = 1e-6
HD = 64
GROUPS = ((128, 1), (512, 4), (2048, 16))
DSA_J = 4
DSA_W = 768
MOBA_W = 512
MLA_QK, MLA_NOPE, MLA_ROPE = 96, 64, 32
CQ, CKV = 384, 256
HEADS = 8
GLA_LEVELS = (128, 64, 32, 16, 8, 4, 2, 1)
GLA_CHUNK = 64
FAR = 1e33
RING = 4
RAW_W = 8 * 288
DOWN_K = ((0, 6), (6, 12), (12, 17), (17, 22))

QA, KA, VA = 0, DSA_W, 2 * DSA_W
QB = 3 * DSA_W
KB, VB = QB + MOBA_W, QB + 2 * MOBA_W
GA = QB + 3 * MOBA_W
C_KV = CQ
C_GQ = CQ + CKV + MLA_ROPE
C_GK, C_GV, C_LR = C_GQ + 256, C_GQ + 512, C_GQ + 1024
C_OG = C_LR + 16
C_GATES = C_OG + 512

VEC = {"norm_ffn1": 0, "norm_mix": 8, "norm_ffn2": 16, "norm_final": 24, "ln_mix_2": 32, "ln_ffn_2": 40,
       "final_norm_2": 48, "mla_norm_cq_2": 56, "mla_norm_ckv_2": 59, "gla_b_gate_2": 61, "gla_norm_2": 63}
NVEC = 64

C_IDENT, C_ONES, C_SEG, C_INV, C_SIGN = 0, 128, 256, 768 + 512, 768 + 513
C_DIST = C_SIGN + 1
NSEG = 384
N_CONST = C_DIST + 5 * NSEG


def constants():
    c = np.zeros((P, N_CONST), np.float32)
    c[:, C_IDENT:C_IDENT + P] = np.eye(P)
    c[:, C_ONES:C_ONES + P] = 1
    t = np.arange(2 * T)
    c[:, C_SEG:C_SEG + 2 * T] = t % GLA_CHUNK != 0
    c[:, C_SEG + 2 * T:C_SEG + 4 * T] = t % T != 0
    half = MLA_ROPE // 2
    inv = (np.float32(1.0) / (np.float32(10000.0) ** (np.arange(half, dtype=np.float32) / half))).astype(np.float32)
    p = np.arange(P)
    c[:, C_INV] = inv[p % half]
    c[:, C_SIGN] = np.where(p % MLA_ROPE < half, -1, 1)
    for g in range(5):
        for q0, k1, at in ((0, P, 0), (P, 2 * P, P)):
            d = (q0 + p[:, None]) - np.arange(k1)[None]
            ok = d >= 0
            if g < 3:
                window, dilation = GROUPS[g]
                ok &= (d <= window) & (d % dilation == 0)
            v = np.where(ok, d if g < 4 else 0, FAR)
            c[:, C_DIST + g * NSEG + at:C_DIST + g * NSEG + at + k1] = v
    m = np.zeros((P, 7, P), np.int32)
    j, i = p[:, None], p[None]
    for n, s in enumerate(GLA_LEVELS[2:]):
        m[:, n] = (j // (2 * s) == i // (2 * s)) & (j % (2 * s) < s) & (i % (2 * s) >= s)
    m[:, 6] = j == i
    return c, m.reshape(P, 7 * P)


class Half:

    def __init__(self, unit, kt, pieces):
        self.unit, self.kt, self.pieces = unit, kt, pieces

    def views(self, raw, part):
        return [(src(raw), dst(part[:, 0:self.kt * P].rearrange("p (k c) -> p k c", c=P)))
                for src, dst in self.pieces]


def plain(kt, width, c0):
    return [(lambda raw: raw[:, 0:kt * width].rearrange("p (k c) -> p k c", c=width)[:, :, c0:c0 + P],
             lambda part: part)]


def block2(kt, width, c0, stride, n, size):
    def src(raw):
        v = raw[:, 0:kt * width].rearrange("p (k g c) -> p k g c", k=kt, c=stride)
        return v[:, :, c0 // stride:c0 // stride + n, c0 % stride:c0 % stride + size]
    return [(src, lambda part: part.rearrange("p k (g c) -> p k g c", c=size))]


def swapped(kt, width, c0, stride, n):
    h = MLA_ROPE // 2
    out = []
    for e in range(2):
        def src(raw, e=e):
            v = raw[:, 0:kt * width].rearrange("p (k g c) -> p k g c", k=kt, c=stride)
            a = c0 % stride + (1 - e) * h
            return v[:, :, c0 // stride:c0 // stride + n, a:a + h]
        out.append((src, lambda part, e=e: part.rearrange("p k (g c) -> p k g c", c=MLA_ROPE)[
            :, :, :, e * h:e * h + h]))
    return out


def spread(width, c0, size, stride, at, n):
    def src(raw):
        v = raw[:, 0:KD * width].rearrange("p (k c) -> p k c", c=width)[:, :, c0:c0 + size]
        return v.unsqueeze(2).to_broadcast([P, KD, n, size])

    def dst(part):
        v = part.rearrange("p k (g c) -> p k g c", c=stride)
        return v[:, :, 0:n, at:at + size]
    return [(src, dst)]


def mix1_plan(w):
    units, halves = [], []
    w_in = w["w_in"].rearrange("(k p) c -> p k c", p=P)

    def cols(c0):
        units.append([(0, KD, 256, w_in[:, :, c0:c0 + 256])])
        for h in range(2):
            halves.append(Half(len(units) - 1, KD, plain(KD, 256, h * P)))
    for c0 in range(QA, GA + 2 * D, 256):
        cols(c0)
    ua = w["w_up_a"].rearrange("(k p) c -> p k c", p=P)
    ub = w["w_up_b"].rearrange("(k p) c -> p k c", p=P)
    for c0 in range(0, D, 256):
        units.append([(0, 2, 256, ua[:, :, c0:c0 + 256]), (2, 4, 256, ub[:, :, c0:c0 + 256])])
        for h in range(2):
            halves.append(Half(len(units) - 1, 6, plain(6, 256, h * P)))
    wo = w["w_out"].rearrange("(k p) c -> p k c", p=P)
    for c0 in range(0, D, 256):
        units.append([(0, KD, 256, wo[:, :, c0:c0 + 256])])
        for h in range(2):
            halves.append(Half(len(units) - 1, KD, plain(KD, 256, h * P)))
    return units, halves


M1 = dict(qa=0, ka=6, va=12, qb=18, kb=22, vb=26, gates=30, merge=46, out=54, end=62)
M1_TOKEN = (12, 14, 16, 26, 28)
M2 = dict(lr=0, og=1, gq=3, gk=5, og2=7, ckv=9, cq=11, gv=14, uq=18, uqr=22, ukv=26, uv=30,
          gates=34, merge=50, out=58, end=66)
M2_TOKEN = (14, 16, 30, 32)


def mix2_plan(w):
    units, halves = [], []
    w_in = w["w_in_2"].rearrange("(k p) c -> p k c", p=P)

    def unit(c0, width):
        units.append([(0, KD, width, w_in[:, :, c0:c0 + width])])
        return len(units) - 1

    def half(u, pieces, kt=KD):
        halves.append(Half(u, kt, pieces))

    units.append([(0, KD, 48, w_in[:, :, C_LR:C_LR + 16]), (0, KD, 48, w_in[:, :, C_KV + CKV:C_KV + CKV + 32], 16)])
    half(0, spread(48, 0, 16, 16, 0, 2) + spread(48, 16, 32, 64, 32, 2)
         + spread(48, 32, 16, P, 64, 1) + spread(48, 16, 16, P, 80, 1))
    for c0 in (C_OG, C_GQ, C_GK, C_OG + 256, C_KV):
        u = unit(c0, 256)
        for h in range(2):
            half(u, plain(KD, 256, h * P))
    u = unit(0, 256)
    for h in range(2):
        half(u, plain(KD, 256, h * P))
    half(unit(256, P), plain(KD, P, 0))
    for c0 in (C_GV, C_GV + 256):
        u = unit(c0, 256)
        for h in range(2):
            half(u, plain(KD, 256, h * P))
    kq, kk = CQ // P, CKV // P
    units.append([(0, kq, 768, w["mla_w_uq_2"].rearrange("(k p) c -> p k c", p=P))])
    u = len(units) - 1
    for c in range(4):
        half(u, block2(kq, 768, 2 * c * MLA_QK, MLA_QK, 2, MLA_NOPE), kq)
    for c in range(2):
        half(u, block2(kq, 768, 4 * c * MLA_QK + MLA_NOPE, MLA_QK, 4, MLA_ROPE), kq)
    for c in range(2):
        half(u, swapped(kq, 768, 4 * c * MLA_QK + MLA_NOPE, MLA_QK, 4), kq)
    units.append([(0, kk, 1024, w["mla_w_ukv_2"].rearrange("(k p) c -> p k c", p=P))])
    u = len(units) - 1
    for part in (0, MLA_NOPE):
        for c in range(4):
            half(u, block2(kk, 1024, 2 * c * P + part, P, 2, HD), kk)
    for c0 in range(C_GATES, C_GATES + 2 * D, 256):
        u = unit(c0, 256)
        for h in range(2):
            half(u, plain(KD, 256, h * P))
    oa = w["mla_w_o_2"].rearrange("(k p) c -> p k c", p=P)
    ob = w["gla_w_o_2"].rearrange("(k p) c -> p k c", p=P)
    for c0 in range(0, D, 256):
        units.append([(0, 4, 256, oa[:, :, c0:c0 + 256]), (4, 4, 256, ob[:, :, c0:c0 + 256])])
        for h in range(2):
            half(len(units) - 1, plain(8, 256, h * P), 8)
    wo = w["w_out_2"].rearrange("(k p) c -> p k c", p=P)
    for c0 in range(0, D, 256):
        units.append([(0, KD, 256, wo[:, :, c0:c0 + 256])])
        for h in range(2):
            half(len(units) - 1, plain(KD, 256, h * P))
    return units, halves


FFN_HALVES, FFN_UNITS = 4 * (NF // 2) + 4 * KD, NF + 4 * KD
FFN_UP = 4 * (NF // 2)
N_HALVES = (FFN_HALVES, M1["end"], FFN_HALVES, M2["end"], FFN_HALVES)
N_UNITS = (FFN_UNITS, 31, FFN_UNITS, 28, FFN_UNITS)
J0 = [sum(N_HALVES[:i]) for i in range(6)]
U0 = [sum(N_UNITS[:i]) for i in range(6)]

ROOTS = {n: i for i, n in enumerate(["x0", "x1", "x2", "x3", "latent", "gla", "x4", "x5"])}
SUMS = {n: i for i, n in enumerate(["x1", "x2", "x3", "latent", "x4", "x5"])}
ROWS = {n: i for i, n in enumerate(["x0", "x1", "x2", "x3", "latent", "x4"])}
RCOL = {"ckv": 4, "cq": 6}

NSEG1, NSEG2 = 20, 8
N_DSA = 12
SCORES1 = [13, 13, 15, 15, 17, 17, 18, 19, 20, 21, 22, 23, 24, 25, 27, 29, 30, 32, 33, 35]
TURN1 = [18, 18, 19, 20, 21, 22, 23, 24, 25, 27, 27, 29, 29, 30, 31, 32, 34, 35, 37, 38]
SCORES2 = [34, 35, 36, 38, 39, 41, 42, 43]
TURN2 = [37, 38, 39, 41, 42, 44, 45, 46]
OUT_LAG = 2
Z_AT, LEVEL_AT, GLA_O_AT, GLA_TURN_AT = 2, 9, 20, 28
LATENT_AT = 15
OG_HALVES = (1, 2, 7, 8)


def alibi(n, of):
    return 2.0 ** (-8.0 * (n + 1) / of)


def build(nc, w, out):
    units1, halves1 = mix1_plan(w)
    units2, halves2 = mix2_plan(w)
    assert len(units1) == N_UNITS[1] and len(halves1) == M1["end"]
    assert len(units2) == N_UNITS[3] and len(halves2) == M2["end"]

    top = [BASE]

    def place(name, shape, dt=F32, at=None):
        words = int(np.prod(shape[1:]))
        if at is None:
            at = top[0]
            top[0] += 4 * words
            top[0] += -top[0] % 32
        return nc.alloc_sbuf_tensor_at(name, list(shape), dt, offset=at)

    raw = place("raw", [P, RING, RAW_W])
    hi = place("hi", [P, RING, 8 * P], F32R)
    lo = place("lo", [P, RING, 8 * P], F32R)
    x = place("x", [P, KD, T])
    x_parts_at = top[0]
    xh = place("xh", [P, KD, T], F32R)
    xl = place("xl", [P, KD, T], F32R)
    cst = place("cst", [P, C_DIST])
    dist_at = top[0]
    dist = place("dist", [P, 5, NSEG])
    masks = place("masks", [P, 7, P], I32)
    vec = place("vec", [P, NVEC])
    vec2 = place("vec2", [P, 16])
    cosT = place("cosT", [P, T], at=dist_at)
    sinT = place("sinT", [P, T], at=dist_at + 1024)
    rope_q = place("rope_q", [P, 2, T], at=dist_at + 2048)
    rope_k = place("rope_k", [P, 2, T], at=dist_at + 4096)
    acc = place("acc", [P, 2, T])
    sq = place("sq", [P, 2, T])
    R = place("R", [P, T])
    R1 = place("R1", [P, T])
    Rq = place("Rq", [P, T])
    pos_i = place("pos_i", [P, T], I32, at=top[0])
    Rkv = place("Rkv", [P, T])
    var = place("var", [P, 2 * TT])
    root = place("root", [P, 2 * TT])
    newton = place("newton", [P, 2 * TT])
    rcol = place("rcol", [P, 4 * TT])
    x_sum = place("x_sum", [P, TT])
    scrap = place("scrap", [P, 8])
    tg = place("tg", [P, 2, T])
    tu = place("tu", [P, 2, T])
    sg = place("sg", [P, 2, T])
    hf = place("hf", [P, 2, T])
    region = top[0]
    hh = place("hh", [P, NF, T], F32R, at=region)
    hl = place("hl", [P, NF, T], F32R, at=region + 4 * NF * T)
    K = 1024
    x_in = place("x_in", [P, TT, D], at=region)
    vrow = place("vrow", [NVEC, P], at=region + 8 * K)
    x_sq = place("x_sq", [P, TT, D], at=region + 9 * K)
    qa = place("qa", [P, 6, T], at=region)
    ka = place("ka", [P, 6, T], at=region + 6 * K)
    va = place("va", [P, TT, DSA_W], at=region + 12 * K)
    gates1 = place("gates1", [P, 16, T], at=region)
    qb = place("qb", [P, 4, T], at=region + 18 * K)
    kb = place("kb", [P, 4, T], at=region + 22 * K)
    vb = place("vb", [P, TT, MOBA_W], at=region + 26 * K)
    mh1 = place("mh1", [P, KD, T], F32R, at=region + 18 * K)
    ml1 = place("ml1", [P, KD, T], F32R, at=region + 26 * K)
    p1 = place("p1", [P, 9, NSEG], at=region + 34 * K)
    pt1 = place("pt1", [P, 3, NSEG], at=region + 34 * K + 4 * 9 * NSEG)
    y1h = place("y1h", [P, 6, T], F32R, at=region + 52 * K)
    y1l = place("y1l", [P, 6, T], F32R, at=region + 58 * K)
    end1 = region + 64 * K
    ckv = place("ckv", [P, 2, T], at=region)
    ckvh = place("ckvh", [P, 2, T], F32R, at=region + 2 * K)
    ckvl = place("ckvl", [P, 2, T], F32R, at=region + 4 * K)
    cq = place("cq", [P, 3, T], at=region + 6 * K)
    cqh = place("cqh", [P, 3, T], F32R, at=region + 9 * K)
    cql = place("cql", [P, 3, T], F32R, at=region + 12 * K)
    gates2 = place("gates2", [P, 16, T], at=region)
    qn = place("qn", [P, 4, T], at=region + 16 * K)
    kn = place("kn", [P, 4, T], at=region + 20 * K)
    mv = place("mv", [P, TT, 512], at=region + 24 * K)
    qr = place("qr", [P, 2, T], at=region + 28 * K)
    kr = place("kr", [P, 1, T], at=region + 30 * K)
    mh2 = place("mh2", [P, KD, T], F32R, at=region + 16 * K)
    ml2 = place("ml2", [P, KD, T], F32R, at=region + 24 * K)
    gq = place("gq", [P, 2, T], at=region + 32 * K)
    gk = place("gk", [P, 2, T], at=region + 34 * K)
    run_chunk = place("run_chunk", [P, 2, T], at=region + 36 * K)
    run_all = place("run_all", [P, 2, T], at=region + 38 * K)
    p2 = place("p2", [P, 5, NSEG], at=region + 32 * K)
    pt2 = place("pt2", [P, 2, NSEG], at=dist_at + 2048)
    gv = place("gv", [P, TT, 512], at=region + 40 * K)
    lvq = place("lvq", [P, 2, 2, T], at=region + 44 * K)
    lvk = place("lvk", [P, 2, 2, T], at=region + 48 * K)
    y2ah = place("y2ah", [P, 4, T], F32R, at=region + 44 * K)
    y2al = place("y2al", [P, 4, T], F32R, at=region + 48 * K)
    at3 = place("at3", [P, 3, 4, P], at=region + 52 * K)
    osq = place("osq", [P, TT, 512], at=region + 44 * K)
    go_y = place("go_y", [P, 4, T], at=region + 52 * K)
    lr = place("lr", [16, T], at=region + 58 * K)
    wg2 = place("wg2", [16, 256], at=region + 59 * K)
    og = place("og", [P, 4, T], at=region + 60 * K)
    y2bh = place("y2bh", [P, 4, T], F32R, at=region + 56 * K)
    y2bl = place("y2bl", [P, 4, T], F32R, at=region + 40 * K)
    go = place("go", [P, TT, 512], at=region + 36 * K)
    zl = place("zl", [P, 2, T], at=region + 52 * K)
    ze = place("ze", [P, 2, T], at=region + 54 * K)
    end2 = region + 64 * K
    top[0] = max(end1, end2, region + 8 * NF * T)
    nmax = place("nmax", [P, 8])
    ssum = place("ssum", [P, 8])
    sinv = place("sinv", [P, 8])
    gss = place("gss", [P, 5, 8])
    assert top[0] <= 207 * K, top[0]
    o_fm = place("o_fm", [P, KD, T], at=x_parts_at)
    o_tm = place("o_tm", [P, TT, D], at=x_parts_at + 8 * K)
    lvd, lve = hf, sg
    ps = [nc.alloc_psum_tensor(f"bank{i}", [P, 512], F32) for i in range(8)]

    ident = cst[:, C_IDENT:C_IDENT + P]
    ones = cst[:, C_ONES:C_ONES + P]

    def sem(name):
        return nc.alloc_semaphore(name)

    raw_landed = [sem(f"raw_landed{i}") for i in range(RING)]
    ident_in, gain_in, vec_in, const_in, small_in, pos_in = (
        sem(n) for n in ("ident_in", "gain_in", "vec_in", "const_in", "small_in", "pos_in"))
    first_landed = [sem(f"first_landed{j}") for j in range(2)]
    x_landed = [sem(f"x_landed{t}") for t in range(TT)]
    split_hi, split_lo, half_done = sem("split_hi"), sem("split_lo"), sem("half_done")
    vec_turned, vec_ready, x_turned = sem("vec_turned"), sem("vec_ready"), sem("x_turned")
    x_updated, xh_ready, xl_ready, acc_ready = (
        sem(n) for n in ("x_updated", "xh_ready", "xl_ready", "acc_ready"))
    sums_ready, var_ready, root_ready, r_ready = (
        sem(n) for n in ("sums_ready", "var_ready", "root_ready", "r_ready"))
    token_sums, row_spread, row_ready = sem("token_sums"), sem("row_spread"), sem("row_ready")
    gate_scaled, up_scaled, silu_ready, hidden_ready, hidden_hi, hidden_lo = (
        sem(n) for n in ("gate_scaled", "up_scaled", "silu_ready", "hidden_ready", "hidden_hi", "hidden_lo"))
    half_taken = sem("half_taken")
    z_ready, tanh_ready, sig_ready = sem("z_ready"), sem("tanh_ready"), sem("sig_ready")
    cx_ready, cx_hi, cx_lo, cx_acc = sem("cx_ready"), sem("cx_hi"), sem("cx_lo"), sem("cx_acc")
    merge_ab, merged, merged_hi, merged_lo = sem("merge_ab"), sem("merged"), sem("merged_hi"), sem("merged_lo")
    seg_scores, seg_biased, seg_max, seg_probs = (
        sem(n) for n in ("seg_scores", "seg_biased", "seg_max", "seg_probs"))
    seg_inv, seg_norm, seg_turned, seg_copied, seg_out, y_hi, y_lo = (
        sem(n) for n in ("seg_inv", "seg_norm", "seg_turned", "seg_copied", "seg_out", "y_hi", "y_lo"))
    single_norm = sem("single_norm")
    decay_raw, decay_taken, decay_logs = sem("decay_raw"), sem("decay_taken"), sem("decay_logs")
    lv_zero, lv_diff, lv_exp, lv_ready, lv_done, lv_taken = (
        sem(n) for n in ("lv_zero", "lv_diff", "lv_exp", "lv_ready", "lv_done", "lv_taken"))
    gla_out, gla_copied, gla_sums, gla_scaled, gla_turned, gla_y, yb_hi, yb_lo = (
        sem(n) for n in ("gla_out", "gla_copied", "gla_sums", "gla_scaled", "gla_turned", "gla_y", "yb_hi", "yb_lo"))
    residual_scaled = sem("residual_scaled")
    sin_arg, sin_ready = sem("sin_arg"), sem("sin_ready")
    fin_ready, fin_turned, out_stored = sem("fin_ready"), sem("fin_turned"), sem("out_stored")
    fin_scaled = [sem(f"fin_scaled{t}") for t in range(TT)]
    dve_step, act_step, pool_step = sem("dve_step"), sem("act_step"), sem("pool_step")

    W_UP = (("ffn1_gate", "ffn1_up", "ffn1_down"), ("ffn2_gate", "ffn2_up", "ffn2_down"),
            ("ffn_w_gate_2", "ffn_w_up_2", "ffn_w_down_2"))
    JF, UF, EF = [J0[0], J0[2], J0[4]], [U0[0], U0[2], U0[4]], [0, NF, 2 * NF]
    GAIN = [vec[:, VEC["norm_ffn1"]:], vec[:, VEC["norm_mix"]:], vec[:, VEC["norm_ffn2"]:], vec2[:, 0:8],
            vec[:, VEC["ln_ffn_2"]:], vec[:, VEC["final_norm_2"]:]]

    def part_of(j):
        n = max(i for i in range(5) if J0[i] <= j)
        return n, j - J0[n]

    def ffn_half(q):
        if q < FFN_UP:
            i, r = divmod(q, 4)
            return 2 * i + r % 2, KD, (r // 2) * P, 256
        k0, k1 = DOWN_K[(q - FFN_UP) % 4]
        return NF + q - FFN_UP, k1 - k0, 0, P

    def half_views(j, part):
        n, q = part_of(j)
        slot = part[:, j % RING, :]
        if n % 2 == 0:
            u, kt, c0, width = ffn_half(q)
            h = Half(u, kt, plain(kt, width, c0))
        else:
            h = (halves1, halves2)[n // 2][q]
        u = U0[n] + h.unit
        return h.views(raw[:, u % RING, :], slot), u

    def last_half(u):
        n = max(i for i in range(5) if U0[i] <= u)
        v = u - U0[n]
        if n % 2 == 0:
            q = 4 * (v // 2) + 2 + v % 2 if v < NF else FFN_UP + v - NF
        else:
            q = max(i for i, h in enumerate((halves1, halves2)[n // 2]) if h.unit == v)
        return J0[n] + q

    def w_part(part, j, k):
        return part[:, j % RING, k * P:(k + 1) * P]

    def w_pair(part, j, k):
        s = j % RING
        return part[:, s:s + 2, k * P:(k + 1) * P]

    def last_segment(k):
        return 3 * k + 2 if k < 4 else N_DSA + k - 4

    def level_scores(lv, e):
        bank = ps[4 + 2 * (lv % 2) + e]
        if lv == 0:
            return bank[:, 0:T].rearrange("p (h c) -> p h c", c=P)
        return bank[:, :].rearrange("p (t h c) -> p t h c", h=2, c=P)

    def ahead(n, pairs):
        return [] if n in pairs else [n + 3, n + 4] if n - 1 in pairs else [n + 4]

    def norm_step(k):
        n = SCORES1[last_segment(k)] + 1
        return n if n in M1_TOKEN else n + 1

    def normalised(k):
        return (seg_norm, 2 * (k + 1)) if k < DSA_J else (single_norm, 2 * (k - DSA_J + 1))

    def probs1(k):
        s = last_segment(k)
        return p1[:, s % 9 - 2:s % 9 + 1, :] if k < 4 else p1[:, s % 9:s % 9 + 1, :]

    def taken(part, n):
        first = M1 if part == 1 else M2
        if n >= first["merge"]:
            return merge_ab, 2 * ((0 if part == 1 else KD) + n - first["merge"] + 1)
        if n >= first["gates"]:
            return z_ready, (0 if part == 1 else 20) + n - first["gates"] + 1
        if part == 1:
            return half_taken, n + 1
        if n in OG_HALVES:
            return z_ready, 16 + OG_HALVES.index(n) + 1
        if M2["ckv"] <= n < M2["gv"]:
            return cx_ready, n - M2["ckv"] + 1
        other = len([i for i in range(n) if i in OG_HALVES or M2["ckv"] <= i < M2["gv"]])
        return half_taken, M1["gates"] + n - other + 1

    block = nc.Block()
    block_ctx = block.__enter__()

    @block_ctx.sync
    def _(sp):
        def load(u, pieces, landed=None, freed=None):
            if u >= RING or freed is not None:
                sp.wait_ge(split_lo, last_half(u - RING) + 1 if freed is None else freed)
            for k0, kt, width, src, *c0 in pieces:
                dst = raw[:, u % RING, k0 * width:(k0 + kt) * width].rearrange("p (k c) -> p k c", c=width)
                if c0:
                    dst = dst[:, :, c0[0]:]
                sp.dma_start(dst[:, :, 0:src.shape[-1]], src).then_inc(landed or raw_landed[u % RING], 16)

        def ffn(f):
            gate, up, down = (w[n] for n in W_UP[f])
            gate = gate.rearrange("(k p) c -> p k c", p=P)
            up = up.rearrange("(k p) c -> p k c", p=P)
            down = down.rearrange("(k p) c -> p k c", p=P)

            def pair(i, at, freed=None):
                for r, src in enumerate((gate, up)):
                    load(UF[f] + 2 * at + r, [(0, KD, 256, src[:, :, bass.ds(i * 256, 256)])],
                         freed=None if freed is None else freed + r)
            for i in range(3):
                if i == 0 and f == 0:
                    for c in (0, P):
                        for u, src in enumerate((gate, up)):
                            load(u, [(0, KD, 256, src[:, :, c:c + P], c)], None if c else first_landed[u])
                    continue
                if i == 2 and f == 0:
                    for name, at in VEC.items():
                        if at:
                            vector(name, vec_in)
                pair(i, i)
            with sp.Fori(0, (NF // 2 - 3) // 2) as i:
                for b in range(2):
                    pair(i * 2 + (3 + b), 3 + b, freed=i * 8 + (JF[f] + 4 * (1 + b) + 3))
            for q in range(4 * KD):
                k0, k1 = DOWN_K[q % 4]
                m = q // 4
                load(UF[f] + NF + q, [(0, k1 - k0, P, down[:, k0:k1, m * P:(m + 1) * P])])

        def mixing(n, units):
            for v, pieces in enumerate(units):
                load(U0[n] + v, pieces)

        def constant(dst, c0, c1):
            sp.dma_start(dst, w["consts"][:, c0:c1]).then_inc(const_in, 16)

        def vector(name, landed):
            n, at = w[name].shape[-1] // P, VEC[name]
            src = w[name] if len(w[name].shape) == 1 else w[name][0]
            sp.dma_start(vrow[at:at + n, :], src.rearrange("(a b) -> a b", b=P)).then_inc(landed, 16)

        sp.dma_start(cst[:, 0:C_SEG], w["consts"][:, 0:C_SEG]).then_inc(ident_in, 16)
        for t in range(TT):
            sp.dma_start(x_in[:, t, :], w["x"][0, t * P:(t + 1) * P, :]).then_inc(x_landed[t], 16)
        ffn(0)
        constant(dist[:, :, :].rearrange("p g c -> p (g c)"), C_DIST, N_CONST)
        mixing(1, units1)
        constant(cst[:, C_SEG:], C_SEG, C_DIST)
        sp.dma_start(masks[:, :, :].rearrange("p g c -> p (g c)"), w["masks"]).then_inc(const_in, 16)
        ffn(1)
        mixing(3, units2)
        ffn(2)
        for c in range(2):
            for t in range(TT):
                sp.wait_ge(fin_scaled[t], c + 1)
                sp.dma_start(out[t * P:(t + 1) * P, c * 512:(c + 1) * 512],
                             o_tm[:, t, c * 512:(c + 1) * 512]).then_inc(out_stored, 16)
        sp.wait_ge(out_stored, 16 * 2 * TT)

    def landed(eng, u, j):
        eng.wait_ge(*((first_landed[j], 16) if j < 2 else (raw_landed[u % RING], LANDED[u])))

    LANDED = {}
    count = [0] * RING
    for u in range(U0[5]):
        n = max(i for i in range(5) if U0[i] <= u)
        pieces = 1 if n % 2 == 0 else len((units1, units2)[n // 2][u - U0[n]])
        count[u % RING] += 16 * pieces
        LANDED[u] = count[u % RING]

    @block_ctx.scalar
    def _(act):
        steps = [0]

        def link(ins):
            steps[0] += 1
            ins.then_inc(act_step, 1)
            act.wait_ge(act_step, steps[0])

        def warm(func):
            link(act.activation(scrap[:, 0:1], ones[:, 0:1], func))

        def split(j):
            views, u = half_views(j, hi)
            landed(act, u, j)
            if j >= RING:
                act.wait_ge(half_done, j - RING + 1)
            for n, (src, dst) in enumerate(views):
                ins = act.activation(dst, src, ACT.Copy)
                if n == len(views) - 1:
                    ins.then_inc(split_hi, 1)

        def x_parts(wv):
            def tile(m):
                act.wait_ge(x_updated, 8 * wv + m + 1)
                act.activation(xh[:, m, :], x[:, m, :], ACT.Copy, scale=GAIN[wv][:, m:m + 1]).then_inc(xh_ready, 1)
            return tile

        def square_root(name, src=var[:, 0:TT], dst=root[:, 0:TT]):
            act.wait_ge(var_ready, ROOTS[name] + 1)
            act.activation(dst, src, ACT.Sqrt).then_inc(root_ready, 1)

        def ffn(f):
            J, E = JF[f], EF[f]

            def pair(e, b, ft):
                act.wait_ge(gate_scaled, e + 1)
                act.activation(sg[:, b, :], tg[:, b, :], ACT.Silu).then_inc(silu_ready, 1)

                def after():
                    act.wait_ge(hidden_ready, e + 1)
                    act.activation(hh[:, ft, :] if isinstance(ft, int) else hh[:, bass.ds(ft, 1), :],
                                   hf[:, b, :], ACT.Copy).then_inc(hidden_hi, 1)
                return after

            def split_in_loop(i, q):
                j = J + q
                views, u = half_views(j, hi)
                act.wait_ge(raw_landed[u % RING], i * 16 + LANDED[u])
                act.wait_ge(half_done, i * 8 + (j - RING + 1))
                for src, dst in views:
                    act.activation(dst, src, ACT.Copy).then_inc(split_hi, 1)

            def run(q0, n):
                for q in range(q0, q0 + n):
                    after = pair(E + q // 2, (q // 2) % 2, q // 2) if q % 2 else None
                    split(J + q + 4)
                    if after:
                        after()

            if f:
                square_root(f"x{2 * f}")
            warm(ACT.Silu)
            run(0, 4)
            with act.Fori(0, 4) as i:
                for q in range(4, 12):
                    after = pair(i * 4 + (E + q // 2), (q // 2) % 2, i * 4 + q // 2) if q % 2 else None
                    split_in_loop(i, q + 4)
                    if after:
                        after()
            run(36, 8)

        def down(f, tile, extra=None):
            J = JF[f]
            for q in range(FFN_UP, FFN_HALVES):
                if q == FFN_HALVES - 1:
                    tile(KD - 1)
                if J + q + 4 < J0[5]:
                    split(J + q + 4)
                if q % 4 == 3 and q < FFN_HALVES - 1:
                    tile((q - FFN_UP) // 4)
                if q == FFN_HALVES - 8:
                    warm(ACT.Sqrt)
                if extra is not None and q in extra:
                    extra[q]()

        def exp(k, probs):
            for t, (a, b) in enumerate(((0, P), (P, NSEG))):
                c = 2 * (k % 4) + t
                act.wait_ge(seg_max, 2 * k + t + 1)
                act.activation(probs[:, :, a:b], probs[:, :, a:b], ACT.Exp, bias=nmax[:, c:c + 1],
                               accum_out=ssum[:, c:c + 1]).then_inc(seg_probs, 1)

        def normalize(k, probs):
            for t, (a, b) in enumerate(((0, P), (P, NSEG))):
                c = 2 * (k % 4) + t
                act.wait_ge(seg_inv, 2 * k + t + 1)
                act.activation(probs[:, :, a:b], probs[:, :, a:b], ACT.Copy,
                               scale=sinv[:, c:c + 1]).then_inc(seg_norm, 1)

        def copy_turned(s, dst):
            act.wait_ge(seg_turned, s + 1)
            act.activation(dst, ps[6 + s % 2][:, 0:NSEG], ACT.Copy).then_inc(seg_copied, 1)

        def y_high(g, dst, rows):
            act.wait_ge(seg_out, g + 1)
            act.activation(dst[rows], ps[3][rows, 0:T], ACT.Copy).then_inc(y_hi, 1)

        def tanh_half(i):
            act.wait_ge(z_ready, i + 1)
            act.activation(tg[:, i % 2, :], tu[:, i % 2, :], ACT.Tanh, scale=0.5).then_inc(tanh_ready, 1)

        def merge_high(i, dst, m):
            act.wait_ge(merged, i + 1)
            act.activation(dst[:, m, :], hf[:, m % 2, :], ACT.Copy).then_inc(merged_hi, 1)

        act.dma_start(vrow[0:KD, :], w["norm_ffn1"][0].rearrange("(a b) -> a b", b=P)).then_inc(gain_in, 16)
        act.wait_ge(ident_in, 16)
        warm(ACT.Sqrt)
        tile = x_parts(0)
        act.wait_ge(vec_ready, 1)
        for m in range(KD):
            tile(m)
            if m == 0:
                split(0)
        split(1)
        for t in range(TT):
            act.wait_ge(x_landed[t], 16)
            act.activation(x_sq[:, t, :], x_in[:, t, :], ACT.Square,
                           accum_out=x_sum[:, t:t + 1]).then_inc(token_sums, 1)
        square_root("x0")
        split(2)
        split(3)
        ffn(0)
        down(0, x_parts(1))

        square_root("x1")
        warm(ACT.Exp)
        tile2 = x_parts(2)
        for n in range(M1["end"]):
            for s in range(NSEG1):
                if n == TURN1[s] + 1:
                    copy_turned(s, pt1[:, s % 3, :])
            for k in range(12):
                if n == TURN1[last_segment(k)] + OUT_LAG + 1:
                    y_high(k, y1h[:, k // 2, :], slice(HD * (k % 2), HD * (k % 2) + HD))
            for k in range(12):
                s = last_segment(k)
                if k < DSA_J and n == norm_step(k) != SCORES1[s] + 1:
                    normalize(k, probs1(k))
                if n == SCORES1[s] + 1:
                    exp(k, probs1(k))
                    if k < DSA_J and n == norm_step(k):
                        normalize(k, probs1(k))
            if n == M1["end"] - 1:
                tile2(KD - 1)
            if n == M1["out"] - 1:
                merge_high(KD - 1, mh1, KD - 1)
            if n == M1["out"] + 4:
                warm(ACT.Sqrt)
            for h in ahead(n, M1_TOKEN):
                split(J0[1] + h)
            if M1["gates"] <= n < M1["merge"]:
                tanh_half(n - M1["gates"])
            if M1["out"] <= n < M1["end"] - 1:
                tile2(n - M1["out"])
            if M1["merge"] <= n < M1["out"] - 1:
                merge_high(n - M1["merge"], mh1, n - M1["merge"])
        act.wait_ge(half_done, J0[2])
        act.dma_start(wg2[:, :], w["gla_w_gate2_2"][0]).then_inc(small_in, 16)
        act.dma_start(pos_i[:, :], w["positions_2"].to_broadcast([P, T])).then_inc(pos_in, 16)
        ffn(1)

        def rope_sines():
            act.wait_ge(sin_arg, 1)
            act.activation(cosT[:, :], tg[:, 0, :], ACT.Sin).then_inc(sin_ready, 1)
            act.wait_ge(sin_arg, 2)
            act.activation(sinT[:, :], tg[:, 1, :], ACT.Sin).then_inc(sin_ready, 1)
        down(1, x_parts(3), {FFN_UP + 14: rope_sines})

        square_root("x3", var[:, :], root[:, :])
        warm(ACT.Tanh)
        tile4 = x_parts(4)
        for n in range(M2["end"]):
            for s in range(NSEG2):
                k = 12 + s
                if n == TURN2[s] + 1:
                    copy_turned(NSEG1 + s, pt2[:, s % 2, :])
                if n == TURN2[s] + OUT_LAG + 1:
                    y_high(k, y2ah[:, s // 2, :], slice(HD * (s % 2), HD * (s % 2) + HD))
            for s in range(NSEG2):
                k = 12 + s
                if n == SCORES2[s] + 1:
                    exp(k, p2[:, s % 5:s % 5 + 1, :])
            if n == M2["end"] - 1:
                tile4(KD - 1)
            if n == M2["out"] - 1:
                merge_high(KD + KD - 1, mh2, KD - 1)
            if n == M2["out"] + 4:
                warm(ACT.Sqrt)
            for h in ahead(n, M2_TOKEN):
                split(J0[3] + h)
            if n in OG_HALVES:
                tanh_half(16 + OG_HALVES.index(n))
            if M2["ckv"] <= n < M2["gv"]:
                i = n - M2["ckv"]
                src, dst, m, g = (ckv, ckvh, i, VEC["mla_norm_ckv_2"]) if i < 2 else (
                    cq, cqh, i - 2, VEC["mla_norm_cq_2"])
                act.wait_ge(cx_ready, i + 1)
                act.activation(dst[:, m, :], src[:, m, :], ACT.Copy,
                               scale=vec[:, g + m:g + m + 1]).then_inc(cx_hi, 1)
            if M2["gates"] <= n < M2["merge"]:
                tanh_half(20 + n - M2["gates"])
            if n == Z_AT + 1:
                act.wait_ge(decay_taken, 2)
                link(act.activation(ze[:, :, :], zl[:, :, :], ACT.Abs))
                link(act.activation(ze[:, :, :], ze[:, :, :], ACT.Exp, scale=-1.0))
                act.activation(ze[:, :, :], ze[:, :, :], ACT.Ln, bias=1.0).then_inc(decay_logs, 1)
            if n == LATENT_AT + 1:
                square_root("latent", var[:, :], root[:, :])
            if n == GLA_O_AT + 1:
                act.wait_ge(gla_out, 1)
                for t in range(TT):
                    act.activation(go[:, t, :], ps[4 + t][:, :], ACT.Copy).then_inc(gla_copied, 1)
            if n in (GLA_O_AT + 1, GLA_O_AT + 2):
                t = n - GLA_O_AT - 1
                act.wait_ge(gla_copied, TT)
                for h in range(4):
                    c = slice(h * P, (h + 1) * P)
                    act.activation(osq[:, t, c], go[:, t, c], ACT.Square,
                                   accum_out=gss[:, 0, 4 * t + h:4 * t + h + 1]).then_inc(gla_sums, 1)
            if n == GLA_O_AT + 3:
                square_root("gla", gss[:, 1, :], gss[:, 2, :])
            lv = n - LEVEL_AT - 1
            if lv in (0, 1):
                act.wait_ge(lv_done, lv + 1)
                for e in range(2):
                    act.activation(at3[:, 0:2, e::2, :] if lv else at3[:, 2, e::2, :], level_scores(lv, e),
                                   ACT.Copy).then_inc(lv_taken, 1)
            lv = n - LEVEL_AT + 2
            if 0 <= lv < 8:
                act.wait_ge(lv_diff, lv + 1)
                if lv:
                    act.wait_ge(lv_ready, 2 * lv)
                s = GLA_LEVELS[lv]
                dv = lvd[:, :, :].rearrange("p a (g c) -> p (a g) c", c=2 * s)
                ev = lve[:, :, :].rearrange("p a (g c) -> p (a g) c", c=2 * s)
                act.activation(ev[:, :, s:], dv[:, :, s:], ACT.Exp, scale=1.0 / 16.0).then_inc(lv_exp, 1)
                act.activation(ev[:, :, 0:s], dv[:, :, 0:s], ACT.Exp, scale=-1.0 / 16.0).then_inc(lv_exp, 1)
            if n == GLA_TURN_AT + 1:
                for h in range(4):
                    act.wait_ge(gla_y, h + 1)
                    act.activation(y2bh[:, h, :], go_y[:, h, :], ACT.Copy).then_inc(yb_hi, 1)
            if M2["out"] <= n < M2["end"] - 1:
                tile4(n - M2["out"])
            if M2["merge"] <= n < M2["out"] - 1:
                merge_high(KD + n - M2["merge"], mh2, n - M2["merge"])
        ffn(2)

        def result_tile(m):
            act.wait_ge(x_updated, 8 * 5 + m + 1)
            act.activation(o_fm[:, m, :], x[:, m, :], ACT.Copy, scale=GAIN[5][:, m:m + 1]).then_inc(fin_ready, 1)
        down(2, result_tile)
        square_root("x5")
        act.wait_ge(r_ready, ROOTS["x5"] + 1)
        act.wait_ge(fin_turned, 2)
        for c in range(2):
            act.activation(o_tm[:, 1, c * 512:(c + 1) * 512], ps[2 + c][:, :], ACT.Copy,
                           scale=rcol[:, 1:2]).then_inc(fin_scaled[1], 1)


    @block_ctx.vector
    def _(dve):
        steps = [0]

        def link(ins):
            steps[0] += 1
            ins.then_inc(dve_step, 1)
            dve.wait_ge(dve_step, steps[0])

        def split(j):
            views, u = half_views(j, lo)
            his = half_views(j, hi)[0]
            dve.wait_ge(split_hi, j + 1)
            for n, (src, dst) in enumerate(views):
                ins = dve.tensor_tensor(dst, src, his[n][1].bitcast(F32), ALU.subtract)
                if n == len(views) - 1:
                    ins.then_inc(split_lo, 1)

        def newton_root(name, v, s, tmp, dst):
            dve.wait_ge(root_ready, ROOTS[name] + 1)
            link(dve.reciprocal(s, s))
            link(dve.tensor_tensor(tmp, s, s, ALU.mult))
            link(dve.tensor_tensor(tmp, tmp, v, ALU.mult))
            link(dve.tensor_scalar(tmp, tmp, -0.5, 1.5, ALU.mult, ALU.add))
            dve.tensor_tensor(dst, tmp, s, ALU.mult).then_inc(r_ready, 1)
            dve.wait_ge(r_ready, ROOTS[name] + 1)

        def variance(dst, sums, n):
            dve.tensor_scalar(dst, sums, 1.0 / n, EPS, ALU.mult, ALU.add).then_inc(var_ready, 1)

        def row(name, src, *dsts):
            dve.wait_ge(row_spread, ROWS[name] + 1)
            for i, dst in enumerate(dsts):
                ins = dve.tensor_copy(dst, src[:, i * T:(i + 1) * T])
            ins.then_inc(row_ready, 1)
            dve.wait_ge(row_ready, ROWS[name] + 1)

        def norm(wv):
            name = f"x{wv}"
            if wv:
                dve.wait_ge(sums_ready, SUMS[name] + 1)
            else:
                dve.wait_ge(token_sums, TT)
            if wv == 3:
                link(dve.tensor_scalar(var[:, TT:], ps[7][:, 0:TT], 1.0 / D, EPS, ALU.mult, ALU.add))
                link(dve.tensor_scalar(var[:, 0:TT], ps[7][:, TT:2 * TT], 1.0 / D, None, ALU.mult))
                dve.scalar_tensor_tensor(out=var[:, 0:TT], in0=var[:, TT:], scalar=EPS, in1=var[:, 0:TT],
                                         op0=ALU.mult, op1=ALU.add).then_inc(var_ready, 1)
                newton_root(name, var[:, :], root[:, :], newton[:, :], rcol[:, 0:2 * TT])
            else:
                variance(var[:, 0:TT], ps[7][:, 0:TT] if wv else x_sum[:, :], D)
                newton_root(name, var[:, 0:TT], root[:, 0:TT], newton[:, 0:TT], rcol[:, 0:TT])

        def norm_row(wv):
            row(f"x{wv}", ps[6], R[:, :], *([R1[:, :]] if wv == 3 else []))

        def update(wv, m, factor):
            if wv == 4:
                dve.wait_ge(residual_scaled, m + 1)
            b = ps[4 + m % 2][:, 0:T]
            if factor == 1.0:
                dve.tensor_tensor(x[:, m, :], b, x[:, m, :], ALU.add).then_inc(x_updated, 1)
            else:
                dve.scalar_tensor_tensor(out=x[:, m, :], in0=b, scalar=factor, in1=x[:, m, :],
                                         op0=ALU.mult, op1=ALU.add).then_inc(x_updated, 1)

        def x_low(wv, m):
            dve.wait_ge(xh_ready, 8 * wv + m + 1)
            dve.scalar_tensor_tensor(out=xl[:, m, :], in0=x[:, m, :], scalar=GAIN[wv][:, m:m + 1],
                                     in1=xh[:, m, :].bitcast(F32), op0=ALU.mult,
                                     op1=ALU.subtract).then_inc(xl_ready, 1)

        def ffn(f):
            J, E = JF[f], EF[f]

            def pair(e, q, done):
                b = (q // 2) % 2
                dve.wait_ge(half_done, done)
                dve.tensor_tensor(tg[:, b, :], ps[(q - 1) % 8][:, 0:T], R[:, :], ALU.mult).then_inc(gate_scaled, 1)
                dve.tensor_tensor(tu[:, b, :], ps[q % 8][:, 0:T], R[:, :], ALU.mult).then_inc(up_scaled, 1)
                dve.wait_ge(up_scaled, e + 1)
                dve.wait_ge(silu_ready, e + 1)
                dve.tensor_tensor(hf[:, b, :], sg[:, b, :], tu[:, b, :], ALU.mult).then_inc(hidden_ready, 1)

            def low(e, q, ft):
                b = (q // 2) % 2
                dve.wait_ge(hidden_ready, e + 1)
                dve.wait_ge(hidden_hi, e + 1)
                o = hl[:, ft, :] if isinstance(ft, int) else hl[:, bass.ds(ft, 1), :]
                h = hh[:, ft, :] if isinstance(ft, int) else hh[:, bass.ds(ft, 1), :]
                src = hf[:, b, :] if isinstance(ft, int) else hf[:, b:b + 1, :]
                dve.tensor_tensor(o, src, h.bitcast(F32), ALU.subtract).then_inc(hidden_lo, 1)

            def run(q0, n):
                for q in range(q0, q0 + n):
                    if q % 2:
                        pair(E + q // 2, q, J + q + 1)
                    split(J + q + 4)
                    if q % 2:
                        low(E + q // 2, q, q // 2)
            run(0, 4)
            with dve.Fori(0, 4) as i:
                for q in range(4, 12):
                    if q % 2:
                        pair(i * 4 + (E + q // 2), q, i * 8 + (J + q + 1))
                    j = J + q + 4
                    views = half_views(j, lo)[0]
                    his = half_views(j, hi)[0]
                    dve.wait_ge(split_hi, i * 8 + (j + 1))
                    for (src, dst), (_, h) in zip(views, his):
                        dve.tensor_tensor(dst, src, h.bitcast(F32), ALU.subtract).then_inc(split_lo, 1)
                    if q % 2:
                        low(i * 4 + (E + q // 2), q, i * 4 + q // 2)
            run(36, 8)

        def down(f, wv, factor, extra=None):
            J = JF[f]
            for q in range(FFN_UP, FFN_HALVES):
                m = (q - FFN_UP) // 4
                if q % 4 == 3:
                    dve.wait_ge(half_done, J + q + 1)
                    update(wv, m, factor)
                if q == FFN_HALVES - 1 and wv < 5:
                    x_low(wv, m)
                if J + q + 4 < J0[5]:
                    split(J + q + 4)
                if q % 4 == 3 and wv < 5 and q < FFN_HALVES - 1:
                    x_low(wv, m)
                if extra is not None and q in extra:
                    extra[q]()

        def gate_half(i, n):
            if i >= 2:
                dve.wait_ge(sig_ready, i - 1)
            dve.tensor_tensor(tu[:, i % 2, :], ps[n % 3][:, 0:T], R[:, :], ALU.mult).then_inc(z_ready, 1)

        def merge(i, m, n, gates):
            a = dve.tensor_tensor(tg[:, m % 2, :], ps[n % 3][:, 0:T], gates[:, m, :], ALU.mult)
            a.then_inc(merge_ab, 1)
            dve.tensor_tensor(tu[:, m % 2, :], ps[n % 3][:, T:2 * T], gates[:, KD + m, :],
                              ALU.mult).then_inc(merge_ab, 1)

        def bias(s, g, slope, dst, turned):
            dve.wait_ge(seg_scores, s + 1)
            if turned > 0:
                dve.wait_ge(seg_turned, turned)
            dve.scalar_tensor_tensor(out=dst, in0=dist[:, g, :], scalar=-slope,
                                     in1=ps[4 + s % 2][:, 0:NSEG], op0=ALU.mult,
                                     op1=ALU.add).then_inc(seg_biased, 1)

        def maxima(k, s, scores):
            dve.wait_ge(seg_biased, s + 1)
            for t, (a, b) in enumerate(((0, P), (P, NSEG))):
                c = 2 * (k % 4) + t
                dve.tensor_reduce(nmax[:, c:c + 1], scores[:, :, a:b], AX.XY, ALU.max,
                                  negate=True).then_inc(seg_max, 1)

        def inverse(k):
            if k >= 4:
                dve.wait_ge(*normalised(k - 4))
            for t in range(2):
                c = 2 * (k % 4) + t
                dve.wait_ge(seg_probs, 2 * k + t + 1)
                dve.reciprocal(sinv[:, c:c + 1], ssum[:, c:c + 1]).then_inc(seg_inv, 1)

        def y_low(k, dst_hi, dst_lo, rows):
            dve.wait_ge(seg_out, k + 1)
            dve.wait_ge(y_hi, k + 1)
            dve.tensor_tensor(dst_lo[rows], ps[3][rows, 0:T], dst_hi[rows].bitcast(F32),
                              ALU.subtract).then_inc(y_lo, 1)

        dve.wait_ge(vec_turned, 1)
        dve.tensor_copy(vec[:, 0:KD], ps[0][:, 0:KD]).then_inc(vec_ready, 1)
        for m in range(KD):
            dve.wait_ge(x_turned, m + 1)
            dve.tensor_copy(x[:, m, :], ps[4 + m // 2][:, (m % 2) * T:(m % 2 + 1) * T]).then_inc(x_updated, 1)
            if m == 3:
                split(0)
        dve.wait_ge(vec_ready, 1)
        dve.wait_ge(x_updated, KD)
        for m in range(KD):
            if m == 4:
                split(1)
            x_low(0, m)
        norm(0)
        split(2)
        norm_row(0)
        split(3)
        dve.wait_ge(vec_turned, 2)
        dve.tensor_copy(vec[:, KD:], ps[7][:, KD:NVEC]).then_inc(vec_ready, 1)
        dve.wait_ge(vec_ready, 2)
        vf, vl = VEC["norm_final"], VEC["ln_mix_2"]
        dve.tensor_tensor(vec2[:, 0:8], vec[:, vf:vf + 8], vec[:, vl:vl + 8], ALU.mult).then_inc(vec_ready, 1)
        dve.tensor_tensor(vec2[:, 8:16], vec[:, vf:vf + 8], vec[:, vf:vf + 8], ALU.mult).then_inc(vec_ready, 1)
        ffn(0)
        down(0, 1, 0.5)

        norm(1)
        norm_row(1)
        dve.wait_ge(const_in, 16)
        for n in range(M1["end"]):
            for s in range(NSEG1):
                if n == SCORES1[s] + 1:
                    if s < N_DSA:
                        k, g = divmod(s, 3)
                        bias(s, g, alibi(4 * g + k, 12), p1[:, s % 9, :], s - 8)
                    else:
                        k, g = 4 + s - N_DSA, 2
                        bias(s, 3, alibi(s - N_DSA, HEADS), p1[:, s % 9, :], s - 8)
                    if g == 2:
                        maxima(k, s, probs1(k))
                        if n in M1_TOKEN:
                            inverse(k)
            for k in range(12):
                if n == TURN1[last_segment(k)] + OUT_LAG + 1:
                    y_low(k, y1h[:, k // 2, :], y1l[:, k // 2, :], slice(HD * (k % 2), HD * (k % 2) + HD))
            if n < M1["out"] and not (n - 1 in M1_TOKEN or n in M1_TOKEN):
                dve.wait_ge(half_done, J0[1] + n + 1)
            bank = ps[n % 3][:, 0:T]
            if n < M1["ka"]:
                dve.scalar_tensor_tensor(out=qa[:, n, :], in0=bank, scalar=HD ** -0.5, in1=R[:, :],
                                         op0=ALU.mult, op1=ALU.mult).then_inc(half_taken, 1)
            elif n < M1["va"]:
                dve.tensor_tensor(ka[:, n - M1["ka"], :], bank, R[:, :], ALU.mult).then_inc(half_taken, 1)
            elif n - 1 in M1_TOKEN:
                dve.wait_ge(half_done, J0[1] + n + 1)
                dst, c = (va, n - 1 - M1["va"]) if n < M1["qb"] else (vb, n - 1 - M1["vb"])
                for t in range(TT):
                    dve.tensor_scalar(dst[:, t, c * P:c * P + 256], ps[(n - 1 + t) % 3][:, 0:T],
                                      rcol[:, t:t + 1], None, ALU.mult).then_inc(half_taken, 1)
            elif n in M1_TOKEN:
                pass
            elif n < M1["kb"]:
                dve.scalar_tensor_tensor(out=qb[:, n - M1["qb"], :], in0=bank, scalar=HD ** -0.5, in1=R[:, :],
                                         op0=ALU.mult, op1=ALU.mult).then_inc(half_taken, 1)
            elif n < M1["vb"]:
                dve.tensor_tensor(kb[:, n - M1["kb"], :], bank, R[:, :], ALU.mult).then_inc(half_taken, 1)
            elif n < M1["merge"]:
                gate_half(n - M1["gates"], n)
            elif n < M1["out"]:
                m = n - M1["merge"]
                if m == 0:
                    dve.wait_ge(sig_ready, 16)
                merge(m, m, n, gates1)
            else:
                m = n - M1["out"]
                dve.wait_ge(half_done, J0[1] + n + 1)
                update(2, m, 1.0)
                if m == KD - 1:
                    x_low(2, m)
            for h in ahead(n, M1_TOKEN):
                split(J0[1] + h)
            if M1["out"] <= n < M1["end"] - 1:
                x_low(2, n - M1["out"])
            for k in range(12):
                if n == SCORES1[last_segment(k)] + 1 and n not in M1_TOKEN:
                    inverse(k)
        norm(2)
        norm_row(2)
        dve.wait_ge(merged_lo, KD)
        ffn(1)

        angle, whole = tg[:, 0, :], tg[:, 1, :]

        def rope_start():
            dve.wait_ge(pos_in, 16)
            dve.wait_ge(const_in, 48)
            link(dve.tensor_copy(angle, pos_i[:, :]))
            link(dve.tensor_scalar(angle, angle, cst[:, C_INV:C_INV + 1], None, ALU.mult))

        def rope_whole(turns):
            magic = 1.5 * 2.0 ** 23
            link(dve.tensor_scalar(whole, angle, 1.0 / (2 * math.pi * turns), None, ALU.mult))
            link(dve.tensor_scalar(whole, whole, magic, None, ALU.add))
            link(dve.tensor_scalar(whole, whole, -magic, None, ALU.add))

        def rope_less(turns):
            c1 = 6.28125
            c2 = float(np.floor((2 * math.pi - c1) * 2.0 ** 20) / 2.0 ** 20)
            for c in (c1, c2, float(np.float32(2 * math.pi - c1 - c2))):
                link(dve.scalar_tensor_tensor(out=angle, in0=whole, scalar=-c * turns, in1=angle,
                                              op0=ALU.mult, op1=ALU.add))

        def rope_arguments():
            lim = 3.1415925
            link(dve.tensor_scalar(whole, angle, -lim, lim, ALU.max, ALU.min))
            link(dve.tensor_scalar(angle, whole, -1.0, None, ALU.mult))
            link(dve.tensor_tensor(angle, whole, angle, ALU.max))
            dve.tensor_scalar(angle, angle, -1.0, math.pi / 2, ALU.mult, ALU.add).then_inc(sin_arg, 2)

        def rope_tables():
            dve.wait_ge(sin_ready, 2)
            link(dve.tensor_scalar(sinT[:, :], sinT[:, :], cst[:, C_SIGN:C_SIGN + 1], None, ALU.mult))
        down(1, 3, 0.5, {FFN_UP + 2: rope_start, FFN_UP + 4: lambda: rope_whole(4096.0),
                         FFN_UP + 5: lambda: rope_less(4096.0), FFN_UP + 8: lambda: rope_whole(1.0),
                         FFN_UP + 9: lambda: rope_less(1.0), FFN_UP + 12: rope_arguments,
                         FFN_UP + 18: rope_tables})

        norm(3)
        norm_row(3)
        link(dve.tensor_tensor(rope_k[:, 0, :], cosT[:, :], R[:, :], ALU.mult))
        link(dve.tensor_tensor(rope_k[:, 1, :], sinT[:, :], R[:, :], ALU.mult))
        for n in range(M2["end"]):
            if n == M2["lr"] + 3:
                dve.wait_ge(*taken(3, M2["lr"]))
                for g in range(4):
                    ins = dve.tensor_tensor(kr[32 * g:32 * g + 32, 0, :], acc[32:64, 0, :], acc[32:64, 1, :],
                                            ALU.add)
                link(ins)
            if n == Z_AT + 1:
                dve.wait_ge(decay_raw, 1)
                for c in range(2):
                    v = VEC["gla_b_gate_2"] + c
                    dve.tensor_scalar(zl[:, c, :], ps[4][:, c * T:(c + 1) * T], vec[:, v:v + 1], None,
                                      ALU.add).then_inc(decay_taken, 1)
            if n == Z_AT + 2:
                dve.wait_ge(decay_logs, 1)
                link(dve.scalar_tensor_tensor(out=zl[:, :, :], in0=zl[:, :, :], scalar=0.0, in1=ze[:, :, :],
                                              op0=ALU.min, op1=ALU.subtract))
                flat = zl[:, :, :].rearrange("p a c -> p (a c)")
                for dst, c in ((run_chunk, C_SEG), (run_all, C_SEG + 2 * T)):
                    link(dve.tensor_tensor_scan(dst[:, :, :].rearrange("p a c -> p (a c)"), cst[:, c:c + 2 * T],
                                                flat, 0.0, ALU.mult, ALU.add))
            lv = n - LEVEL_AT + 1
            if 0 <= lv + 1 < 8:
                s = GLA_LEVELS[lv + 1]
                if lv >= 0:
                    dve.wait_ge(lv_exp, 2 * (lv + 1))
                src = (run_all if s >= GLA_CHUNK else run_chunk)[:, :, :].rearrange("p a (g c) -> p (a g) c", c=2 * s)
                g = 2 * T // (2 * s)
                dve.tensor_tensor(lvd[:, :, :].rearrange("p a (g c) -> p (a g) c", c=2 * s), src,
                                  src[:, :, s - 1:s].to_broadcast([P, g, 2 * s]), ALU.subtract).then_inc(lv_diff, 1)
            lv = n - LEVEL_AT - 1
            if 2 <= lv < 9:
                dve.wait_ge(lv_done, lv + 1)
                dve.wait_ge(lv_taken, 2 * lv)
                m_ = masks[:, lv - 2:lv - 1, :].unsqueeze(2).to_broadcast([P, 2, 2, P])
                for e in range(2):
                    dve.copy_predicated(at3[:, 0:2, e::2, :], m_, level_scores(lv, e)).then_inc(lv_taken, 1)
            if n == LATENT_AT + 1:
                dve.wait_ge(sums_ready, SUMS["latent"] + 1)
                dve.tensor_scalar(var[:, 0:TT], ps[3][:, 0:TT], 1.0 / CKV, EPS, ALU.mult, ALU.add)
                variance(var[:, TT:], ps[3][:, TT:2 * TT], CQ)
            if n == LATENT_AT + 2:
                newton_root("latent", var[:, :], root[:, :], newton[:, :], rcol[:, RCOL["ckv"]:])
            if n == LATENT_AT + 3:
                row("latent", ps[3], Rkv[:, :], Rq[:, :])
                for c, tab in enumerate((cosT, sinT)):
                    link(dve.scalar_tensor_tensor(out=rope_q[:, c, :], in0=tab[:, :], scalar=MLA_QK ** -0.5,
                                                  in1=Rq[:, :], op0=ALU.mult, op1=ALU.mult))
            if n == GLA_O_AT + 3:
                dve.wait_ge(gla_sums, 8)
                variance(gss[:, 1, :], gss[:, 0, :], P)
            if n == GLA_O_AT + 4:
                newton_root("gla", gss[:, 1, :], gss[:, 2, :], gss[:, 3, :], gss[:, 4, :])
            if n == GLA_TURN_AT + 1:
                dve.wait_ge(gla_turned, 1)
                dve.wait_ge(sig_ready, 20)
                v = VEC["gla_norm_2"]
                for h in range(4):
                    dve.scalar_tensor_tensor(out=go_y[:, h, :], in0=ps[4 + h // 2][:, (h % 2) * T:(h % 2 + 1) * T],
                                             scalar=vec[:, v:v + 1], in1=og[:, h, :], op0=ALU.mult,
                                             op1=ALU.mult).then_inc(gla_y, 1)
            for s in range(NSEG2):
                k = 12 + s
                if n == SCORES2[s] + 1:
                    bias(NSEG1 + s, 4, 1.0, p2[:, s % 5, :], NSEG1 + s - 4 if s >= 5 else 0)
                    maxima(k, NSEG1 + s, p2[:, s % 5:s % 5 + 1, :])
                if n == TURN2[s] + OUT_LAG + 1:
                    y_low(k, y2ah[:, s // 2, :], y2al[:, s // 2, :], slice(HD * (s % 2), HD * (s % 2) + HD))
            if n < M2["out"] and not (n - 1 in M2_TOKEN or n in M2_TOKEN):
                dve.wait_ge(half_done, J0[3] + n + 1)
            bank = ps[n % 3][:, 0:T]
            rot = acc[:, 1, :]
            if n == M2["lr"]:
                dve.tensor_tensor(lr[:, :], bank[0:16, :], R[0:16, :], ALU.mult)
                dve.tensor_tensor(acc[32:64, 0, :], bank[32:64, :], rope_k[32:64, 0, :], ALU.mult)
                dve.tensor_tensor(acc[32:64, 1, :], bank[64:96, :], rope_k[64:96, 1, :],
                                  ALU.mult).then_inc(half_taken, 1)
            elif n in OG_HALVES:
                gate_half(16 + OG_HALVES.index(n), n)
            elif n < M2["gk"]:
                dve.scalar_tensor_tensor(out=gq[:, n - M2["gq"], :], in0=bank, scalar=HD ** -0.5, in1=R[:, :],
                                         op0=ALU.mult, op1=ALU.mult).then_inc(half_taken, 1)
            elif n < M2["og2"]:
                dve.tensor_tensor(gk[:, n - M2["gk"], :], bank, R[:, :], ALU.mult).then_inc(half_taken, 1)
            elif n < M2["gv"]:
                i = n - M2["ckv"]
                dst, m = (ckv, i) if i < 2 else (cq, i - 2)
                dve.tensor_tensor(dst[:, m, :], bank, R[:, :], ALU.mult).then_inc(cx_ready, 1)
            elif n - 1 in M2_TOKEN:
                dve.wait_ge(half_done, J0[3] + n + 1)
                dst, c, r = (gv, n - 1 - M2["gv"], 0) if n < M2["uq"] else (mv, n - 1 - M2["uv"], RCOL["ckv"])
                for t in range(TT):
                    dve.tensor_scalar(dst[:, t, c * P:c * P + 256], ps[(n - 1 + t) % 3][:, 0:T],
                                      rcol[:, r + t:r + t + 1], None, ALU.mult).then_inc(half_taken, 1)
            elif n in M2_TOKEN:
                pass
            elif n < M2["uqr"]:
                dve.scalar_tensor_tensor(out=qn[:, n - M2["uq"], :], in0=bank, scalar=MLA_QK ** -0.5,
                                         in1=Rq[:, :], op0=ALU.mult, op1=ALU.mult).then_inc(half_taken, 1)
            elif n < M2["uqr"] + 2:
                dve.tensor_tensor(qr[:, n - M2["uqr"], :], bank, rope_q[:, 0, :], ALU.mult).then_inc(half_taken, 1)
            elif n < M2["ukv"]:
                c = n - M2["uqr"] - 2
                dve.tensor_tensor(rot, bank, rope_q[:, 1, :], ALU.mult).then_inc(half_taken, 1)
                dve.wait_ge(*taken(3, n))
                link(dve.tensor_tensor(qr[:, c, :], qr[:, c, :], rot, ALU.add))
            elif n < M2["uv"]:
                dve.tensor_tensor(kn[:, n - M2["ukv"], :], bank, Rkv[:, :], ALU.mult).then_inc(half_taken, 1)
            elif n < M2["merge"]:
                gate_half(20 + n - M2["gates"], n)
            elif n < M2["out"]:
                m = n - M2["merge"]
                if m == 0:
                    dve.wait_ge(sig_ready, 36)
                merge(KD + m, m, n, gates2)
            else:
                m = n - M2["out"]
                dve.wait_ge(half_done, J0[3] + n + 1)
                update(4, m, 1.0)
                if m == KD - 1:
                    x_low(4, m)
            for h in ahead(n, M2_TOKEN):
                split(J0[3] + h)
            if M2["ckv"] <= n < M2["gv"]:
                i = n - M2["ckv"]
                src, dh, dl, m, g = (ckv, ckvh, ckvl, i, VEC["mla_norm_ckv_2"]) if i < 2 else (
                    cq, cqh, cql, i - 2, VEC["mla_norm_cq_2"])
                dve.wait_ge(cx_ready, i + 1)
                dve.wait_ge(cx_hi, i + 1)
                dve.scalar_tensor_tensor(out=dl[:, m, :], in0=src[:, m, :], scalar=vec[:, g + m:g + m + 1],
                                         in1=dh[:, m, :].bitcast(F32), op0=ALU.mult,
                                         op1=ALU.subtract).then_inc(cx_lo, 1)
            if M2["out"] <= n < M2["end"] - 1:
                x_low(4, n - M2["out"])
            for s in range(NSEG2):
                if n == SCORES2[s] + 1:
                    inverse(12 + s)
        norm(4)
        norm_row(4)
        dve.wait_ge(merged_lo, 2 * KD)
        ffn(2)
        down(2, 5, 1.0)
        norm(5)
        dve.wait_ge(fin_turned, 2)
        for c in range(2):
            dve.tensor_scalar(o_tm[:, 0, c * 512:(c + 1) * 512], ps[c][:, :], rcol[:, 0:1], None,
                              ALU.mult).then_inc(fin_scaled[0], 1)

    @block_ctx.gpsimd
    def _(pool):
        steps = [0]

        def link(ins):
            steps[0] += 1
            ins.then_inc(pool_step, 1)
            pool.wait_ge(pool_step, steps[0])

        def squares(wv, m):
            pool.wait_ge(x_updated, 8 * wv + m + 1)
            two = wv == 3
            first = m == 0
            if wv > 1 or m:
                pool.wait_ge(acc_ready, 8 * (wv - 1) + m)
            to = acc[:, 0, :] if first else sq[:, 0, :]
            ins = pool.tensor_tensor(to, x[:, m, :], x[:, m, :], ALU.mult)
            if m == KD - 1 or first and not two:
                ins.then_inc(acc_ready, 1)
                return
            link(ins)
            if two:
                ins = pool.tensor_scalar(acc[:, 1, :] if first else sq[:, 1, :], to, vec2[:, 8 + m:9 + m], None,
                                         ALU.mult)
                if first:
                    ins.then_inc(acc_ready, 1)
                    return
                link(ins)
                link(pool.tensor_tensor(acc[:, 0, :], acc[:, 0, :], sq[:, 0, :], ALU.add))
                pool.tensor_tensor(acc[:, 1, :], acc[:, 1, :], sq[:, 1, :], ALU.add).then_inc(acc_ready, 1)
            else:
                pool.tensor_tensor(acc[:, 0, :], acc[:, 0, :], sq[:, 0, :], ALU.add).then_inc(acc_ready, 1)

        def sigmoid(i, dst):
            pool.wait_ge(tanh_ready, i + 1)
            pool.tensor_scalar(dst, tg[:, i % 2, :], 0.5, 0.5, ALU.mult, ALU.add).then_inc(sig_ready, 1)

        def add_parts(i):
            pool.wait_ge(merge_ab, 2 * (i + 1))
            if i >= 2:
                pool.wait_ge(merged_lo, i - 1)
            pool.tensor_tensor(hf[:, i % 2, :], tg[:, i % 2, :], tu[:, i % 2, :], ALU.add).then_inc(merged, 1)

        def merge_low(i, m, dst_hi, dst_lo):
            pool.wait_ge(merged, i + 1)
            pool.wait_ge(merged_hi, i + 1)
            pool.tensor_tensor(dst_lo[:, m, :], hf[:, m % 2, :], dst_hi[:, m, :].bitcast(F32),
                               ALU.subtract).then_inc(merged_lo, 1)

        for m in range(KD):
            squares(1, m)
        def normalize(k, probs):
            for t, (a, b) in enumerate(((0, P), (P, NSEG))):
                c = 2 * (k % 4) + t
                pool.wait_ge(seg_inv, 2 * k + t + 1)
                pool.tensor_scalar(probs[:, a:b], probs[:, a:b], sinv[:, c:c + 1], None,
                                   ALU.mult).then_inc(single_norm, 1)

        for n in range(M1["out"]):
            for k in range(DSA_J, 12):
                if n == SCORES1[last_segment(k)] + 2:
                    normalize(k, p1[:, last_segment(k) % 9, :])
            if M1["gates"] <= n < M1["merge"]:
                sigmoid(n - M1["gates"], gates1[:, n - M1["gates"], :])
            if n >= M1["merge"]:
                m = n - M1["merge"]
                add_parts(m)
                if m:
                    merge_low(m - 1, m - 1, mh1, ml1)
        merge_low(KD - 1, KD - 1, mh1, ml1)
        for wv in (2, 3):
            for m in range(KD):
                squares(wv, m)

        def og_half(c):
            i = 16 + c
            pool.wait_ge(tanh_ready, i + 1)
            link(pool.tensor_scalar(tg[:, i % 2, :], tg[:, i % 2, :], 0.5, 0.5, ALU.mult, ALU.add))
            pool.tensor_tensor(og[:, c, :], tu[:, i % 2, :], tg[:, i % 2, :], ALU.mult).then_inc(sig_ready, 1)

        def level_zero(lv):
            if lv >= 2:
                pool.wait_ge(lv_done, lv - 1)
            link(pool.memset(lvq[:, lv % 2, :, :], 0.0))
            pool.memset(lvk[:, lv % 2, :, :], 0.0).then_inc(lv_zero, 1)

        def cx_squares(i):
            pool.wait_ge(cx_ready, i + 1)
            c, first = (0, i == 0) if i < 2 else (1, i == 2)
            src = ckv[:, i, :] if i < 2 else cq[:, i - 2, :]
            ins = pool.tensor_tensor(acc[:, c, :] if first else sq[:, 0, :], src, src, ALU.mult)
            if first:
                ins.then_inc(cx_acc, 1)
            else:
                link(ins)
                pool.wait_ge(cx_acc, i)
                pool.tensor_tensor(acc[:, c, :], acc[:, c, :], sq[:, 0, :], ALU.add).then_inc(cx_acc, 1)

        def level_parts(lv):
            s = GLA_LEVELS[lv]

            def at(v, a, b):
                return v.rearrange("p a (g c) -> p (a g) c", c=2 * s)[:, :, a:b]
            pool.wait_ge(*taken(3, M2["gk"] + 1))
            pool.wait_ge(lv_exp, 2 * (lv + 1))
            pool.wait_ge(lv_zero, lv + 1)
            pool.tensor_tensor(at(lvq[:, lv % 2, :, :], s, 2 * s), at(gq[:, :, :], s, 2 * s),
                               at(lve[:, :, :], s, 2 * s), ALU.mult).then_inc(lv_ready, 1)
            pool.tensor_tensor(at(lvk[:, lv % 2, :, :], 0, s), at(gk[:, :, :], 0, s),
                               at(lve[:, :, :], 0, s), ALU.mult).then_inc(lv_ready, 1)

        def scale_residual(m):
            v = VEC["norm_final"] + m
            pool.wait_ge(xh_ready, 24 + m + 1)
            pool.wait_ge(xl_ready, 24 + m + 1)
            pool.wait_ge(row_ready, ROWS["x3"] + 1)
            link(pool.tensor_scalar(x[:, m, :], x[:, m, :], vec[:, v:v + 1], None, ALU.mult))
            pool.tensor_tensor(x[:, m, :], x[:, m, :], R1[:, :], ALU.mult).then_inc(residual_scaled, 1)

        for n in range(M2["out"]):
            if n == 3:
                level_zero(0)
            if n == 4:
                level_zero(1)
            lv = n - LEVEL_AT + 1
            if 0 <= lv < 8:
                if lv >= 2:
                    level_zero(lv)
                level_parts(lv)
            if n in OG_HALVES:
                og_half(OG_HALVES.index(n))
            if M2["ckv"] <= n < M2["gv"]:
                cx_squares(n - M2["ckv"])
            if M2["gates"] + 4 <= n < M2["gates"] + 4 + KD:
                scale_residual(n - M2["gates"] - 4)
            if n == GLA_O_AT + 4:
                pool.wait_ge(r_ready, ROOTS["gla"] + 1)
                gh = go[:, :, :].rearrange("p t (h c) -> p (t h) c", c=P)
                for a in (0, 4):
                    pool.tensor_tensor(gh[:, a:a + 4, :], gh[:, a:a + 4, :],
                                       gss[:, 4, a:a + 4].unsqueeze(2).to_broadcast([P, 4, P]),
                                       ALU.mult).then_inc(gla_scaled, 1)
            if n == GLA_TURN_AT + 1:
                for h in range(4):
                    pool.wait_ge(gla_y, h + 1)
                    pool.wait_ge(yb_hi, h + 1)
                    pool.tensor_tensor(y2bl[:, h, :], go_y[:, h, :], y2bh[:, h, :].bitcast(F32),
                                       ALU.subtract).then_inc(yb_lo, 1)
            for s in range(NSEG2):
                if n == SCORES2[s] + 2:
                    normalize(12 + s, p2[:, s % 5, :])
            if M2["gates"] <= n < M2["merge"]:
                i = n - M2["gates"]
                sigmoid(20 + i, gates2[:, i, :])
            if n >= M2["merge"]:
                m = n - M2["merge"]
                add_parts(KD + m)
                if m:
                    merge_low(KD + m - 1, m - 1, mh2, ml2)
        merge_low(2 * KD - 1, KD - 1, mh2, ml2)
        for wv in (4, 5):
            for m in range(KD):
                squares(wv, m)

    @block_ctx.tensor
    def _(pe):
        def feature_half(j, bank, k0, kt, xs, start=True, stop=True, at=0):
            for k in range(kt):
                a = (w_part(hi, j, k0 + k), w_part(lo, j, k0 + k))
                b = (xs[0][:, k, :], xs[1][:, k, :])
                pe.matmul(bank[:, at:at + T], a[0], b[0], start=start and k == 0, stop=False)
                pe.matmul(bank[:, at:at + T], a[0], b[1], start=False, stop=False)
                ins = pe.matmul(bank[:, at:at + T], a[1], b[0], start=False, stop=stop and k == kt - 1)
            return ins

        def turned(dst, src, unit=ident):
            return pe.transpose(dst, src, unit)

        def first_half(j, bank, xs, ready, base):
            for k in range(KD):
                pe.wait_ge(ready[0], base + k + 1)
                pe.matmul(bank[:, 0:T], w_part(hi, j, k), xs[0][:, k, :], start=k == 0, stop=False)
                pe.matmul(bank[:, 0:T], w_part(lo, j, k), xs[0][:, k, :], start=False, stop=False)
            for k in range(KD):
                pe.wait_ge(ready[1], base + k + 1)
                ins = pe.matmul(bank[:, 0:T], w_part(hi, j, k), xs[1][:, k, :], start=False, stop=k == KD - 1)
            return ins

        x_ready = (xh_ready, xl_ready)

        def sums(wv):
            pe.wait_ge(acc_ready, 8 * wv)
            for e in range(2 if wv == 3 else 1):
                factor = vec2[:, 8 + KD - 1:8 + KD] if e else ones[:, 0:1]
                for t in range(TT):
                    at, tok = e * TT + t, slice(t * P, (t + 1) * P)
                    pe.matmul(ps[7][:, at:at + 1], acc[:, e, tok], ones[:, 0:1], start=True, stop=False)
                    ins = pe.matmul(ps[7][:, at:at + 1], sq[:, 0, tok], factor, start=False, stop=True)
            ins.then_inc(sums_ready, 1)

        def token_sum(bank, at, e):
            for t in range(TT):
                ins = pe.matmul(bank[:, at + t:at + t + 1], acc[:, e, t * P:(t + 1) * P], ones[:, 0:1],
                                start=True, stop=True)
            return ins

        def row(name, bank, *cols):
            pe.wait_ge(r_ready, ROOTS[name] + 1)
            for i, c in enumerate(cols):
                for t in range(TT):
                    ins = pe.matmul(bank[:, i * T + t * P:i * T + (t + 1) * P],
                                    rcol[:, c + t:c + t + 1].to_broadcast([P, P]), ident, start=True, stop=True)
            ins.then_inc(row_spread, 1)

        def x_row(wv):
            row(f"x{wv}", ps[6], 0, *([TT] if wv == 3 else []))

        def ffn(f, wv):
            J, E = JF[f], EF[f]

            def up_half(q, ready, free=None, first=None):
                pe.wait_ge(split_lo, ready)
                if free is not None:
                    pe.wait_ge(up_scaled, free)
                if first is not None:
                    first_half(J + q, ps[q % 8], (xh, xl), x_ready, 8 * first).then_inc(half_done, 1)
                else:
                    feature_half(J + q, ps[q % 8], 0, KD, (xh, xl)).then_inc(half_done, 1)

            for q in range(4):
                up_half(q, J + q + 1, first=wv if q == 0 else None)
                if q == 0 and f:
                    sums(wv)
                if q == 1:
                    if f == 0:
                        pe.wait_ge(x_updated, 8)
                    x_row(wv)
                if q == 2 and f == 0:
                    pe.wait_ge(vec_in, 16 * (len(VEC) - 1))
                    turned(ps[7][:, 0:NVEC], vrow[:, :], ident[0:NVEC, 0:NVEC]).then_inc(vec_turned, 1)
            if f == 0:
                pe.wait_ge(vec_ready, 2)
            pe.wait_ge(x_updated, 8 * (wv + 1))
            pe.wait_ge(row_ready, ROWS[f"x{wv}"] + 1)
            for q in range(4, 12):
                up_half(q, J + q + 1, free=E + q // 2 - 3 if q >= 8 else None)
            with pe.Fori(0, 4) as i:
                for q in range(12, 20):
                    up_half(q, i * 8 + (J + q + 1), free=i * 4 + (E + q // 2 - 3))
            pe.wait_ge(up_scaled, E + NF - 2)
            with pe.Fori(0, 4) as i:
                for q in range(8):
                    k0, k1 = DOWN_K[q % 4]
                    m = q // 4
                    j = J + FFN_UP + q
                    pe.wait_ge(split_lo, i * 8 + (j + 1))
                    pe.wait_ge(hidden_lo, E + k1)
                    if q % 4 == 0:
                        pe.wait_ge(x_updated, i * 2 + (8 * (wv + 1) + m - 1))
                    feature_half(j, ps[4 + m], 0, k1 - k0, (hh[:, k0:k1, :], hl[:, k0:k1, :]),
                                 start=q % 4 == 0, stop=q % 4 == 3).then_inc(half_done, 1)

        def scores(s, q, k, rope=None):
            if s >= 2:
                pe.wait_ge(seg_biased, s - 1)
            b = ps[4 + s % 2]
            for a, c0, w_ in ((0, 0, P), (P, P, 2 * P)):
                ins = pe.matmul(b[:, c0:c0 + w_], q[:, a:a + P], k[:, 0:w_], start=True, stop=rope is None)
                if rope is not None:
                    ins = pe.matmul(b[:, c0:c0 + w_], rope[0][:, a:a + P], rope[1][:, 0:w_],
                                    start=False, stop=True)
            ins.then_inc(seg_scores, 1)

        def turn(s, k, probs):
            pe.wait_ge(*normalised(k))
            if s >= 2:
                pe.wait_ge(seg_copied, s - 1)
            for c in range(3):
                ins = turned(ps[6 + s % 2][:, c * P:(c + 1) * P], probs[:, c * P:(c + 1) * P])
            ins.then_inc(seg_turned, 1)

        def weighted(s, k, first, last, v, pt):
            pe.wait_ge(seg_copied, s + 1)
            if first and k >= 2:
                pe.wait_ge(y_lo, k - 1)
            rows = slice(HD * (k % 2), HD * (k % 2) + HD)
            pe.matmul(ps[3][rows, 0:T], v[0], pt[:, 0:T], start=first, stop=False)
            ins = pe.matmul(ps[3][rows, P:T], v[1], pt[:, T:T + P], start=False, stop=last)
            if last:
                ins.then_inc(seg_out, 1)

        def mixing_half(part, n, j):
            pe.wait_ge(split_lo, j + 1)
            if n >= 3:
                pe.wait_ge(*taken(part, n - 3))

        def token_pair(part, n, j, kt, xs):
            pe.wait_ge(split_lo, j + 1)
            for t in range(TT):
                pe.wait_ge(*taken(part, n - 4 + t))
                bank = ps[(n - 1 + t) % 3][:, 0:T].rearrange("p (a c) -> p a c", c=P)
                for k in range(kt):
                    a = (xs[0][:, k, t * P:(t + 1) * P], xs[1][:, k, t * P:(t + 1) * P])
                    b = (w_pair(hi, j - 1, k), w_pair(lo, j - 1, k))
                    pe.matmul(bank, a[0], b[0], start=k == 0, stop=False)
                    pe.matmul(bank, a[0], b[1], start=False, stop=False)
                    ins = pe.matmul(bank, a[1], b[0], start=False, stop=k == kt - 1)
            ins.then_inc(half_done, 2)

        def head_rows(h):
            return slice(HD * (h % 2), HD * (h % 2) + HD)

        pe.wait_ge(ident_in, 16)
        pe.wait_ge(gain_in, 16)
        turned(ps[0][:, 0:KD], vrow[0:KD, :], ident[0:KD, 0:KD]).then_inc(vec_turned, 1)
        for t in range(TT):
            pe.wait_ge(x_landed[t], 16)
            for m in range(KD):
                a = (m % 2) * T + t * P
                ins = turned(ps[4 + m // 2][:, a:a + P], x_in[:, t, m * P:(m + 1) * P])
                if t == TT - 1 and m % 2:
                    ins.then_inc(x_turned, 2)
        pe.wait_ge(vec_ready, 1)
        ffn(0, 0)

        for n in range(M1["end"]):
            j = J0[1] + n
            if n in M1_TOKEN:
                pass
            elif n - 1 in M1_TOKEN:
                token_pair(1, n, j, KD, (xh, xl))
            elif n < M1["merge"]:
                mixing_half(1, n, j)
                if n == 0:
                    first_half(j, ps[n % 3], (xh, xl), x_ready, 8 * 1).then_inc(half_done, 1)
                else:
                    feature_half(j, ps[n % 3], 0, KD, (xh, xl)).then_inc(half_done, 1)
            elif n < M1["out"]:
                mixing_half(1, n, j)
                if n == M1["merge"]:
                    pe.wait_ge(y_lo, 12)
                feature_half(j, ps[n % 3], 0, 2, (y1h[:, 0:2, :], y1l[:, 0:2, :]))
                feature_half(j, ps[n % 3], 2, 4, (y1h[:, 2:6, :], y1l[:, 2:6, :]), at=T).then_inc(half_done, 1)
            else:
                m = n - M1["out"]
                pe.wait_ge(split_lo, j + 1)
                if m >= 2:
                    pe.wait_ge(x_updated, 8 * 2 + m - 1)
                if m == 0:
                    ins = first_half(j, ps[4], (mh1, ml1), (merged_hi, merged_lo), 0)
                else:
                    ins = feature_half(j, ps[4 + m % 2], 0, KD, (mh1, ml1))
                ins.then_inc(half_done, 1)
            if n == 0:
                sums(1)
            if n == 1:
                x_row(1)
            for s in range(NSEG1):
                k = s // 3 if s < N_DSA else 4 + s - N_DSA
                head = 4 * (s % 3) + k if s < N_DSA else s - N_DSA
                if n == TURN1[s] + OUT_LAG:
                    pe.wait_ge(*taken(1, M1["qb"] - 1 if s < N_DSA else M1["gates"] - 1))
                    v = va if s < N_DSA else vb
                    weighted(s, k, s >= N_DSA or s % 3 == 0, s >= N_DSA or s % 3 == 2,
                             [v[:, t, head * HD:(head + 1) * HD] for t in range(TT)], pt1[:, s % 3, :])
            for s in range(NSEG1):
                k = s // 3 if s < N_DSA else 4 + s - N_DSA
                head = 4 * (s % 3) + k if s < N_DSA else s - N_DSA
                if n == TURN1[s]:
                    if s < 2:
                        pe.wait_ge(row_ready, ROWS["x1"] + 1)
                    turn(s, k, p1[:, s % 9, :])
                if n == SCORES1[s]:
                    q, kk = (qa, ka) if s < N_DSA else (qb, kb)
                    pe.wait_ge(*taken(1, M1["va"] - 1 if s < N_DSA else M1["kb"] + head // 2))
                    scores(s, q[head_rows(head), head // 2, :], kk[head_rows(head), head // 2, :])
        ffn(1, 2)

        for n in range(M2["end"]):
            j = J0[3] + n
            if n in M2_TOKEN:
                pass
            elif n - 1 in M2_TOKEN:
                token_pair(3, n, j, KD if n < M2["uq"] else CKV // P, (xh, xl) if n < M2["uq"] else (ckvh, ckvl))
            elif M2["uq"] <= n < M2["ukv"]:
                mixing_half(3, n, j)
                pe.wait_ge(cx_lo, 5)
                feature_half(j, ps[n % 3], 0, CQ // P, (cqh, cql)).then_inc(half_done, 1)
            elif M2["ukv"] <= n < M2["uv"]:
                mixing_half(3, n, j)
                feature_half(j, ps[n % 3], 0, CKV // P, (ckvh, ckvl)).then_inc(half_done, 1)
            elif n < M2["merge"]:
                mixing_half(3, n, j)
                if n == 0:
                    first_half(j, ps[n % 3], (xh, xl), x_ready, 8 * 3).then_inc(half_done, 1)
                else:
                    feature_half(j, ps[n % 3], 0, KD, (xh, xl)).then_inc(half_done, 1)
            elif n < M2["out"]:
                mixing_half(3, n, j)
                if n == M2["merge"]:
                    pe.wait_ge(y_lo, 20)
                    pe.wait_ge(yb_lo, 4)
                feature_half(j, ps[n % 3], 0, 4, (y2ah, y2al))
                feature_half(j, ps[n % 3], 4, 4, (y2bh, y2bl), at=T).then_inc(half_done, 1)
            else:
                m = n - M2["out"]
                pe.wait_ge(split_lo, j + 1)
                if m >= 2:
                    pe.wait_ge(x_updated, 8 * 4 + m - 1)
                if m == 0:
                    ins = first_half(j, ps[4], (mh2, ml2), (merged_hi, merged_lo), KD)
                else:
                    ins = feature_half(j, ps[4 + m % 2], 0, KD, (mh2, ml2))
                ins.then_inc(half_done, 1)
            if n == 0:
                sums(3)
            if n == 1:
                x_row(3)
            if n == Z_AT:
                pe.wait_ge(*taken(3, M2["lr"]))
                pe.wait_ge(small_in, 16)
                for c in range(2):
                    ins = pe.matmul(ps[4][:, c * T:(c + 1) * T], wg2[:, c * P:(c + 1) * P], lr[0:16, :],
                                    start=True, stop=True)
                ins.then_inc(decay_raw, 1)
            lv = n - LEVEL_AT
            if 0 <= lv < 9:
                b = 4 + 2 * (lv % 2)
                if lv >= 2:
                    pe.wait_ge(lv_taken, 2 * (lv - 1))
                elif lv == 0:
                    pe.wait_ge(decay_taken, 2)
                else:
                    pe.wait_ge(row_ready, ROWS["x3"] + 1)
                if lv < 8:
                    pe.wait_ge(lv_ready, 2 * (lv + 1))
                for t in range(TT) if lv else (0,):
                    j0, i0 = (t * P, t * P) if lv else (0, P)
                    for h in range(4):
                        r, c = head_rows(h), h // 2
                        kk = lvk[r, lv % 2, c, :] if lv < 8 else gk[r, c, :]
                        qq = lvq[r, lv % 2, c, :] if lv < 8 else gq[r, c, :]
                        a = (2 * t + c) * P
                        ins = pe.matmul(ps[b + h % 2][:, a:a + P], kk[:, j0:j0 + P], qq[:, i0:i0 + P],
                                        start=True, stop=True)
                ins.then_inc(lv_done, 1)
            if n == LATENT_AT:
                pe.wait_ge(cx_acc, 5)
                for e in range(2):
                    ins = token_sum(ps[3], e * TT, e)
                ins.then_inc(sums_ready, 1)
            if n == LATENT_AT + 2:
                row("latent", ps[3], RCOL["ckv"], RCOL["cq"])
            if n == GLA_O_AT:
                pe.wait_ge(lv_taken, 18)
                pe.wait_ge(*taken(3, M2["uq"] - 1))
                for t in range(TT):
                    for h in range(4):
                        o = ps[4 + t][:, h * P:(h + 1) * P]
                        if t == 0:
                            ins = pe.matmul(o, at3[:, 0, h, :], gv[:, 0, h * P:(h + 1) * P], start=True, stop=True)
                        else:
                            pe.matmul(o, at3[:, 2, h, :], gv[:, 0, h * P:(h + 1) * P], start=True, stop=False)
                            ins = pe.matmul(o, at3[:, 1, h, :], gv[:, 1, h * P:(h + 1) * P], start=False, stop=True)
                ins.then_inc(gla_out, 1)
            if n == GLA_TURN_AT:
                pe.wait_ge(gla_scaled, 2)
                for h in range(4):
                    for t in range(TT):
                        a = (h % 2) * T + t * P
                        ins = turned(ps[4 + h // 2][:, a:a + P], go[:, t, h * P:(h + 1) * P])
                ins.then_inc(gla_turned, 1)
            for s in range(NSEG2):
                if n == TURN2[s] + OUT_LAG:
                    pe.wait_ge(*taken(3, M2["gates"] - 1))
                    if s < 2:
                        pe.wait_ge(row_ready, ROWS["latent"] + 1)
                    weighted(NSEG1 + s, 12 + s, True, True,
                             [mv[:, t, s * HD:(s + 1) * HD] for t in range(TT)], pt2[:, s % 2, :])
            for s in range(NSEG2):
                if n == TURN2[s]:
                    turn(NSEG1 + s, 12 + s, p2[:, s % 5, :])
                if n == SCORES2[s]:
                    pe.wait_ge(*taken(3, M2["uv"] - 1))
                    if s == 0:
                        pe.wait_ge(gla_y, 4)
                    r = slice(32 * (s % 4), 32 * (s % 4) + 32)
                    scores(NSEG1 + s, qn[head_rows(s), s // 2, :], kn[head_rows(s), s // 2, :],
                           (qr[r, s // 4, :], kr[r, 0, :]))
        ffn(2, 4)

        for m in range(KD):
            pe.wait_ge(fin_ready, m + 1)
            if m == 5:
                sums(5)
            for t in range(TT):
                ins = turned(ps[2 * t + m // 4][:, (m % 4) * P:(m % 4 + 1) * P],
                                   o_fm[:, m, t * P:(t + 1) * P])
        ins.then_inc(fin_turned, 2)

    block.__exit__(None, None, None)


_INS = ["x", "norm_ffn1", "ffn1_gate", "ffn1_up", "ffn1_down", "norm_mix", "w_in", "w_up_a", "w_up_b", "w_out",
        "norm_ffn2", "ffn2_gate", "ffn2_up", "ffn2_down", "norm_final", "positions_2", "ln_mix_2", "w_in_2",
        "mla_norm_cq_2", "mla_w_uq_2", "mla_norm_ckv_2", "mla_w_ukv_2", "mla_w_o_2", "gla_w_gate2_2",
        "gla_b_gate_2", "gla_norm_2", "gla_w_o_2", "w_out_2", "ln_ffn_2", "ffn_w_gate_2", "ffn_w_up_2",
        "ffn_w_down_2", "final_norm_2"]


def kernel(**inputs):
    import concourse.bacc as bacc
    from concourse.bass_utils import run_bass_kernel_spmd

    nc = bacc.Bacc("TRN2", target_bir_lowering=False, num_devices=1)
    arrays = {f"in_{n}": np.ascontiguousarray(inputs[n]) for n in _INS}
    arrays["in_consts"], arrays["in_masks"] = constants()
    w = {}
    for name, a in arrays.items():
        ap = nc.dram_tensor(name, a.shape, mybir.dt.from_np(a.dtype), kind="ExternalInput").ap()
        w[name[3:]] = ap[0] if len(a.shape) == 3 and name not in ("in_x", "in_gla_w_gate2_2") else ap
    out = nc.dram_tensor("out_0", (1, T, D), F32, kind="ExternalOutput").ap()
    build(nc, w, out[0])
    r = run_bass_kernel_spmd(nc, [arrays], core_ids=[0])
    return r.results[0]["out_0"]
```
